# Optimizing a Trainium2 kernel written in Bass

```python
import jax, jax.numpy as jnp
from jax import lax
import numpy as np

D_MODEL = 1024
BATCH = 1
SEQ = 256
DEPTH = 1

MEM_LEN = 256
D_RNN = D_MODEL
LRU_HEADS = 16
LRU_HEAD_DIM = D_RNN // LRU_HEADS
LRU_CONV = 4
LRU_C = 8.0
D_CONV = D_MODEL
CONF_KERNEL = 31
N_BRANCH = 2
D_IN = 2 * D_RNN + 2 * D_CONV + N_BRANCH * D_MODEL
XA_HEADS = 4
XA_HEAD_DIM = D_MODEL // XA_HEADS
N_EXPERTS = 32
TOP_K = 4
D_EXPERT = D_MODEL
SWIGLU_ALPHA = 1.702
SWIGLU_LIMIT = 7.0
MOE_BLOCK = 256
NORM_EPS = 1e-5

kernel_name = "hybrid_rglru_conformer_xattn_moe_encoder"

def rms_norm(x, g):
    xf = x.astype(jnp.float32)
    y = xf * lax.rsqrt(jnp.mean(xf * xf, axis=-1, keepdims=True) + NORM_EPS)
    return (y * g.astype(jnp.float32)).astype(x.dtype)

def layer_norm(x, g, b):
    xf = x.astype(jnp.float32)
    mu = jnp.mean(xf, axis=-1, keepdims=True)
    xc = xf - mu
    var = jnp.mean(xc * xc, axis=-1, keepdims=True)
    y = xc * lax.rsqrt(var + NORM_EPS) * g.astype(jnp.float32) + b.astype(jnp.float32)
    return y.astype(x.dtype)

def depthwise_conv(x, w, b, pad_left, pad_right):
    C = x.shape[-1]
    y = lax.conv_general_dilated(
        x, w[:, None, :].astype(x.dtype), window_strides=(1,),
        padding=[(pad_left, pad_right)], dimension_numbers=('NWC', 'WIO', 'NWC'),
        feature_group_count=C)
    return y + b.astype(x.dtype)

def rg_lru_bidirectional(x, w_a, b_a, w_i, b_i, lam):
    B, S, _ = x.shape
    xd = jnp.stack([x, jnp.flip(x, axis=1)])
    xh = xd.reshape(2, B, S, LRU_HEADS, LRU_HEAD_DIM)
    r = jax.nn.sigmoid(jnp.einsum('zbshi,zhij->zbshj', xh, w_a).reshape(2, B, S, D_RNN)
                       + b_a[:, None, None, :])
    i = jax.nn.sigmoid(jnp.einsum('zbshi,zhij->zbshj', xh, w_i).reshape(2, B, S, D_RNN)
                       + b_i[:, None, None, :])
    log_a = (-LRU_C * jax.nn.softplus(-lam.astype(jnp.float32)))[:, None, None, :] * r.astype(jnp.float32)
    a = jnp.exp(log_a)
    u = jnp.sqrt(-jnp.expm1(2.0 * log_a)) * (i * xd).astype(jnp.float32)

    def step(h, au):
        a_t, u_t = au
        h = a_t * h + u_t
        return h, h

    _, hs = lax.scan(step, jnp.zeros((2, B, D_RNN), jnp.float32),
                     (jnp.moveaxis(a, 2, 0), jnp.moveaxis(u, 2, 0)))
    hs = jnp.moveaxis(hs, 0, 2)
    return (hs[0] + jnp.flip(hs[1], axis=1)).astype(x.dtype)

def parallel_mixer(h, w_in, b_branch_gate, lru_conv_w, lru_conv_b, lru_w_a, lru_b_a,
                   lru_w_i, lru_b_i, lru_lambda, w_rnn_out, conf_dw_w, conf_dw_b,
                   conf_ln_g, conf_ln_b, w_conf_out, w_out):
    B, S, _ = h.shape
    z = h @ w_in
    x_rnn, g_rnn, x_conf, g_br = jnp.split(
        z, [D_RNN, 2 * D_RNN, 2 * D_RNN + 2 * D_CONV], axis=-1)
    xc = depthwise_conv(x_rnn, lru_conv_w, lru_conv_b, LRU_CONV // 2, LRU_CONV - 1 - LRU_CONV // 2)
    y_a = (rg_lru_bidirectional(xc, lru_w_a, lru_b_a, lru_w_i, lru_b_i, lru_lambda)
           * jax.nn.gelu(g_rnn)) @ w_rnn_out
    c_val, c_gate = jnp.split(x_conf, 2, axis=-1)
    c = depthwise_conv(c_val * jax.nn.sigmoid(c_gate), conf_dw_w, conf_dw_b,
                       CONF_KERNEL // 2, CONF_KERNEL // 2)
    y_b = jax.nn.silu(layer_norm(c, conf_ln_g, conf_ln_b)) @ w_conf_out
    gates = jax.nn.sigmoid(g_br.reshape(B, S, N_BRANCH, D_MODEL) + b_branch_gate)
    merged = gates[:, :, 0, :] * y_a + gates[:, :, 1, :] * y_b
    return merged @ w_out

def memory_cross_attention(h, mem_n, w_q, w_kv, w_o):
    B, S, _ = h.shape
    M = mem_n.shape[1]
    q = (h @ w_q).reshape(B, S, XA_HEADS, XA_HEAD_DIM)
    k, v = jnp.split(mem_n @ w_kv, 2, axis=-1)
    k = k.reshape(B, M, XA_HEADS, XA_HEAD_DIM)
    v = v.reshape(B, M, XA_HEADS, XA_HEAD_DIM)
    s = jnp.einsum('bshd,bmhd->bhsm', q, k).astype(jnp.float32) * (XA_HEAD_DIM ** -0.5)
    p = jax.nn.softmax(s, axis=-1).astype(v.dtype)
    o = jnp.einsum('bhsm,bmhd->bshd', p, v).reshape(B, S, D_MODEL)
    return o @ w_o

def moe_ffn(h, router_w, router_b, exp_w_up, exp_b_up, exp_w_down, exp_b_down):
    B, S, D = h.shape
    N = B * S
    t = h.reshape(N, D)
    logits = (t @ router_w + router_b).astype(jnp.float32)
    top_val, top_idx = lax.top_k(logits, TOP_K)
    gate = jax.nn.softmax(top_val, axis=-1)
    A = N * TOP_K
    e_flat = top_idx.reshape(A)
    w_flat = gate.reshape(A)
    tok_flat = jnp.arange(A, dtype=jnp.int32) // TOP_K
    order = jnp.argsort(e_flat)
    e_sorted = e_flat[order]
    counts = jnp.bincount(e_flat, length=N_EXPERTS)
    start = jnp.cumsum(counts) - counts
    padded = (counts + MOE_BLOCK - 1) // MOE_BLOCK * MOE_BLOCK
    padded_end = jnp.cumsum(padded)
    padded_start = padded_end - padded
    dest = padded_start[e_sorted] + jnp.arange(A, dtype=jnp.int32) - start[e_sorted]
    n_blocks = -(-(A + N_EXPERTS * (MOE_BLOCK - 1)) // MOE_BLOCK)
    P = n_blocks * MOE_BLOCK
    row_tok = jnp.zeros((P,), jnp.int32).at[dest].set(tok_flat[order])
    row_w = jnp.zeros((P,), jnp.float32).at[dest].set(w_flat[order])
    block_start = jnp.arange(n_blocks, dtype=jnp.int32) * MOE_BLOCK
    block_exp = jnp.minimum(jnp.searchsorted(padded_end, block_start, side='right'),
                            N_EXPERTS - 1)

    def block_step(y, blk):
        tok, wt, e = blk
        gu = t[tok] @ exp_w_up[e] + exp_b_up[e]
        g, u = jnp.split(gu, 2, axis=-1)
        g = jnp.minimum(g, SWIGLU_LIMIT)
        u = jnp.clip(u, -SWIGLU_LIMIT, SWIGLU_LIMIT)
        act = (u + 1.0) * (g * jax.nn.sigmoid(SWIGLU_ALPHA * g))
        out = act @ exp_w_down[e] + exp_b_down[e]
        return y.at[tok].add(out * wt[:, None].astype(out.dtype)), None

    y, _ = lax.scan(block_step, jnp.zeros_like(t),
                    (row_tok.reshape(n_blocks, MOE_BLOCK), row_w.reshape(n_blocks, MOE_BLOCK), block_exp))
    return y.reshape(B, S, D)

def setup_inputs(seed: int = 0) -> dict:
    key = jax.random.key(seed)
    ks = jax.random.split(key, 40)
    L = DEPTH

    def nrm(k, shape, scale):
        return jax.random.normal(k, shape, jnp.float32) * scale

    a0 = jax.random.uniform(ks[30], (L, 2, D_RNN), jnp.float32, 0.9, 0.999)
    a_base = a0 ** (1.0 / LRU_C)
    lru_lambda = jnp.log(a_base) - jnp.log1p(-a_base)
    return {
        "x": nrm(ks[0], (BATCH, SEQ, D_MODEL), 1.0),
        "mem": nrm(ks[1], (BATCH, MEM_LEN, D_MODEL), 1.0),
        "norm_mix_g": 1.0 + nrm(ks[2], (L, D_MODEL), 0.02),
        "w_in": nrm(ks[3], (L, D_MODEL, D_IN), D_MODEL ** -0.5),
        "b_branch_gate": nrm(ks[4], (L, N_BRANCH, D_MODEL), 0.02),
        "lru_conv_w": nrm(ks[5], (L, LRU_CONV, D_RNN), LRU_CONV ** -0.5),
        "lru_conv_b": nrm(ks[6], (L, D_RNN), 0.02),
        "lru_w_a": nrm(ks[7], (L, 2, LRU_HEADS, LRU_HEAD_DIM, LRU_HEAD_DIM), LRU_HEAD_DIM ** -0.5),
        "lru_b_a": nrm(ks[8], (L, 2, D_RNN), 0.02),
        "lru_w_i": nrm(ks[9], (L, 2, LRU_HEADS, LRU_HEAD_DIM, LRU_HEAD_DIM), LRU_HEAD_DIM ** -0.5),
        "lru_b_i": nrm(ks[10], (L, 2, D_RNN), 0.02),
        "lru_lambda": lru_lambda,
        "w_rnn_out": nrm(ks[11], (L, D_RNN, D_MODEL), D_RNN ** -0.5),
        "conf_dw_w": nrm(ks[12], (L, CONF_KERNEL, D_CONV), CONF_KERNEL ** -0.5),
        "conf_dw_b": nrm(ks[13], (L, D_CONV), 0.02),
        "conf_ln_g": 1.0 + nrm(ks[14], (L, D_CONV), 0.02),
        "conf_ln_b": nrm(ks[15], (L, D_CONV), 0.02),
        "w_conf_out": nrm(ks[16], (L, D_CONV, D_MODEL), D_CONV ** -0.5),
        "w_out": nrm(ks[17], (L, D_MODEL, D_MODEL), D_MODEL ** -0.5),
        "norm_xa_g": 1.0 + nrm(ks[18], (L, D_MODEL), 0.02),
        "norm_mem_g": 1.0 + nrm(ks[19], (L, D_MODEL), 0.02),
        "xa_w_q": nrm(ks[20], (L, D_MODEL, D_MODEL), D_MODEL ** -0.5),
        "xa_w_kv": nrm(ks[21], (L, D_MODEL, 2 * D_MODEL), D_MODEL ** -0.5),
        "xa_w_o": nrm(ks[22], (L, D_MODEL, D_MODEL), D_MODEL ** -0.5),
        "norm_ffn_g": 1.0 + nrm(ks[23], (L, D_MODEL), 0.02),
        "router_w": nrm(ks[24], (L, D_MODEL, N_EXPERTS), D_MODEL ** -0.5),
        "router_b": nrm(ks[25], (L, N_EXPERTS), 0.01),
        "exp_w_up": nrm(ks[26], (L, N_EXPERTS, D_MODEL, 2 * D_EXPERT), D_MODEL ** -0.5),
        "exp_b_up": nrm(ks[27], (L, N_EXPERTS, 2 * D_EXPERT), 0.01),
        "exp_w_down": nrm(ks[28], (L, N_EXPERTS, D_EXPERT, D_MODEL), D_EXPERT ** -0.5),
        "exp_b_down": nrm(ks[29], (L, N_EXPERTS, D_MODEL), 0.01),
        "final_norm_g": 1.0 + nrm(ks[31], (D_MODEL,), 0.02),
    }

def reference(x, mem, norm_mix_g, w_in, b_branch_gate, lru_conv_w, lru_conv_b, lru_w_a,
              lru_b_a, lru_w_i, lru_b_i, lru_lambda, w_rnn_out, conf_dw_w, conf_dw_b,
              conf_ln_g, conf_ln_b, w_conf_out, w_out, norm_xa_g, norm_mem_g, xa_w_q,
              xa_w_kv, xa_w_o, norm_ffn_g, router_w, router_b, exp_w_up, exp_b_up,
              exp_w_down, exp_b_down, final_norm_g):
    for l in range(DEPTH):
        h = rms_norm(x, norm_mix_g[l])
        x = x + parallel_mixer(h, w_in[l], b_branch_gate[l], lru_conv_w[l], lru_conv_b[l],
                               lru_w_a[l], lru_b_a[l], lru_w_i[l], lru_b_i[l], lru_lambda[l],
                               w_rnn_out[l], conf_dw_w[l], conf_dw_b[l], conf_ln_g[l],
                               conf_ln_b[l], w_conf_out[l], w_out[l])
        h = rms_norm(x, norm_xa_g[l])
        x = x + memory_cross_attention(h, rms_norm(mem, norm_mem_g[l]),
                                       xa_w_q[l], xa_w_kv[l], xa_w_o[l])
        h = rms_norm(x, norm_ffn_g[l])
        x = x + moe_ffn(h, router_w[l], router_b[l], exp_w_up[l], exp_b_up[l],
                        exp_w_down[l], exp_b_down[l])
    return rms_norm(x, final_norm_g)


_drawn_inputs = setup_inputs


def setup_inputs(seed=0):
    import zlib

    import numpy as np

    out = dict(_drawn_inputs(seed))
    spreads = {}
    factors = {'lru_b_a': 6.987,
     'lru_b_i': 4.598,
     'conf_ln_b': 3.188,
     'norm_xa_g': 4.651,
     'norm_mem_g': 3.027,
     'exp_b_up': 27.252,
     'exp_b_down': 31.101,
     'final_norm_g': 8.418,
     'b_branch_gate': 3.851,
     'norm_ffn_g': 3.009,
     'router_b': 3.918}
    for name, (base, spread) in spreads.items():
        noise = np.random.default_rng([zlib.crc32(name.encode()), seed]).standard_normal(out[name].shape)
        drawn = base * np.exp(spread * noise) if base else spread * noise
        out[name] = __import__('jax').numpy.asarray(drawn.astype(out[name].dtype))
    for name, factor in factors.items():
        out[name] = (out[name] * factor).astype(out[name].dtype)
    return out
```

```python
from contextlib import ExitStack

import concourse.bass as bass
from concourse import mybir

F32 = mybir.dt.float32
I32 = mybir.dt.int32
U32 = mybir.dt.uint32
ALU = mybir.AluOpType
ACT = mybir.ActivationFunctionType
AX = mybir.AxisListType

P = 128
D = 1024
KT = D // P
T = 256
TT = T // P
HEADS = 4
HD = D // HEADS
NE = 32
TOP = 4
F = D
EPS = 1e-5
SWIGLU_ALPHA, LIMIT = 1.702, 7.0
LRU_TAPS, CONF_TAPS = 4, 31
LRU_LEFT, CONF_LEFT = 2, 15

CHUNK = 2048
COLS = CHUNK // KT
PRE_SLOTS = 4
UP_CHUNKS = KT
DOWN_CHUNKS = KT // 2
SLOTS = UP_CHUNKS + DOWN_CHUNKS
CAP = 64
MAX_ROUNDS = T // CAP
JOBS_MAX = NE * MAX_ROUNDS
POS_W = NE * (MAX_ROUNDS + 1)
NBANK = 4

(P_MIX_G, P_LRU_CB, P_BA, P_BI, P_LAM, P_DW_B, P_LN_G, P_LN_B, P_XA_G, P_MEM_G, P_FFN_G, P_GATE_B,
 P_LRU_W, P_DW_W, N_PAR) = (0, 1, 2, 4, 6, 8, 9, 10, 11, 12, 13, 14, 16, 20, 51)

WEIGHTED = ("cg", "cv", "xr", "gr", "k", "v", "ga", "gb", "ya", "yb", "wo", "q", "o")
PRODUCTS = (
    [("sum_x2", 0), ("sum_m2", 0)]
    + [(n, i) for i in range(4) for n in ("cg", "cv")]
    + [("xr", i) for i in range(4)] + [("gr", i) for i in range(4)] + [("k", i) for i in range(4)]
    + [("v", 0), ("ln_mean", 0), ("v", 1), ("v", 2), ("v", 3), ("ln_var", 0)]
    + [(n, i) for i in range(4) for n in ("ra0", "ri0")] + [("ga", i) for i in range(4)]
    + [(n, i) for i in range(4) for n in ("ra1", "ri1")] + [("gb", i) for i in range(4)]
    + [("yb", i) for i in range(4)] + [("ya", i) for i in range(4)]
    + [("wo", i) for i in range(4)] + [("sum_x1", 0)] + [("q", i) for i in range(4)]
    + [("score", h) for h in range(HEADS)]
    + [("probT", 0), ("probT", 1), ("attn", 0), ("probT", 2), ("attn", 1), ("probT", 3), ("attn", 2), ("attn", 3)]
    + [("o", i) for i in range(4)] + [("sum_xf", 0), ("logit", 0)]
    + [("htok", i) for i in range(4)] + [("gfin", 0), ("gfin", 1), ("rank", 0), ("gateT", 0)]
)
AT = {name: i for i, name in enumerate(PRODUCTS)}
CHUNKS = [x for x in PRODUCTS if x[0] in WEIGHTED]
CHUNK_AT = {name: i for i, name in enumerate(CHUNKS)}


def encoder_kernel(nc, xT_d, memT_d, par_d, w_in, lru_w_a, lru_w_i, w_rnn_out, w_conf_out, w_out,
                   w_q, w_kv, w_o, router_w, router_b, w_up, b_up, w_down, b_down, g_final, out):
    sources = {"xr": (w_in, 0), "gr": (w_in, D), "cv": (w_in, 2 * D), "cg": (w_in, 3 * D),
               "ga": (w_in, 4 * D), "gb": (w_in, 5 * D), "k": (w_kv, 0), "v": (w_kv, D),
               "ya": (w_rnn_out, 0), "yb": (w_conf_out, 0), "wo": (w_out, 0), "q": (w_q, 0),
               "o": (w_o, 0)}

    with ExitStack() as ctx:
        def sb(name, shape, dt=F32):
            return ctx.enter_context(nc.sbuf_tensor(name, shape, dt))

        def sem(name):
            return ctx.enter_context(nc.semaphore(name))

        ring = sb("ring", [P, SLOTS, CHUNK])
        lru_gate_w = ring[:, 4:6, :].rearrange("p s (a m n) -> p (s a) m n", m=KT, n=P)
        memT = ring[:, 6, :].rearrange("p (k t) -> p k t", k=KT)
        lru_t = memT
        xc = ring[:, 7, :].rearrange("p (k t) -> p k t", k=KT)
        pre_slot = [ring[:, SLOTS - PRE_SLOTS + i, :].rearrange("p (k n) -> p k n", k=KT)
                    for i in range(PRE_SLOTS)]

        def act_tile(name, width=T):
            return sb(name, [P, KT, width])

        xT = act_tile("xT")
        hT = act_tile("hT")
        glu = act_tile("glu", T + CONF_TAPS - 1)
        cv = act_tile("cv")
        xr = act_tile("xr", T + LRU_TAPS - 1)
        gl = act_tile("gl")
        keyT = act_tile("keyT")
        val = sb("val", [P, TT, D])
        lru_a = act_tile("lru_a")
        lru_u = act_tile("lru_u")
        lru_h = act_tile("lru_h")
        gate_a, gate_b = glu[:, :, 0:T], xr[:, :, 0:T]
        qT = lru_a
        prob = lru_u[:, :, :].rearrange("p (h t) m -> p h t m", h=HEADS)
        probT = lru_h[:, :, :].rearrange("p (h t) m -> p h t m", h=HEADS)
        attnT = gl
        sig = sb("sig", [P, 2, 2 * T])
        par = sb("par", [P, KT, N_PAR])
        ident = sb("ident", [P, P])
        ones = sb("ones", [P, P])
        before = sb("before", [P, P])
        stat = sb("stat", [P, T])
        mstat = sb("mstat", [P, T])
        lam = sb("lam", [P, 7, KT, 2])
        router = sb("router", [P, KT, NE])
        rb_row = sb("rb_row", [1, NE])
        bd_sb = sb("bd_sb", [NE, D])
        sm = sb("sm", [P, 4, HEADS, TT])
        lg = sb("lg", [P, TT, NE])
        top_v = sb("top_v", [P, TT, 8])
        top_i = sb("top_i", [P, TT, 8], U32)
        top_f = sb("top_f", [P, TT, 8])
        top_g = sb("top_g", [P, TT, 8])
        t1 = sb("t1", [P, TT, 4])
        iota_i = sb("iota_i", [P, P], I32)
        iota_f = sb("iota_f", [P, P])
        iota_c = sb("iota_c", [P, P])
        mask = sb("mask", [P, TT, NE])
        gate = sb("gate", [P, TT, NE])
        oh = sb("oh", [P, NE])
        rank = sb("rank", [P, TT, NE])
        pos = sb("pos", [P, TT, POS_W])
        gatej = sb("gatej", [P, TT, POS_W])
        count = sb("count", [1, 4])
        n_i = sb("n_i", [1, 2], I32)
        gateT = sb("gateT", [NE, TT, P])
        h_tok = keyT[:, :, :].rearrange("p (t k) c -> p t (k c)", t=TT)
        gc, uc = val[:, 0, 0:512], val[:, 0, 512:1024]
        sg, act = val[:, 1, 0:512], val[:, 1, 512:1024]
        xg = lru_a[:, 0:2, :].rearrange("p a (k c) -> p (a k) c", c=CAP)
        actT = lru_a[:, 2:4, :].rearrange("p a (h c) -> p (a h) c", c=P)
        job_out = lru_a[:, 4:6, :].rearrange("p a c -> p (a c)")
        pick = lru_a[:, 6, 0:TT * CAP].rearrange("p (t c) -> p t c", t=TT)
        wpick = lru_a[:, 7, :].rearrange("p (t c) -> p t c", t=TT)
        wpickT = lru_u[:, 0, :].rearrange("p (t c) -> p t c", t=TT)
        bup_row = lru_h[0:1, :, :].rearrange("p k t -> p (k t)")
        y_sb = cv[:, :, :].rearrange("p (t k) c -> p t (k c)", t=TT)
        gfin = gl[:, 0:4, :].rearrange("p k t -> p (k t)")
        gfin_row = gl[0:1, 4:8, :].rearrange("p k t -> p (k t)")
        fin = sb("fin", [P, 4])

        bank = [ctx.enter_context(nc.psum_tensor(f"bank{i}", [P, 512], F32)) for i in range(NBANK)]
        y_ps = ctx.enter_context(nc.psum_tensor("y_ps", [P, TT, D], F32))

        x_in, mem_in, par_in, lruw_in, router_in, late_in = map(sem, (
            "x_in", "mem_in", "par_in", "lruw_in", "router_in", "late_in"))
        zeroed, consts = sem("zeroed"), sem("consts")
        pre_loaded = [sem(f"pre_loaded{i}") for i in range(PRE_SLOTS)]
        product = sem("product")
        mean_read, logit_read, rank_read, yb_read, ya_read = map(sem, (
            "mean_read", "logit_read", "rank_read", "yb_read", "ya_read"))
        x_sq, m_sq, ln_sq, x1_sq, xf_sq = map(sem, ("x_sq", "m_sq", "ln_sq", "x1_sq", "xf_sq"))
        var_ready, root_ready = sem("var_ready"), sem("root_ready")
        lam_abs, lam_exp, lam_ready = sem("lam_abs"), sem("lam_exp"), sem("lam_ready")
        h_ready, mem_ready = sem("h_ready"), sem("mem_ready")
        sig_ready, glu_ready, xr_ready, gl_ready, kv_ready = map(sem, (
            "sig_ready", "glu_ready", "xr_ready", "gl_ready", "kv_ready"))
        conv_ready, xc_ready, centred, ln_ready, swish_ready = map(sem, (
            "conv_ready", "xc_ready", "centred", "ln_ready", "swish_ready"))
        lru_gates, lru_exp, lru_sq, lru_root, lru_scanned, lru_ready = map(sem, (
            "lru_gates", "lru_exp", "lru_sq", "lru_root", "lru_scanned", "lru_ready"))
        mgate_ready, merged, x1_ready, xf_ready = map(sem, ("mgate_ready", "merged", "x1_ready", "xf_ready"))
        q_ready, smax_ready, sexp_ready, prob_ready, probT_ready, attn_ready = map(sem, (
            "q_ready", "smax_ready", "sexp_ready", "prob_ready", "probT_ready", "attn_ready"))
        top_ready, texp_ready, mask_ready, count_ready, htok_ready, gateT_ready, gfin_ready = map(sem, (
            "top_ready", "texp_ready", "mask_ready", "count_ready", "htok_ready", "gateT_ready", "gfin_ready"))
        loaded = [sem(f"loaded{s}") for s in range(SLOTS)]
        chunk_used, bias_in, bias_used = sem("chunk_used"), sem("bias_in"), sem("bias_used")
        pick_ready, wpickT_done, wpickT_ready, gathered, xg_ready = map(sem, (
            "pick_ready", "wpickT_done", "wpickT_ready", "gathered", "xg_ready"))
        gclip_ready, sigm_ready, act_ready, actT_done, actT_ready = map(sem, (
            "gclip_ready", "sigm_ready", "act_ready", "actT_done", "actT_ready"))
        job_out_ready, y_done, ysum_ready, yvar_ready, yroot_ready, y_ready, stored = map(sem, (
            "job_out_ready", "y_done", "ysum_ready", "yvar_ready", "yroot_ready", "y_ready", "stored"))
        gate_ready = sem("gate_ready")
        v_chain, uclip_ready, ug_ready = sem("v_chain"), sem("uclip_ready"), sem("ug_ready")

        bank_g, bank_u, bank_x, bank_a = bank
        xg_ps = bank_x[:].rearrange("p (k c) -> p k c", c=CAP)

        def pair(x):
            return x[:].rearrange("p (m t) -> p m t", m=2)

        def ps(name, i=0):
            return bank[AT[(name, i)] % NBANK]

        def wait_product(eng, name, i=0):
            eng.wait_ge(product, AT[(name, i)] + 1)

        read = {("sum_x2", 0): (var_ready, 1), ("sum_m2", 0): (var_ready, 2), ("ln_mean", 0): (mean_read, 1),
                ("ln_var", 0): (var_ready, 3), ("sum_x1", 0): (var_ready, 4), ("sum_xf", 0): (var_ready, 5),
                ("logit", 0): (logit_read, 1), ("rank", 0): (rank_read, 1), ("gateT", 0): (gateT_ready, 1)}
        for i in range(4):
            read.update({("cg", i): (sig_ready, i + 1), ("cv", i): (glu_ready, i + 1), ("xr", i): (xr_ready, i + 1),
                         ("gr", i): (gl_ready, i + 1), ("k", i): (kv_ready, i + 1), ("v", i): (kv_ready, i + 5),
                         ("ga", i): (mgate_ready, 2 * i + 2), ("gb", i): (mgate_ready, 2 * i + 10),
                         ("yb", i): (yb_read, i + 1), ("ya", i): (ya_read, i + 1), ("wo", i): (x1_ready, i + 1),
                         ("q", i): (q_ready, i + 1), ("score", i): (sexp_ready, 2 * i + 2),
                         ("probT", i): (probT_ready, i + 1), ("attn", i): (attn_ready, i + 1),
                         ("o", i): (xf_ready, i + 1), ("htok", i): (htok_ready, i + 1)})
            for d in range(2):
                read.update({(f"ra{d}", i): (lru_gates, 16 * d + 4 * i + 2),
                             (f"ri{d}", i): (lru_gates, 16 * d + 4 * i + 4)})
        for i in range(2):
            read[("gfin", i)] = (gfin_ready, i + 1)

        block = ctx.enter_context(nc.Block())

        @block.sync
        def _(sp):
            sp.dma_start(xT[:], xT_d).then_inc(x_in, 16)

            def load_projection(n):
                name, i = CHUNKS[n]
                w, col = sources[name]
                src = w[:, col + COLS * i:col + COLS * (i + 1)].rearrange("(k p) n -> p k n", p=P)
                if n >= PRE_SLOTS:
                    wait_product(sp, *CHUNKS[n - PRE_SLOTS])
                sp.dma_start(pre_slot[n % PRE_SLOTS], src).then_inc(pre_loaded[n % PRE_SLOTS], 16)

            def expert_source(e, s):
                if s < UP_CHUNKS:
                    return w_up[e, P * s:P * (s + 1), :].rearrange("a p n -> p (a n)")
                k = 2 * (s - UP_CHUNKS)
                return w_down[e, P * k:P * (k + 2), :].rearrange("a (k p) n -> p (a k) n", p=P)

            def expert_slot(s):
                return ring[:, s, :] if s < UP_CHUNKS else ring[:, s, :].rearrange("p (k n) -> p k n", k=2)

            for n in range(len(CHUNKS)):
                load_projection(n)
                if n == CHUNK_AT[("ga", 0)]:
                    for s in range(4):
                        sp.dma_start(expert_slot(s), expert_source(slice(0, 1), s)).then_inc(loaded[s], 16)
                if n == CHUNK_AT[("wo", 3)]:
                    wait_product(sp, "ri1", 3)
                    sp.wait_ge(lru_ready, 1)
                    for s in range(4, 8):
                        sp.dma_start(expert_slot(s), expert_source(slice(0, 1), s)).then_inc(loaded[s], 16)
            wait_product(sp, "attn", 3)
            sp.dma_start(bup_row, b_up[0:1, :]).then_inc(bias_in, 16)
            wait_product(sp, *CHUNKS[-1])
            for s in range(8, SLOTS):
                sp.dma_start(expert_slot(s), expert_source(slice(0, 1), s)).then_inc(loaded[s], 16)

            sp.wait_ge(count_ready, 2)
            rounds = sp.value_load(n_i[0:1, 1:2], min_val=1, max_val=MAX_ROUNDS)
            with sp.Fori(0, rounds) as r:
                first = sp.snap((((r + 3) >> 2) + 1) & 1)
                base = sp.snap(r * NE)
                with sp.Fori(first, NE) as e:
                    job = sp.snap(base + e)
                    sp.wait_ge(bias_used, job)
                    sp.dma_start(bup_row, b_up[bass.ds(e, 1), :]).then_inc(bias_in, 16)
                    for s in range(SLOTS):
                        sp.wait_ge(chunk_used, job * SLOTS + (s + 1))
                        sp.dma_start(expert_slot(s), expert_source(bass.ds(e, 1), s)).then_inc(loaded[s], 16)

            for t in range(TT):
                sp.wait_ge(y_ready, t + 1)
                sp.dma_start(out[P * t:P * (t + 1), :], y_sb[:, t, :]).then_inc(stored, 16)
            sp.wait_ge(stored, 16 * TT)

        @block.gpsimd
        def _(pool):
            pool.memset(lru_gate_w, 0.0).then_inc(zeroed, 1)
            pool.memset(ones[:], 1.0).then_inc(consts, 1)
            pool.memset(ident[:], 0.0).then_inc(consts, 1)
            pool.wait_ge(consts, 2)
            pool.affine_select(out=ident[:], in_=ident[:], compare_op=ALU.not_equal, fill=1.0, base=0,
                               pattern=[[-1, P]], channel_multiplier=1).then_inc(consts, 1)
            pool.affine_select(out=before[:], in_=ones[:], compare_op=ALU.is_gt, fill=0.0, base=0,
                               pattern=[[1, P]], channel_multiplier=-1).then_inc(consts, 1)
            pool.iota(iota_i[:], pattern=[[1, P]], base=0, channel_multiplier=0).then_inc(consts, 1)
            pool.memset(glu[:, :, 0:CONF_LEFT], 0.0).then_inc(consts, 1)
            pool.memset(glu[:, :, CONF_LEFT + T:], 0.0).then_inc(consts, 1)
            pool.memset(xr[:, :, 0:LRU_LEFT], 0.0).then_inc(consts, 1)
            pool.memset(xr[:, :, LRU_LEFT + T:], 0.0).then_inc(consts, 1)
        CONSTS = 9

        @block.scalar
        def _(a):
            a.dma_start(par[:], par_d).then_inc(par_in, 16)
            a.dma_start(memT, memT_d).then_inc(mem_in, 16)
            a.wait_ge(zeroed, 1)
            for d in range(2):
                for g, w in enumerate((lru_w_a, lru_w_i)):
                    for odd in range(2):
                        src = w[d].rearrange("(m o) i j -> o i m j", o=2)[odd]
                        a.dma_start(lru_gate_w[64 * odd:64 * odd + 64, 2 * d + g, :, 64 * odd:64 * odd + 64],
                                    src).then_inc(lruw_in, 16)
            a.dma_start(router[:], router_w.rearrange("(k p) e -> p k e", p=P)).then_inc(router_in, 16)
            a.dma_start(rb_row[:], router_b).then_inc(router_in, 16)
            a.dma_start(bd_sb[:], b_down).then_inc(router_in, 16)

            def root(n, buf):
                a.wait_ge(var_ready, n)
                a.activation(buf[:], buf[:], ACT.Sqrt).then_inc(root_ready, 1)

            a.wait_ge(x_in, 16)
            a.activation(lru_a[:], xT[:], ACT.Square).then_inc(x_sq, 1)
            a.wait_ge(mem_in, 16)
            a.activation(lru_u[:], memT, ACT.Square).then_inc(m_sq, 1)
            root(1, stat)
            root(2, mstat)
            a.wait_ge(lam_abs, 1)
            a.activation(lam[:, 1], lam[:, 0], ACT.Exp).then_inc(lam_exp, 1)

            for i in range(4):
                wait_product(a, "cg", i)
                if i >= 2:
                    a.wait_ge(glu_ready, i - 1)
                a.activation(sig[:, i % 2], ps("cg", i)[:], ACT.Sigmoid).then_inc(sig_ready, 1)
            a.wait_ge(consts, CONSTS)
            for i in range(4):
                wait_product(a, "xr", i)
                a.activation(xr[:, 2 * i:2 * i + 2, LRU_LEFT:LRU_LEFT + T], pair(ps("xr", i)),
                             ACT.Copy).then_inc(xr_ready, 1)
            for i in range(4):
                wait_product(a, "gr", i)
                a.activation(gl[:, 2 * i:2 * i + 2, :], pair(ps("gr", i)),
                             ACT.Gelu_apprx_tanh).then_inc(gl_ready, 1)
            for i in range(4):
                wait_product(a, "k", i)
                a.activation(keyT[:, 2 * i:2 * i + 2, :], pair(ps("k", i)), ACT.Copy).then_inc(kv_ready, 1)
            for i in range(4):
                if i == 2:
                    a.wait_ge(centred, 1)
                    a.wait_ge(h_ready, KT)
                    a.activation(lru_a[:], cv[:], ACT.Square).then_inc(ln_sq, 1)
                wait_product(a, "v", i)
                a.activation(val[:, :, COLS * i:COLS * (i + 1)], pair(ps("v", i)), ACT.Copy).then_inc(kv_ready, 1)
            root(3, stat)

            def lru(d):
                if d == 1:
                    a.wait_ge(lru_scanned, KT)
                for i in range(4):
                    for name, bias, dst in (("ra", P_BA, lru_a), ("ri", P_BI, lru_u)):
                        wait_product(a, f"{name}{d}", i)
                        for m in range(2):
                            a.activation(dst[:, 2 * i + m, :], ps(f"{name}{d}", i)[:, m * T:(m + 1) * T], ACT.Sigmoid,
                                         bias=par[:, 2 * i + m, bias + d:bias + d + 1]).then_inc(lru_gates, 1)
                a.wait_ge(lam_ready, 1)
                a.wait_ge(lru_gates, 16 * (d + 1))
                for m in range(KT):
                    a.activation(lru_t[:, m, :], lru_a[:, m, :], ACT.Tanh, scale=lam[:, 5, m, d:d + 1])
                for m in range(KT):
                    a.activation(lru_a[:, m, :], lru_a[:, m, :], ACT.Exp,
                                 scale=lam[:, 6, m, d:d + 1]).then_inc(lru_exp, 1)
                for i in range(4):
                    a.wait_ge(lru_sq, 4 * d + i + 1)
                    a.activation(lru_t[:, 2 * i:2 * i + 2, :], lru_t[:, 2 * i:2 * i + 2, :],
                                 ACT.Sqrt).then_inc(lru_root, 1)

            def merge_gate(name, col, dst):
                for i in range(4):
                    wait_product(a, name, i)
                    for m in range(2):
                        a.activation(dst[:, 2 * i + m, :], ps(name, i)[:, m * T:(m + 1) * T], ACT.Sigmoid,
                                     bias=par[:, 2 * i + m, col:col + 1]).then_inc(mgate_ready, 1)

            lru(0)
            a.wait_ge(conv_ready, 4)
            merge_gate("ga", P_GATE_B, gate_a)
            a.wait_ge(ln_ready, 1)
            for m in range(KT):
                a.activation(cv[:, m, :], cv[:, m, :], ACT.Silu, bias=par[:, m, P_LN_B:P_LN_B + 1],
                             scale=par[:, m, P_LN_G:P_LN_G + 1]).then_inc(swish_ready, 1)
            lru(1)
            a.wait_ge(xc_ready, 4)
            merge_gate("gb", P_GATE_B + 1, gate_b)

            def squares(i, ready, done):
                a.wait_ge(ready, i + 1)
                a.activation(lru_a[:, 2 * i:2 * i + 2, :], xT[:, 2 * i:2 * i + 2, :], ACT.Square).then_inc(done, 1)

            for i in range(4):
                squares(i, x1_ready, x1_sq)
            root(4, stat)
            for i in range(4):
                wait_product(a, "q", i)
                a.activation(qT[:, 2 * i:2 * i + 2, :], pair(ps("q", i)), ACT.Copy).then_inc(q_ready, 1)
            for h in range(HEADS):
                a.wait_ge(smax_ready, h + 1)
                for t in range(TT):
                    a.activation(prob[:, h, t, :], ps("score", h)[:, t * T:(t + 1) * T], ACT.Exp,
                                 bias=sm[:, 1, h, t:t + 1], scale=HD ** -0.5,
                                 accum_out=sm[:, 2, h, t:t + 1]).then_inc(sexp_ready, 1)
            for name, i in (("probT", 0), ("probT", 1), ("attn", 0), ("probT", 2), ("attn", 1), ("probT", 3),
                            ("attn", 2), ("attn", 3)):
                wait_product(a, name, i)
                if name == "probT":
                    a.activation(probT[:, i, :, :], pair(ps(name, i)), ACT.Copy).then_inc(probT_ready, 1)
                else:
                    a.activation(attnT[:, 2 * i:2 * i + 2, :], pair(ps(name, i)), ACT.Copy).then_inc(attn_ready, 1)
            for i in range(4):
                squares(i, xf_ready, xf_sq)
            a.dma_start(gfin_row, g_final).then_inc(late_in, 16)
            root(5, stat)
            for i in range(4):
                wait_product(a, "htok", i)
                a.activation(h_tok[:, i // 2, 512 * (i % 2):512 * (i % 2) + 512], ps("htok", i)[:],
                             ACT.Copy).then_inc(htok_ready, 1)
            a.wait_ge(top_ready, 1)
            for t in range(TT):
                a.activation(top_g[:, t, 0:TOP], top_v[:, t, 0:TOP], ACT.Exp, bias=t1[:, t, 0:1],
                             accum_out=t1[:, t, 1:2]).then_inc(texp_ready, 1)
            for i in range(2):
                wait_product(a, "gfin", i)
                a.activation(gfin[:, 512 * i:512 * (i + 1)], ps("gfin", i)[:], ACT.Copy).then_inc(gfin_ready, 1)
            wait_product(a, "gateT")
            a.activation(gateT[:], ps("gateT")[0:NE, 0:T].rearrange("p (t c) -> p t c", t=TT),
                         ACT.Copy).then_inc(gateT_ready, 1)

            wait_product(a, "gateT")
            a.wait_ge(gathered, 1)
            a.activation(xg, xg_ps, ACT.Copy).then_inc(xg_ready, 1)
            a.wait_ge(count_ready, 2)
            jobs = a.value_load(n_i[0:1, 0:1], min_val=NE, max_val=JOBS_MAX)
            with a.Fori(0, jobs) as j:
                a.wait_ge(gclip_ready, j + 1)
                a.activation(sg, gc, ACT.Sigmoid, scale=SWIGLU_ALPHA).then_inc(sigm_ready, 1)
                a.wait_ge(gathered, j + 2)
                a.activation(xg, xg_ps, ACT.Copy).then_inc(xg_ready, 1)
                a.wait_ge(chunk_used, SLOTS * j + 2 * SLOTS)
                a.activation(job_out, bank_g[:], ACT.Copy).then_inc(job_out_ready, 1)

            a.wait_ge(y_done, 1)
            for t in range(TT):
                a.activation(y_sb[:, t, :], y_ps[:, t, :], ACT.Square, accum_out=fin[:, t:t + 1]).then_inc(ysum_ready, 1)
            a.wait_ge(yvar_ready, 1)
            a.activation(fin[:, 0:TT], fin[:, 0:TT], ACT.Sqrt).then_inc(yroot_ready, 1)

        @block.tensor
        def _(pe):
            def product_bank(name, i=0):
                n = AT[(name, i)]
                if n >= NBANK:
                    pe.wait_ge(*read[PRODUCTS[n - NBANK]])
                return bank[n % NBANK]

            def sum_channels(name, src, start_wait):
                dst = product_bank(name)
                for s, v in start_wait:
                    pe.wait_ge(s, v)
                for k in range(KT):
                    last = nc.tensor.matmul(dst[:, 0:T], ones[:], src[:, k, :], start=k == 0, stop=k == KT - 1)
                last.then_inc(product, 1)

            def project(name, i, src, token_major=False):
                n = CHUNK_AT[(name, i)]
                dst = product_bank(name, i)
                w = pre_slot[n % PRE_SLOTS]
                pe.wait_ge(pre_loaded[n % PRE_SLOTS], 16 * (n // PRE_SLOTS + 1))
                for m in range(2):
                    for k in range(KT):
                        if token_major:
                            lhsT, rhs = src[:, k, m * P:(m + 1) * P], w[:, k, :]
                        else:
                            lhsT, rhs = w[:, k, m * P:(m + 1) * P], src[:, k, :]
                        last = nc.tensor.matmul(dst[:, m * T:(m + 1) * T], lhsT, rhs, start=k == 0, stop=k == KT - 1)
                last.then_inc(product, 1)

            pe.wait_ge(consts, CONSTS)
            sum_channels("sum_x2", lru_a, [(x_sq, 1)])
            sum_channels("sum_m2", lru_u, [(m_sq, 1)])
            pe.wait_ge(h_ready, KT)
            for i in range(4):
                project("cg", i, hT)
                project("cv", i, hT)
            for i in range(4):
                project("xr", i, hT)
            for i in range(4):
                project("gr", i, hT)
            pe.wait_ge(mem_ready, KT)
            for i in range(4):
                project("k", i, memT)
            project("v", 0, memT, token_major=True)
            sum_channels("ln_mean", cv, [(conv_ready, 4)])
            for i in range(1, 4):
                project("v", i, memT, token_major=True)
            sum_channels("ln_var", lru_a, [(ln_sq, 1)])

            def lru_gates_of(d):
                for i in range(4):
                    for g, name in enumerate((f"ra{d}", f"ri{d}")):
                        dst = product_bank(name, i)
                        for m in range(2):
                            last = nc.tensor.matmul(dst[:, m * T:(m + 1) * T], lru_gate_w[:, 2 * d + g, 2 * i + m, :],
                                                    xc[:, 2 * i + m, :], start=True, stop=True)
                        last.then_inc(product, 1)

            pe.wait_ge(lruw_in, 16 * 8)
            pe.wait_ge(xc_ready, 4)
            lru_gates_of(0)
            for i in range(4):
                project("ga", i, hT)
            lru_gates_of(1)
            for i in range(4):
                project("gb", i, hT)
            pe.wait_ge(swish_ready, KT)
            for i in range(4):
                project("yb", i, cv)
            pe.wait_ge(lru_ready, 1)
            for i in range(4):
                project("ya", i, gl)
            pe.wait_ge(merged, 4)
            for i in range(4):
                project("wo", i, gate_a)
            sum_channels("sum_x1", lru_a, [(x1_sq, 4)])
            pe.wait_ge(h_ready, 2 * KT)
            for i in range(4):
                project("q", i, hT)
            for h in range(HEADS):
                dst = product_bank("score", h)
                pe.wait_ge(q_ready, h + 1)
                for t in range(TT):
                    for k in range(2):
                        last = nc.tensor.matmul(dst[:, t * T:(t + 1) * T], qT[:, 2 * h + k, t * P:(t + 1) * P],
                                                keyT[:, 2 * h + k, :], start=k == 0, stop=k == 1)
                last.then_inc(product, 1)

            def transpose_prob(h):
                dst = product_bank("probT", h)
                pe.wait_ge(prob_ready, h + 1)
                for m in range(TT):
                    for t in range(TT):
                        last = nc.tensor.transpose(dst[:, m * T + t * P:m * T + (t + 1) * P],
                                                   prob[:, h, t, m * P:(m + 1) * P], ident[:])
                last.then_inc(product, 1)

            def attend(h):
                dst = product_bank("attn", h)
                pe.wait_ge(probT_ready, h + 1)
                for k in range(2):
                    for m in range(TT):
                        last = nc.tensor.matmul(dst[:, k * T:(k + 1) * T], val[:, m, h * HD + k * P:h * HD + (k + 1) * P],
                                                probT[:, h, m, :], start=m == 0, stop=m == TT - 1)
                last.then_inc(product, 1)

            transpose_prob(0)
            for h in range(HEADS):
                if h + 1 < HEADS:
                    transpose_prob(h + 1)
                attend(h)
            pe.wait_ge(attn_ready, 4)
            for i in range(4):
                project("o", i, attnT)
            sum_channels("sum_xf", lru_a, [(xf_sq, 4)])
            pe.wait_ge(h_ready, 3 * KT)
            pe.wait_ge(router_in, 48)
            dst = product_bank("logit")
            for t in range(TT):
                for k in range(KT):
                    nc.tensor.matmul(dst[:, t * NE:(t + 1) * NE], hT[:, k, t * P:(t + 1) * P], router[:, k, :],
                                     start=k == 0, stop=False)
                last = nc.tensor.matmul(dst[:, t * NE:(t + 1) * NE], ones[0:1, :], rb_row[:], start=False, stop=True)
            last.then_inc(product, 1)
            for i in range(4):
                dst = product_bank("htok", i)
                for k in range(4):
                    last = nc.tensor.transpose(dst[:, k * P:(k + 1) * P],
                                               hT[:, 4 * (i % 2) + k, (i // 2) * P:(i // 2 + 1) * P], ident[:])
                last.then_inc(product, 1)
            pe.wait_ge(late_in, 16)
            for i in range(2):
                nc.tensor.matmul(product_bank("gfin", i)[:], ones[0:1, :], gfin_row[:, 512 * i:512 * (i + 1)],
                                 start=True, stop=True).then_inc(product, 1)
            for t in range(TT):
                for k in range(KT):
                    last = nc.tensor.matmul(y_ps[:, t, k * P:(k + 1) * P], xT[:, k, t * P:(t + 1) * P], ident[:],
                                            start=k % 4 == 0, stop=False, skip_group_check=True)
            last.then_inc(chunk_used, SLOTS)
            dst = product_bank("rank")
            pe.wait_ge(mask_ready, 1)
            nc.tensor.matmul(dst[:, 0:NE], before[:], mask[:, 0, :], start=True, stop=True)
            nc.tensor.matmul(dst[:, NE:2 * NE], ones[:], mask[:, 0, :], start=True, stop=False)
            nc.tensor.matmul(dst[:, NE:2 * NE], before[:], mask[:, 1, :], start=False, stop=True)
            for t in range(TT):
                last = nc.tensor.matmul(dst[:, 2 * NE:3 * NE], ones[:], mask[:, t, :], start=t == 0, stop=t == TT - 1)
            last.then_inc(product, 1)
            dst = product_bank("gateT")
            pe.wait_ge(gate_ready, 1)
            for t in range(TT):
                last = nc.tensor.transpose(dst[0:NE, t * P:(t + 1) * P], gate[:, t, :], ident[:])
            last.then_inc(product, 1)

            def gather():
                for k in range(KT):
                    for t in range(TT):
                        last = nc.tensor.matmul(bank_x[:, k * CAP:(k + 1) * CAP], h_tok[:, t, k * P:(k + 1) * P],
                                                pick[:, t, :], start=t == 0, stop=t == TT - 1)
                last.then_inc(gathered, 1)

            for i in range(NBANK):
                pe.wait_ge(*read[PRODUCTS[len(PRODUCTS) - NBANK + i]])
            pe.wait_ge(htok_ready, 4)
            pe.wait_ge(pick_ready, 1)
            gather()
            pe.wait_ge(count_ready, 2)
            jobs = pe.value_load(n_i[0:1, 0:1], min_val=NE, max_val=JOBS_MAX)
            with pe.Fori(0, jobs) as j:
                pe.wait_ge(pick_ready, j + 1)
                for t in range(TT):
                    last = nc.tensor.transpose(bank_a[:, t * P:(t + 1) * P], wpick[:, t, :], ident[:])
                last.then_inc(wpickT_done, 1)
                pe.wait_ge(bias_in, 16 * j + 16)
                for dst, col in ((bank_g, 0), (bank_u, F)):
                    for half in range(2):
                        last = nc.tensor.matmul(dst[CAP * half:CAP * (half + 1), :], ones[0:1, 0:CAP],
                                                bup_row[0:1, col + 512 * half:col + 512 * (half + 1)],
                                                start=True, stop=False)
                last.then_inc(bias_used, 1)
                pe.wait_ge(xg_ready, j + 1)
                for k in range(KT):
                    pe.wait_ge(loaded[k], 16 * j + 16)
                    for dst, col in ((bank_g, 0), (bank_u, F)):
                        for half in range(2):
                            last = nc.tensor.matmul(dst[CAP * half:CAP * (half + 1), :], xg[:, k, :],
                                                    ring[:, k, col + 512 * half:col + 512 * (half + 1)],
                                                    start=False, stop=k == KT - 1)
                    last.then_inc(chunk_used, 1)
                pe.wait_ge(pick_ready, j + 2)
                gather()
                pe.wait_ge(act_ready, j + 1)
                pe.wait_ge(wpickT_ready, j + 1)
                for c in range(4):
                    last = nc.tensor.transpose(bank_a[:, c * P:(c + 1) * P], act[:, c * P:(c + 1) * P], ident[:])
                last.then_inc(actT_done, 1)
                pe.wait_ge(actT_ready, j + 1)
                for k in range(KT):
                    s = UP_CHUNKS + k // 2
                    if k % 2 == 0:
                        pe.wait_ge(loaded[s], 16 * j + 16)
                    for half in range(2):
                        col = D * (k % 2) + 512 * half
                        last = nc.tensor.matmul(bank_g[CAP * half:CAP * (half + 1), :],
                                                actT[:, k % 4, CAP * (k // 4):CAP * (k // 4 + 1)],
                                                ring[:, s, col:col + 512], start=k == 0, stop=k == KT - 1)
                    if k % 2:
                        last.then_inc(chunk_used, 1)
                pe.wait_ge(job_out_ready, j + 1)
                for t in range(TT):
                    for half in range(2):
                        nc.tensor.matmul(y_ps[:, t, 512 * half:512 * (half + 1)],
                                         wpickT[CAP * half:CAP * (half + 1), t, :],
                                         job_out[CAP * half:CAP * (half + 1), :],
                                         start=False, stop=False, skip_group_check=True)
            pe.wait_ge(gateT_ready, 1)
            for t in range(TT):
                for half in range(2):
                    last = nc.tensor.matmul(y_ps[:, t, 512 * half:512 * (half + 1)], gateT[:, t, :],
                                            bd_sb[:, 512 * half:512 * (half + 1)], start=False, stop=True,
                                            skip_group_check=True)
            last.then_inc(y_done, 1)

        @block.vector
        def _(v):
            done = [0]

            def step(ins, lag=0):
                done[0] += 1
                ins.then_inc(v_chain, 1)
                if done[0] > lag:
                    v.wait_ge(v_chain, done[0] - lag)

            def variance(name, buf):
                wait_product(v, name)
                nc.vector.tensor_scalar(buf[:], ps(name)[:, 0:T], 1.0 / D, EPS, ALU.mult, ALU.add).then_inc(var_ready, 1)

            def inverse_root(n, buf):
                v.wait_ge(root_ready, n)
                step(nc.vector.reciprocal(buf[:], buf[:]))

            def rms(dst, src, buf, col, ready):
                for k in range(KT):
                    nc.vector.scalar_tensor_tensor(dst[:, k, :], src[:, k, :], par[:, k, col:col + 1], buf[:],
                                                   ALU.mult, ALU.mult).then_inc(ready, 1)

            v.wait_ge(consts, CONSTS)
            v.wait_ge(x_in, 16)
            v.wait_ge(par_in, 16)
            variance("sum_x2", stat)
            variance("sum_m2", mstat)
            inverse_root(1, stat)
            rms(hT, xT, stat, P_MIX_G, h_ready)
            inverse_root(2, mstat)
            v.wait_ge(mem_in, 16)
            rms(memT, memT, mstat, P_MEM_G, mem_ready)

            lam_in = par[:, :, P_LAM:P_LAM + 2]
            nc.vector.scalar_tensor_tensor(lam[:, 0], lam_in, -1.0, lam_in, ALU.mult, ALU.min).then_inc(lam_abs, 1)
            v.wait_ge(lam_exp, 1)
            step(nc.vector.tensor_scalar(lam[:, 2], lam[:, 1], 2.0, None, ALU.add))
            step(nc.vector.reciprocal(lam[:, 2], lam[:, 2]))
            step(nc.vector.tensor_tensor(lam[:, 2], lam[:, 1], lam[:, 2], ALU.mult))
            step(nc.vector.tensor_tensor(lam[:, 3], lam[:, 2], lam[:, 2], ALU.mult))
            step(nc.vector.memset(lam[:, 4], 1.0 / 17))
            for n in (15, 13, 11, 9, 7, 5, 3, 1):
                step(nc.vector.tensor_tensor(lam[:, 4], lam[:, 4], lam[:, 3], ALU.mult))
                step(nc.vector.tensor_scalar(lam[:, 4], lam[:, 4], 1.0 / n, None, ALU.add))
            step(nc.vector.scalar_tensor_tensor(lam[:, 4], lam[:, 4], 2.0, lam[:, 2], ALU.mult, ALU.mult))
            step(nc.vector.tensor_scalar(lam[:, 3], lam_in, -1.0, 0.0, ALU.mult, ALU.max))
            step(nc.vector.tensor_tensor(lam[:, 4], lam[:, 3], lam[:, 4], ALU.add))
            step(nc.vector.tensor_scalar(lam[:, 5], lam[:, 4], 8.0, None, ALU.mult))
            nc.vector.tensor_scalar(lam[:, 6], lam[:, 4], -8.0, None, ALU.mult).then_inc(lam_ready, 1)

            def conv(dst, src, taps, w_col, b_col, m0, ready):
                for tap in range(taps):
                    for m in (m0, m0 + 1):
                        x = src[:, m, tap:tap + T]
                        w = par[:, m, w_col + tap:w_col + tap + 1]
                        if tap == 0:
                            ins = nc.vector.tensor_scalar(dst[:, m, :], x, w, par[:, m, b_col:b_col + 1],
                                                          ALU.mult, ALU.add)
                        else:
                            ins = nc.vector.scalar_tensor_tensor(dst[:, m, :], x, w, dst[:, m, :], ALU.mult, ALU.add)
                        if tap == taps - 1 and m == m0 + 1:
                            ins.then_inc(ready, 1)
                        else:
                            step(ins, lag=1)

            for i in range(4):
                wait_product(v, "cv", i)
                v.wait_ge(sig_ready, i + 1)
                nc.vector.tensor_tensor(glu[:, 2 * i:2 * i + 2, CONF_LEFT:CONF_LEFT + T], pair(ps("cv", i)),
                                        sig[:, i % 2].rearrange("p (m t) -> p m t", m=2), ALU.mult).then_inc(glu_ready, 1)
                v.wait_ge(glu_ready, i + 1)
                conv(cv, glu, CONF_TAPS, P_DW_W, P_DW_B, 2 * i, conv_ready)
            v.wait_ge(xr_ready, 4)
            for i in range(4):
                conv(xc, xr, LRU_TAPS, P_LRU_W, P_LRU_CB, 2 * i, xc_ready)

            wait_product(v, "ln_mean")
            nc.vector.tensor_scalar(mstat[:], ps("ln_mean")[:, 0:T], 1.0 / D, None, ALU.mult).then_inc(mean_read, 1)
            v.wait_ge(mean_read, 1)
            v.wait_ge(conv_ready, 4)
            spread = lambda s: s[:].rearrange("p (a t) -> p a t", a=1).to_broadcast([P, KT, T])
            nc.vector.tensor_tensor(cv[:], cv[:], spread(mstat), ALU.subtract).then_inc(centred, 1)
            variance("ln_var", stat)
            inverse_root(3, stat)
            v.wait_ge(centred, 1)
            nc.vector.tensor_tensor(cv[:], cv[:], spread(stat), ALU.mult).then_inc(ln_ready, 1)

            v.wait_ge(xc_ready, 4)
            for d in range(2):
                for i in range(4):
                    pr = slice(2 * i, 2 * i + 2)
                    tmp = sig[:, i % 2].rearrange("p (m t) -> p m t", m=2)
                    v.wait_ge(lru_gates, 16 * d + 4 * i + 4)
                    step(nc.vector.tensor_tensor(lru_u[:, pr, :], lru_u[:, pr, :], xc[:, pr, :], ALU.mult), lag=1)
                    v.wait_ge(lru_exp, KT * d + 2 * i + 2)
                    step(nc.vector.tensor_tensor(tmp, lru_a[:, pr, :], lru_a[:, pr, :], ALU.mult))
                    nc.vector.scalar_tensor_tensor(lru_t[:, pr, :], tmp, 1.0, lru_t[:, pr, :], ALU.add,
                                                   ALU.mult).then_inc(lru_sq, 1)
                for i in range(4):
                    pr = slice(2 * i, 2 * i + 2)
                    v.wait_ge(lru_root, 4 * d + i + 1)
                    step(nc.vector.tensor_tensor(lru_u[:, pr, :], lru_u[:, pr, :], lru_t[:, pr, :], ALU.mult))
                    for m in (2 * i, 2 * i + 1):
                        dst, c, u = (x[:, m, :] for x in ((lru_t if d else lru_h), lru_a, lru_u))
                        if d:
                            dst, c, u = dst[:, ::-1], c[:, ::-1], u[:, ::-1]
                        nc.vector.tensor_tensor_scan(dst, c, u, 0.0, ALU.mult, ALU.add).then_inc(lru_scanned, 1)
            v.wait_ge(lru_scanned, 2 * KT)
            step(nc.vector.tensor_tensor(lru_h[:], lru_h[:], lru_t, ALU.add))
            v.wait_ge(gl_ready, 4)
            nc.vector.tensor_tensor(gl[:], gl[:], lru_h[:], ALU.mult).then_inc(lru_ready, 1)

            for i in range(4):
                pr = slice(2 * i, 2 * i + 2)
                wait_product(v, "yb", i)
                v.wait_ge(mgate_ready, 10 + 2 * i)
                nc.vector.tensor_tensor(gate_b[:, pr, :], pair(ps("yb", i)), gate_b[:, pr, :], ALU.mult).then_inc(yb_read, 1)
            for i in range(4):
                pr = slice(2 * i, 2 * i + 2)
                wait_product(v, "ya", i)
                nc.vector.tensor_tensor(gate_a[:, pr, :], pair(ps("ya", i)), gate_a[:, pr, :], ALU.mult).then_inc(ya_read, 1)
                v.wait_ge(ya_read, i + 1)
                v.wait_ge(yb_read, i + 1)
                nc.vector.tensor_tensor(gate_a[:, pr, :], gate_a[:, pr, :], gate_b[:, pr, :], ALU.add).then_inc(merged, 1)

            def residual(name, ready):
                for i in range(4):
                    pr = slice(2 * i, 2 * i + 2)
                    wait_product(v, name, i)
                    nc.vector.tensor_tensor(xT[:, pr, :], pair(ps(name, i)), xT[:, pr, :], ALU.add).then_inc(ready, 1)

            residual("wo", x1_ready)
            variance("sum_x1", stat)
            inverse_root(4, stat)
            rms(hT, xT, stat, P_XA_G, h_ready)

            for h in range(HEADS):
                wait_product(v, "score", h)
                step(nc.vector.reduce_max(sm[:, 0, h, :], pair(ps("score", h)), AX.X))
                nc.vector.tensor_scalar(sm[:, 1, h, :], sm[:, 0, h, :], -HD ** -0.5, None, ALU.mult).then_inc(smax_ready, 1)
            for h in range(HEADS):
                v.wait_ge(sexp_ready, 2 * h + 2)
                step(nc.vector.reciprocal(sm[:, 3, h, :], sm[:, 2, h, :]))
                for t in range(TT):
                    ins = nc.vector.tensor_scalar(prob[:, h, t, :], prob[:, h, t, :], sm[:, 3, h, t:t + 1], None, ALU.mult)
                    if t == 0:
                        step(ins)
                    else:
                        ins.then_inc(prob_ready, 1)

            residual("o", xf_ready)
            variance("sum_xf", stat)
            inverse_root(5, stat)
            rms(hT, xT, stat, P_FFN_G, h_ready)

            step(nc.vector.tensor_copy(iota_f[:], iota_i[:]))
            step(nc.vector.tensor_scalar(iota_c[:], iota_f[:], float(CAP), float(CAP), ALU.is_ge, ALU.mult))
            step(nc.vector.tensor_tensor(iota_c[:], iota_f[:], iota_c[:], ALU.subtract))
            wait_product(v, "logit")
            nc.vector.tensor_copy(lg[:], ps("logit")[:, 0:TT * NE].rearrange("p (t e) -> p t e", t=TT)).then_inc(logit_read, 1)
            v.wait_ge(logit_read, 1)
            for t in range(TT):
                step(nc.vector.max(top_v[:, t, :], lg[:, t, :]))
                step(nc.vector.max_index(top_i[:, t, :], top_v[:, t, :], lg[:, t, :]))
            step(nc.vector.tensor_copy(top_f[:], top_i[:]))
            nc.vector.tensor_scalar(t1[:, :, 0:1], top_v[:, :, 0:1], -1.0, None, ALU.mult).then_inc(top_ready, 1)
            for t in range(TT):
                step(nc.vector.tensor_scalar(mask[:, t, :], iota_f[:, 0:NE], top_f[:, t, 0:1], None, ALU.is_equal))
                for n in range(1, TOP):
                    ins = nc.vector.scalar_tensor_tensor(mask[:, t, :], iota_f[:, 0:NE], top_f[:, t, n:n + 1],
                                                         mask[:, t, :], ALU.is_equal, ALU.add)
                    if t == TT - 1 and n == TOP - 1:
                        ins.then_inc(mask_ready, 1)
                    else:
                        step(ins)
            v.wait_ge(texp_ready, TT)
            step(nc.vector.reciprocal(t1[:, :, 2:3], t1[:, :, 1:2]))
            for t in range(TT):
                step(nc.vector.tensor_scalar(top_g[:, t, 0:TOP], top_g[:, t, 0:TOP], t1[:, t, 2:3], None, ALU.mult))
                step(nc.vector.tensor_scalar(gate[:, t, :], iota_f[:, 0:NE], top_f[:, t, 0:1], top_g[:, t, 0:1],
                                             ALU.is_equal, ALU.mult))
                for n in range(1, TOP):
                    step(nc.vector.tensor_scalar(oh[:], iota_f[:, 0:NE], top_f[:, t, n:n + 1], top_g[:, t, n:n + 1],
                                                 ALU.is_equal, ALU.mult))
                    step(nc.vector.tensor_tensor(gate[:, t, :], gate[:, t, :], oh[:], ALU.add))
            for r in range(MAX_ROUNDS + 1):
                nc.vector.tensor_copy(gatej[:, :, NE * r:NE * (r + 1)], gate[:]).then_inc(gate_ready, 1)

            wait_product(v, "rank")
            v.wait_ge(mask_ready, 1)
            rank_ps = ps("rank")[:, 0:TT * NE].rearrange("p (t e) -> p t e", t=TT)
            step(nc.vector.scalar_tensor_tensor(rank[:], rank_ps, 1.0, mask[:], ALU.add, ALU.mult))
            for r in range(MAX_ROUNDS + 1):
                step(nc.vector.tensor_scalar(pos[:, :, NE * r:NE * (r + 1)], rank[:], -1.0 - CAP * r, None, ALU.add))
            nc.vector.reduce_max(count[:, 0:1], ps("rank")[0:1, 2 * NE:3 * NE], AX.X).then_inc(rank_read, 1)
            v.wait_ge(rank_read, 1)
            step(nc.vector.tensor_scalar(count[:, 1:2], count[:, 0:1], float(CAP), 1.0, ALU.is_gt, ALU.add))
            for r in range(2, MAX_ROUNDS):
                step(nc.vector.scalar_tensor_tensor(count[:, 1:2], count[:, 0:1], float(CAP * r), count[:, 1:2],
                                                    ALU.is_gt, ALU.add))
            nc.vector.tensor_scalar(n_i[:, 0:1], count[:, 1:2], float(NE), None, ALU.mult).then_inc(count_ready, 1)
            nc.vector.tensor_copy(n_i[:, 1:2], count[:, 1:2]).then_inc(count_ready, 1)

            def picks(j):
                for t in range(TT):
                    nc.vector.tensor_scalar(pick[:, t, :], iota_f[:, 0:CAP], pos[:, t, bass.ds(j, 1)], None, ALU.is_equal)
                for t in range(TT):
                    last = nc.vector.tensor_scalar(wpick[:, t, :], iota_c[:], pos[:, t, bass.ds(j, 1)],
                                                   gatej[:, t, bass.ds(j, 1)], ALU.is_equal, ALU.mult)
                last.then_inc(pick_ready, 1)

            v.wait_ge(gate_ready, MAX_ROUNDS + 1)
            picks(0)
            v.wait_ge(count_ready, 2)
            jobs = v.value_load(n_i[0:1, 0:1], min_val=NE, max_val=JOBS_MAX)
            with v.Fori(0, jobs) as j:
                v.wait_ge(wpickT_done, j + 1)
                nc.vector.tensor_copy(wpickT, bank_a[:, 0:TT * P].rearrange("p (t c) -> p t c", t=TT)).then_inc(wpickT_ready, 1)
                picks(v.snap(j + 1))
                v.wait_ge(chunk_used, SLOTS * j + SLOTS + UP_CHUNKS)
                nc.vector.tensor_scalar(gc, bank_g[:], LIMIT, None, ALU.min).then_inc(gclip_ready, 1)
                nc.vector.tensor_scalar(uc, bank_u[:], LIMIT, -LIMIT, ALU.min, ALU.max).then_inc(uclip_ready, 1)
                v.wait_ge(uclip_ready, j + 1)
                nc.vector.scalar_tensor_tensor(uc, uc, 1.0, gc, ALU.add, ALU.mult).then_inc(ug_ready, 1)
                v.wait_ge(ug_ready, j + 1)
                v.wait_ge(sigm_ready, j + 1)
                nc.vector.tensor_tensor(act, uc, sg, ALU.mult).then_inc(act_ready, 1)
                v.wait_ge(actT_done, j + 1)
                nc.vector.tensor_copy(actT, bank_a[:].rearrange("p (c n) -> p c n", c=4)).then_inc(actT_ready, 1)

            v.wait_ge(ysum_ready, TT)
            nc.vector.tensor_scalar(fin[:, 0:TT], fin[:, 0:TT], 1.0 / D, EPS, ALU.mult, ALU.add).then_inc(yvar_ready, 1)
            v.wait_ge(yroot_ready, 1)
            step(nc.vector.reciprocal(fin[:, TT:2 * TT], fin[:, 0:TT]))
            v.wait_ge(gfin_ready, 2)
            for t in range(TT):
                nc.vector.scalar_tensor_tensor(y_sb[:, t, :], y_ps[:, t, :], fin[:, TT + t:TT + t + 1], gfin,
                                               ALU.mult, ALU.mult).then_inc(y_ready, 1)


_PLAIN = ["w_in", "lru_w_a", "lru_w_i", "w_rnn_out", "w_conf_out", "w_out", "xa_w_q", "xa_w_kv", "xa_w_o",
          "router_w", "router_b", "exp_w_up", "exp_b_up", "exp_w_down", "exp_b_down"]


def kernel(**inputs):
    import numpy as np
    import concourse.bacc as bacc
    from concourse.bass_utils import run_bass_kernel_spmd

    a = {k: np.asarray(v) for k, v in inputs.items()}
    rows = [a["norm_mix_g"], a["lru_conv_b"], a["lru_b_a"][0], a["lru_b_i"][0], a["lru_lambda"][0], a["conf_dw_b"],
            a["conf_ln_g"], a["conf_ln_b"], a["norm_xa_g"], a["norm_mem_g"], a["norm_ffn_g"],
            a["b_branch_gate"][0], a["lru_conv_w"][0], a["conf_dw_w"][0]]
    par = np.ascontiguousarray(np.concatenate(rows, axis=0).reshape(N_PAR, KT, P).transpose(2, 1, 0))

    def channel_major(x):
        return np.ascontiguousarray(x[0].reshape(T, KT, P).transpose(2, 1, 0))

    arrays = {"xT": channel_major(a["x"]), "memT": channel_major(a["mem"]), "par": par}
    for name in _PLAIN:
        arrays[name] = np.ascontiguousarray(a[name] if name == "router_b" else a[name][0])
    arrays["final_norm_g"] = np.ascontiguousarray(a["final_norm_g"].reshape(1, D))

    nc = bacc.Bacc("TRN2", target_bir_lowering=False, num_devices=1)
    aps = [nc.dram_tensor("in_" + k, x.shape, mybir.dt.from_np(x.dtype), kind="ExternalInput").ap()
           for k, x in arrays.items()]
    out = nc.dram_tensor("out_y", (T, D), F32, kind="ExternalOutput").ap()
    encoder_kernel(nc, *aps, out)
    r = run_bass_kernel_spmd(nc, [{"in_" + k: x for k, x in arrays.items()}], core_ids=[0])
    return r.results[0]["out_y"].reshape(1, T, D)
```

```python
from contextlib import ExitStack

import concourse.bass as bass
from concourse import mybir

F32 = mybir.dt.float32
F32R = mybir.dt.float32r
I32 = mybir.dt.int32
U32 = mybir.dt.uint32
ALU = mybir.AluOpType
ACT = mybir.ActivationFunctionType
AX = mybir.AxisListType

P = 128
D = 1024
KT = D // P
T = 256
TT = T // P
HEADS = 4
HD = D // HEADS
NE = 32
TOP = 4
F = D
EPS = 1e-5
SWIGLU_ALPHA, LIMIT = 1.702, 7.0
LRU_TAPS, CONF_TAPS = 4, 31
LRU_LEFT, CONF_LEFT = 2, 15

CHUNK = 2048
COLS = CHUNK // KT
PRE_SLOTS = 3
SPLIT_BUFS = 2
UP_CHUNKS = KT
DOWN_CHUNKS = KT // 2
JOB_CHUNKS = UP_CHUNKS + DOWN_CHUNKS
SLOTS = 16
MAIN_SLOTS = 12
GROUP = SLOTS // 4
CAP = 64
MAX_ROUNDS = T // CAP
JOBS_MAX = NE * MAX_ROUNDS
POS_W = NE * (MAX_ROUNDS + 1)
NBANK = 4

(P_MIX_G, P_LRU_CB, P_BA, P_BI, P_LAM, P_DW_B, P_LN_G, P_LN_B, P_XA_G, P_MEM_G, P_FFN_G, P_GATE_B,
 P_LRU_W, P_DW_W, N_PAR) = (0, 1, 2, 4, 6, 8, 9, 10, 11, 12, 13, 14, 16, 20, 51)

WEIGHTED = ("cg", "cv", "xr", "gr", "k", "v", "ga", "gb", "ya", "yb", "wo", "q", "o")
PRODUCTS = (
    [("sum_x2", 0)] + [(n, 0) for n in ("cg", "cv", "xr", "gr")] + [("sum_m2", 0)]
    + [(n, i) for i in range(1, 4) for n in ("cg", "cv", "xr", "gr")]
    + [("k", i) for i in range(4)] + [("ga", 0)]
    + [("ln_mean", 0), ("ga", 1)] + [(n, i) for i in range(4) for n in ("ra0", "ri0")]
    + [("ga", 2), ("ln_var", 0), ("ga", 3)]
    + [("gb", 0)] + [(n, i) for i in range(2) for n in ("ra1", "ri1")]
    + [("gb", 1)] + [(n, i) for i in range(2, 4) for n in ("ra1", "ri1")] + [("gb", 2), ("gb", 3)]
    + [("yb", i) for i in range(4)] + [("ya", i) for i in range(4)]
    + [("v", 0)]
    + [("wo", i) for i in range(4)] + [("v", 1), ("sum_x1", 0), ("v", 2), ("v", 3)]
    + [("q", i) for i in range(4)]
    + [("score", h) for h in range(HEADS)]
    + [("probT", 0), ("probT", 1), ("attn", 0), ("probT", 2), ("attn", 1), ("probT", 3), ("attn", 2), ("attn", 3)]
    + [("o", i) for i in range(4)] + [("sum_xf", 0), ("gfin", 0), ("gfin", 1), ("logitT", 0), ("logit", 0)]
    + [("htok", i) for i in range(4)] + [("rank", 0)]
)
AT = {name: i for i, name in enumerate(PRODUCTS)}
CHUNKS = [x for x in PRODUCTS if x[0] in WEIGHTED]
CHUNK_AT = {name: i for i, name in enumerate(CHUNKS)}
SPLIT = [x for x in CHUNKS if x[0] not in ("k", "v")]
SPLIT_AT = {name: i for i, name in enumerate(SPLIT)}


def encoder_kernel(nc, xT_d, memT_d, par_d, w_in, lru_w_a, lru_w_i, w_rnn_out, w_conf_out, w_out,
                   w_q, w_kv, w_o, router_w, router_b, w_up, b_up, w_down, b_down, g_final, out):
    sources = {"xr": (w_in, 0), "gr": (w_in, D), "cv": (w_in, 2 * D), "cg": (w_in, 3 * D),
               "ga": (w_in, 4 * D), "gb": (w_in, 5 * D), "k": (w_kv, 0), "v": (w_kv, D),
               "ya": (w_rnn_out, 0), "yb": (w_conf_out, 0), "wo": (w_out, 0), "q": (w_q, 0),
               "o": (w_o, 0)}

    with ExitStack() as ctx:
        def sb(name, shape, dt=F32):
            return ctx.enter_context(nc.sbuf_tensor(name, shape, dt))

        def sem(name):
            return ctx.enter_context(nc.semaphore(name))

        def split_tile(name, shape, over):
            return nc.alloc_sbuf_tensor_at(name, shape, F32R, offset=over)

        def next_offset():
            return -(-nc.sbuf_base // 32) * 32

        place = {}
        place["ring"] = next_offset()
        ring = sb("ring", [P, MAIN_SLOTS, CHUNK])
        w_hi = split_tile("w_hi", [P, SPLIT_BUFS, KT, COLS], place["ring"])
        w_lo = split_tile("w_lo", [P, SPLIT_BUFS, KT, COLS], place["ring"] + SPLIT_BUFS * CHUNK * 4)
        lru_gate_w = ring[:, 4:6, :].rearrange("p s (a m n) -> p (s a) m n", m=KT, n=P)
        memT = ring[:, 6, :].rearrange("p (k t) -> p k t", k=KT)
        lru_t = ring[:, 8, :].rearrange("p (k t) -> p k t", k=KT)
        xc = ring[:, 7, :].rearrange("p (k t) -> p k t", k=KT)
        pre_slot = [ring[:, MAIN_SLOTS - PRE_SLOTS + i, :].rearrange("p (k n) -> p k n", k=KT)
                    for i in range(PRE_SLOTS)]

        def act_tile(name, width=T):
            place[name] = next_offset()
            return sb(name, [P, KT, width])

        xT = act_tile("xT")
        hT = act_tile("hT")
        glu = act_tile("glu", T + CONF_TAPS - 1)
        cv = act_tile("cv")
        xr = act_tile("xr", T + LRU_TAPS - 1)
        gl = act_tile("gl")
        keyT = act_tile("keyT")
        place["val"] = next_offset()
        val = sb("val", [P, TT, D])
        lru_a = act_tile("lru_a")
        lru_u = act_tile("lru_u")
        lru_h = act_tile("lru_h")
        gate_a, gate_b = glu[:, :, 0:T], xr[:, :, 0:T]
        qT = lru_a
        prob = lru_u[:, :, :].rearrange("p (h t) m -> p h t m", h=HEADS)
        probT = lru_h[:, :, :].rearrange("p (h t) m -> p h t m", h=HEADS)
        x_tile = lambda name, over: split_tile(name, [P, KT, T], place[over])
        x_hi = x_tile("x_hi", "hT")
        h1_lo, lru_hi, lru_lo = x_tile("h1_lo", "val"), x_tile("lru_hi", "lru_a"), x_tile("lru_lo", "lru_u")
        mid_lo, attn_lo = x_tile("mid_lo", "lru_h"), x_tile("attn_lo", "gl")
        h1_parts, swish_parts, lru_parts = (x_hi, h1_lo), (x_hi, h1_lo), (lru_hi, lru_lo)
        merged_parts, h2_parts, attn_parts = (x_hi, mid_lo), (x_hi, mid_lo), (x_hi, attn_lo)
        sig = sb("sig", [P, 2, 2 * T])
        lgT = sig[:, 0, 0:T]
        hot = sig[:, 1, 0:T].rearrange("p (t n e) -> p t n e", t=TT, n=TOP)
        ghot = sig[:, 1, T:2 * T].rearrange("p (t n e) -> p t n e", t=TT, n=TOP)
        par = sb("par", [P, KT, N_PAR])
        ident = sb("ident", [P, P])
        ones = sb("ones", [P, P])
        before = sb("before", [P, P])
        stat = sb("stat", [P, T])
        mstat = sb("mstat", [P, T])
        lam = sb("lam", [P, 7, KT, 2])
        router = sb("router", [P, KT, NE])
        rb_row = sb("rb_row", [1, NE])
        sm = sb("sm", [P, 4, HEADS, TT])
        lg = sb("lg", [P, TT, NE])
        top_v = sb("top_v", [P, TT, 8])
        top_i = sb("top_i", [P, TT, 8], U32)
        top_f = sb("top_f", [P, TT, 8])
        top_g = sb("top_g", [P, TT, 8])
        t1 = sb("t1", [P, TT, 4])
        iota_i = sb("iota_i", [P, P], I32)
        iota_f = sb("iota_f", [P, P])
        iota_c = sb("iota_c", [P, P])
        mask = sb("mask", [P, TT, NE])
        gate = sb("gate", [P, TT, NE])
        roff = sb("roff", [P, MAX_ROUNDS + 1])
        rank = sb("rank", [P, TT, NE])
        pos = sb("pos", [P, TT, POS_W])
        gatej = sb("gatej", [P, TT, POS_W])
        count = sb("count", [1, 4])
        n_i = sb("n_i", [1, 3], I32)
        h_tok = keyT[:, :, :].rearrange("p (t k) c -> p t (k c)", t=TT)
        gc, uc = val[:, 0, 0:512], val[:, 0, 512:1024]
        sg, act = val[:, 1, 0:512], val[:, 1, 512:1024]
        xg = lru_a[:, 0:2, :].rearrange("p a (h c) -> p (a h) c", c=P)
        xtok = lru_u[:, 1:3, :].rearrange("p a c -> p (a c)")
        actT = lru_a[:, 2:4, :].rearrange("p a (h c) -> p (a h) c", c=P)
        job_out = lru_a[:, 4:6, :].rearrange("p a c -> p (a c)")
        pick = lru_a[:, 6, 0:TT * CAP].rearrange("p (t c) -> p t c", t=TT)
        wpick = lru_a[:, 7, :].rearrange("p (t c) -> p t c", t=TT)
        wpickT = lru_u[:, 0, :].rearrange("p (t c) -> p t c", t=TT)
        bup_row = lru_h[0:1, :, :].rearrange("p k t -> p (k t)")
        more_slots = [x[:, :, :].rearrange("p k t -> p (k t)")[:, 0:CHUNK] for x in (glu, xr, gl, hT)]
        expert_slot = [ring[:, i, :] for i in range(MAIN_SLOTS)] + more_slots
        y_sb = xT[:, :, :].rearrange("p (t k) c -> p t (k c)", t=TT)
        gfin = cv[:, 0:4, :].rearrange("p k t -> p (k t)")
        gfin_row = cv[0:1, 4:8, :].rearrange("p k t -> p (k t)")
        fin = sb("fin", [P, 4])

        bank = [ctx.enter_context(nc.psum_tensor(f"bank{i}", [P, 512], F32)) for i in range(NBANK)]
        y_ps = ctx.enter_context(nc.psum_tensor("y_ps", [P, TT, D], F32))

        x_in = [sem("x_in0"), sem("x_in1")]
        mem_in, par_in, lruw_in, router_in, gfin_in = map(sem, (
            "mem_in", "par_in", "lruw_in", "router_in", "gfin_in"))
        zeroed, consts = sem("zeroed"), sem("consts")
        pre_loaded = [sem(f"pre_loaded{i}") for i in range(PRE_SLOTS)]
        w_hi_ready = [sem(f"w_hi_ready{b}") for b in range(SPLIT_BUFS)]
        w_lo_ready = [sem(f"w_lo_ready{b}") for b in range(SPLIT_BUFS)]
        h1_hi, h1_done, h2_hi, h2_done, sw_hi, sw_done = map(sem, (
            "h1_hi", "h1_lo_ready", "h2_hi", "h2_lo_ready", "swish_hi", "swish_lo_ready"))
        lr_hi, lr_done, mg_hi, mg_done, at_hi, at_done = map(sem, (
            "lru_hi_ready", "lru_lo_ready", "merged_hi", "merged_lo_ready", "attn_hi", "attn_lo_ready"))
        product = sem("product")
        mean_read, logit_read, rank_read, yb_read, ya_read = map(sem, (
            "mean_read", "logit_read", "rank_read", "yb_read", "ya_read"))
        logitT_ready = sem("logitT_ready")
        x_sq, m_sq, ln_sq, x1_sq, xf_sq = map(sem, ("x_sq", "m_sq", "ln_sq", "x1_sq", "xf_sq"))
        var_ready, root_ready = sem("var_ready"), sem("root_ready")
        lam_abs, lam_exp, lam_ready = sem("lam_abs"), sem("lam_exp"), sem("lam_ready")
        h_ready, mem_ready = sem("h_ready"), sem("mem_ready")
        sig_ready, glu_ready, xr_ready, gl_ready, k_ready, v_ready = map(sem, (
            "sig_ready", "glu_ready", "xr_ready", "gl_ready", "k_ready", "v_ready"))
        conv_ready, xc_ready, centred, ln_ready, swish_ready = map(sem, (
            "conv_ready", "xc_ready", "centred", "ln_ready", "swish_ready"))
        lru_gates, lru_exp, lru_sq, lru_root, lru_scanned, lru_ready = map(sem, (
            "lru_gates", "lru_exp", "lru_sq", "lru_root", "lru_scanned", "lru_ready"))
        mgate_ready, merged, x1_ready, xf_ready = map(sem, ("mgate_ready", "merged", "x1_ready", "xf_ready"))
        q_ready, smax_ready, sexp_ready, prob_ready, probT_ready = map(sem, (
            "q_ready", "smax_ready", "sexp_ready", "prob_ready", "probT_ready"))
        top_ready, texp_ready, mask_ready, count_ready, htok_ready, gfin_ready = map(sem, (
            "top_ready", "texp_ready", "mask_ready", "count_ready", "htok_ready", "gfin_ready"))
        loaded = [sem(f"loaded{s}") for s in range(SLOTS)]
        chunk_used, bias_in, bias_used = sem("chunk_used"), sem("bias_in"), sem("bias_used")
        pick_ready, wpickT_done, wpickT_ready, gathered, xtok_ready, xgT_done, xg_ready = map(sem, (
            "pick_ready", "wpickT_done", "wpickT_ready", "gathered", "xtok_ready", "xgT_done", "xg_ready"))
        gclip_ready, sigm_ready, act_ready, actT_done, actT_ready = map(sem, (
            "gclip_ready", "sigm_ready", "act_ready", "actT_done", "actT_ready"))
        job_out_ready, y_done, ysum_ready, yvar_ready, yroot_ready, y_ready, stored = map(sem, (
            "job_out_ready", "y_done", "ysum_ready", "yvar_ready", "yroot_ready", "y_ready", "stored"))
        wpick_ready, bdown_in = sem("wpick_ready"), sem("bdown_in")
        v_chain, uclip_ready, ug_ready = sem("v_chain"), sem("uclip_ready"), sem("ug_ready")

        bank_g, bank_u, bank_x, bank_a = bank

        def pair(x):
            return x[:].rearrange("p (m t) -> p m t", m=2)

        def ps(name, i=0):
            return bank[AT[(name, i)] % NBANK]

        def wait_product(eng, name, i=0):
            eng.wait_ge(product, AT[(name, i)] + 1)

        read = {("sum_x2", 0): (var_ready, 1), ("sum_m2", 0): (var_ready, 2), ("ln_mean", 0): (mean_read, 1),
                ("ln_var", 0): (var_ready, 3), ("sum_x1", 0): (var_ready, 4), ("sum_xf", 0): (var_ready, 5),
                ("logit", 0): (logit_read, 1), ("logitT", 0): (logitT_ready, 1), ("rank", 0): (rank_read, 1)}
        for i in range(4):
            read.update({("cg", i): (sig_ready, i + 1), ("cv", i): (glu_ready, i + 1), ("xr", i): (xr_ready, i + 1),
                         ("gr", i): (gl_ready, i + 1), ("k", i): (k_ready, i + 1), ("v", i): (v_ready, i + 1),
                         ("ga", i): (mgate_ready, 2 * i + 2), ("gb", i): (mgate_ready, 2 * i + 10),
                         ("yb", i): (yb_read, i + 1), ("ya", i): (ya_read, i + 1), ("wo", i): (x1_ready, i + 1),
                         ("q", i): (q_ready, i + 1), ("score", i): (sexp_ready, 2 * i + 2),
                         ("probT", i): (probT_ready, i + 1), ("attn", i): (at_done, i + 1),
                         ("o", i): (xf_ready, i + 1), ("htok", i): (htok_ready, i + 1)})
            for d in range(2):
                read.update({(f"ra{d}", i): (lru_gates, 16 * d + 4 * i + 2),
                             (f"ri{d}", i): (lru_gates, 16 * d + 4 * i + 4)})
        for i in range(2):
            read[("gfin", i)] = (gfin_ready, i + 1)

        HALF = KT // 2

        def split_w_hi(eng, copy, name, i):
            s, n = SPLIT_AT[(name, i)], CHUNK_AT[(name, i)]
            b = s % SPLIT_BUFS
            eng.wait_ge(pre_loaded[n % PRE_SLOTS], 16 * (n // PRE_SLOTS + 1))
            if s >= SPLIT_BUFS:
                wait_product(eng, *SPLIT[s - SPLIT_BUFS])
            for ks in (slice(0, HALF), slice(HALF, KT)):
                copy(w_hi[:, b, ks, :], pre_slot[n % PRE_SLOTS][:, ks, :]).then_inc(w_hi_ready[b], 1)

        block = ctx.enter_context(nc.Block())

        @block.sync
        def _(sp):
            for half in range(2):
                ks = slice(HALF * half, HALF * (half + 1))
                sp.dma_start(xT[:, ks, :], xT_d[:, ks, :]).then_inc(x_in[half], 16)

            def former_used(n):
                if CHUNKS[n] in SPLIT_AT:
                    s = SPLIT_AT[CHUNKS[n]]
                    sp.wait_ge(w_lo_ready[s % SPLIT_BUFS], 2 * (s // SPLIT_BUFS) + 2)
                else:
                    wait_product(sp, *CHUNKS[n])

            def load_projection(n):
                name, i = CHUNKS[n]
                w, col = sources[name]
                src = w[:, col + COLS * i:col + COLS * (i + 1)].rearrange("(k p) n -> p k n", p=P)
                if n >= PRE_SLOTS:
                    former_used(n - PRE_SLOTS)
                sp.dma_start(pre_slot[n % PRE_SLOTS], src).then_inc(pre_loaded[n % PRE_SLOTS], 16)

            def expert_source(e, s):
                if s < UP_CHUNKS:
                    return w_up[e, P * s:P * (s + 1), :].rearrange("a p n -> p (a n)")
                k = 2 * (s - UP_CHUNKS)
                return w_down[e, P * k:P * (k + 2), :].rearrange("a (k p) n -> p (a k) n", p=P)

            def load_expert(e, c, slot):
                dst = expert_slot[slot] if c < UP_CHUNKS else expert_slot[slot].rearrange("p (k n) -> p k n", k=2)
                sp.dma_start(dst, expert_source(e, c)).then_inc(loaded[slot], 16)

            def load_first(slot):
                e = slot // JOB_CHUNKS
                load_expert(slice(e, e + 1), slot % JOB_CHUNKS, slot)

            early = {("v", 1): 4, ("v", 2): 5, ("v", 3): 7, ("q", 0): 8, ("q", 1): 12, ("q", 2): 13, ("q", 3): 6}
            for n in range(len(CHUNKS)):
                load_projection(n)
                if n == 3:
                    sp.wait_ge(zeroed, 1)
                    for d in range(2):
                        for g, w in enumerate((lru_w_a, lru_w_i)):
                            for odd in range(2):
                                src = w[d].rearrange("(m o) i j -> o i m j", o=2)[odd]
                                sp.dma_start(lru_gate_w[64 * odd:64 * odd + 64, 2 * d + g, :, 64 * odd:64 * odd + 64],
                                            src).then_inc(lruw_in, 16)
                    sp.dma_start(router[:], router_w.rearrange("(k p) e -> p k e", p=P)).then_inc(router_in, 16)
                    sp.dma_start(rb_row[:], router_b).then_inc(router_in, 16)
                if CHUNKS[n] in early:
                    slot = early[CHUNKS[n]]
                    sp.wait_ge(mg_done, 4)
                    if slot == 6:
                        wait_product(sp, "v", 3)
                    load_first(slot)
            wait_product(sp, "attn", 3)
            sp.dma_start(bup_row, b_up[0:1, :]).then_inc(bias_in, 16)
            for n in range(len(CHUNKS) - PRE_SLOTS, len(CHUNKS)):
                former_used(n)
                load_first(MAIN_SLOTS - PRE_SLOTS + n % PRE_SLOTS)
            for b in range(SPLIT_BUFS):
                wait_product(sp, *SPLIT[len(SPLIT) - SPLIT_BUFS + b])
                load_first(b)
                load_first(SPLIT_BUFS + b)
            load_first(14)
            wait_product(sp, "htok", 3)
            load_first(15)

            sp.wait_ge(job_out_ready, 1)
            for half in range(2):
                sp.dma_start(job_out[CAP * half:CAP * half + NE, :],
                             b_down[:, 512 * half:512 * (half + 1)]).then_inc(bdown_in, 16)

            def load_chunk(expert, job, u, c, first_chunk):
                n = u * JOB_CHUNKS + c
                if c == SLOTS - JOB_CHUNKS:
                    sp.wait_ge(bias_used, job)
                    sp.dma_start(bup_row, b_up[expert, :]).then_inc(bias_in, 16)
                sp.wait_ge(chunk_used, first_chunk + n + 1)
                load_expert(expert, c, n % SLOTS)

            for n in range(SLOTS, GROUP * JOB_CHUNKS):
                u, c = divmod(n, JOB_CHUNKS)
                load_chunk(slice(u, u + 1), u, u, c, 0)
            sp.wait_ge(count_ready, 3)
            rounds = sp.value_load(n_i[0:1, 1:2], min_val=1, max_val=MAX_ROUNDS)
            with sp.Fori(0, rounds) as r:
                first = sp.snap((((r + 3) >> 2) + 1) & 1)
                base = sp.snap(r * NE)
                with sp.Fori(first, NE // GROUP) as g:
                    e0 = sp.snap(g * GROUP)
                    job0 = sp.snap(base + e0)
                    first_chunk = sp.snap(job0 * JOB_CHUNKS)
                    for u in range(GROUP):
                        e, job = sp.snap(e0 + u), sp.snap(job0 + u)
                        for c in range(JOB_CHUNKS):
                            load_chunk(bass.ds(e, 1), job, u, c, first_chunk)

            for t in range(TT):
                sp.wait_ge(y_ready, t + 1)
                sp.dma_start(out[P * t:P * (t + 1), :], y_sb[:, t, :]).then_inc(stored, 16)
            sp.wait_ge(stored, 16 * TT)

        @block.gpsimd
        def _(pool):
            pool.memset(lru_gate_w, 0.0).then_inc(zeroed, 1)
            pool.memset(ones[:], 1.0).then_inc(consts, 1)
            pool.memset(ident[:], 0.0).then_inc(consts, 1)
            pool.wait_ge(consts, 2)
            pool.affine_select(out=ident[:], in_=ident[:], compare_op=ALU.not_equal, fill=1.0, base=0,
                               pattern=[[-1, P]], channel_multiplier=1).then_inc(consts, 1)
            pool.affine_select(out=before[:], in_=ones[:], compare_op=ALU.is_gt, fill=0.0, base=0,
                               pattern=[[1, P]], channel_multiplier=-1).then_inc(consts, 1)
            pool.iota(iota_i[:], pattern=[[1, P]], base=0, channel_multiplier=0).then_inc(consts, 1)
            pool.memset(glu[:, :, 0:CONF_LEFT], 0.0).then_inc(consts, 1)
            pool.memset(glu[:, :, CONF_LEFT + T:], 0.0).then_inc(consts, 1)
            pool.memset(xr[:, :, 0:LRU_LEFT], 0.0).then_inc(consts, 1)
            pool.memset(xr[:, :, LRU_LEFT + T:], 0.0).then_inc(consts, 1)
            for s, chunk in enumerate(SPLIT):
                b, n = s % SPLIT_BUFS, CHUNK_AT[chunk]
                if s >= SPLIT_BUFS:
                    wait_product(pool, *SPLIT[s - SPLIT_BUFS])
                for half, ks in enumerate((slice(0, HALF), slice(HALF, KT))):
                    pool.wait_ge(w_hi_ready[b], 2 * (s // SPLIT_BUFS) + half + 1)
                    pool.tensor_tensor(w_lo[:, b, ks, :], pre_slot[n % PRE_SLOTS][:, ks, :], w_hi[:, b, ks, :],
                                       ALU.subtract).then_inc(w_lo_ready[b], 1)
            wait_product(pool, "sum_xf")
            pool.memset(job_out, 0.0).then_inc(job_out_ready, 1)
        CONSTS = 9

        @block.scalar
        def _(a):
            a.dma_start(par[:], par_d).then_inc(par_in, 16)
            a.dma_start(memT, memT_d).then_inc(mem_in, 16)

            def root(n, buf):
                a.wait_ge(var_ready, n)
                a.activation(buf[:], buf[:], ACT.Sqrt).then_inc(root_ready, 1)

            def split_w(name, i):
                split_w_hi(a, lambda dst, src: a.activation(dst, src, ACT.Copy), name, i)

            def split_x(src, ready, done, start=0, step=1):
                for n in range(KT // step):
                    a.wait_ge(ready, start + n + 1)
                    ks = slice(n * step, (n + 1) * step)
                    a.activation(x_hi[:, ks, :], src[:, ks, :], ACT.Copy).then_inc(done, 1)

            for half in range(2):
                ks = slice(HALF * half, HALF * (half + 1))
                a.wait_ge(x_in[half], 16)
                a.activation(lru_a[:, ks, :], xT[:, ks, :], ACT.Square).then_inc(x_sq, 1)
            split_w("cg", 0)
            root(1, stat)
            split_x(lru_h, h_ready, h1_hi)
            split_w("cv", 0)
            a.wait_ge(mem_in, 16)
            a.activation(lru_u[:], memT, ACT.Square).then_inc(m_sq, 1)
            a.wait_ge(lam_abs, 1)
            a.activation(lam[:, 1], lam[:, 0], ACT.Exp).then_inc(lam_exp, 1)

            a.wait_ge(consts, CONSTS)
            for i in range(4):
                split_w("xr", i)
                wait_product(a, "cg", i)
                if i >= 2:
                    a.wait_ge(glu_ready, i - 1)
                a.activation(sig[:, i % 2], ps("cg", i)[:], ACT.Sigmoid).then_inc(sig_ready, 1)
                split_w("gr", i)
                if i < 3:
                    split_w("cg", i + 1)
                wait_product(a, "xr", i)
                a.activation(xr[:, 2 * i:2 * i + 2, LRU_LEFT:LRU_LEFT + T], pair(ps("xr", i)),
                             ACT.Copy).then_inc(xr_ready, 1)
                if i < 3:
                    split_w("cv", i + 1)
                wait_product(a, "gr", i)
                a.activation(gl[:, 2 * i:2 * i + 2, :], pair(ps("gr", i)),
                             ACT.Gelu_apprx_tanh).then_inc(gl_ready, 1)
                if i == 1:
                    root(2, mstat)
            for i in range(4):
                if i >= 2:
                    split_w("ga", i - 2)
                wait_product(a, "k", i)
                a.activation(keyT[:, 2 * i:2 * i + 2, :], pair(ps("k", i)), ACT.Copy).then_inc(k_ready, 1)

            def copy_v(i):
                wait_product(a, "v", i)
                a.activation(val[:, :, COLS * i:COLS * (i + 1)], pair(ps("v", i)), ACT.Copy).then_inc(v_ready, 1)

            def lru_sigmoids(d, pairs=range(4)):
                for i in pairs:
                    for name, bias, dst in (("ra", P_BA, lru_a), ("ri", P_BI, lru_u)):
                        wait_product(a, f"{name}{d}", i)
                        for m in range(2):
                            a.activation(dst[:, 2 * i + m, :], ps(f"{name}{d}", i)[:, m * T:(m + 1) * T], ACT.Sigmoid,
                                         bias=par[:, 2 * i + m, bias + d:bias + d + 1]).then_inc(lru_gates, 1)

            def lru_exponentials(d):
                a.wait_ge(lru_gates, 16 * (d + 1))
                for m in range(KT):
                    a.activation(lru_t[:, m, :], lru_a[:, m, :], ACT.Tanh, scale=lam[:, 5, m, d:d + 1])
                for m in range(KT):
                    a.activation(lru_a[:, m, :], lru_a[:, m, :], ACT.Exp,
                                 scale=lam[:, 6, m, d:d + 1]).then_inc(lru_exp, 1)

            def lru_roots(d):
                for i in range(4):
                    a.wait_ge(lru_sq, 4 * d + i + 1)
                    a.activation(lru_t[:, 2 * i:2 * i + 2, :], lru_t[:, 2 * i:2 * i + 2, :],
                                 ACT.Sqrt).then_inc(lru_root, 1)

            def merge_gate(name, i, col, dst):
                wait_product(a, name, i)
                for m in range(2):
                    a.activation(dst[:, 2 * i + m, :], ps(name, i)[:, m * T:(m + 1) * T], ACT.Sigmoid,
                                 bias=par[:, 2 * i + m, col:col + 1]).then_inc(mgate_ready, 1)

            a.wait_ge(lam_ready, 1)
            a.wait_ge(conv_ready, 4)
            for i in range(2):
                merge_gate("ga", i, P_GATE_B, gate_a)
                split_w("ga", i + 2)
            lru_sigmoids(0)
            a.wait_ge(centred, 1)
            a.activation(lru_h[:], cv[:], ACT.Square).then_inc(ln_sq, 1)
            lru_exponentials(0)
            lru_roots(0)
            merge_gate("ga", 2, P_GATE_B, gate_a)
            root(3, stat)
            merge_gate("ga", 3, P_GATE_B, gate_a)
            a.wait_ge(xc_ready, 4)
            a.wait_ge(lru_scanned, KT)
            for i in range(2):
                split_w("gb", i + 2)
                merge_gate("gb", i, P_GATE_B + 1, gate_b)
                lru_sigmoids(1, (2 * i, 2 * i + 1))
            a.wait_ge(ln_ready, 1)
            for m in range(KT):
                a.activation(cv[:, m, :], cv[:, m, :], ACT.Silu, bias=par[:, m, P_LN_B:P_LN_B + 1],
                             scale=par[:, m, P_LN_G:P_LN_G + 1]).then_inc(swish_ready, 1)
            split_w("yb", 0)
            merge_gate("gb", 2, P_GATE_B + 1, gate_b)
            lru_exponentials(1)
            split_w("yb", 1)
            merge_gate("gb", 3, P_GATE_B + 1, gate_b)
            lru_roots(1)
            split_w("yb", 2)
            split_w("yb", 3)
            for i in range(4):
                a.wait_ge(lru_ready, i + 1)
                a.activation(lru_hi[:, 2 * i:2 * i + 2, :], gl[:, 2 * i:2 * i + 2, :], ACT.Copy).then_inc(lr_hi, 1)
            split_w("ya", 0)
            split_w("ya", 1)
            wait_product(a, "yb", 3)
            a.dma_start(gfin_row, g_final).then_inc(gfin_in, 16)
            split_x(gate_a, merged, mg_hi, step=2)
            copy_v(0)

            def squares(i, ready, done):
                a.wait_ge(ready, i + 1)
                a.activation(lru_a[:, 2 * i:2 * i + 2, :], xT[:, 2 * i:2 * i + 2, :], ACT.Square).then_inc(done, 1)

            for i in range(4):
                squares(i, x1_ready, x1_sq)
            copy_v(1)
            root(4, stat)
            split_x(lru_u, h_ready, h2_hi, start=KT)
            split_w("q", 0)
            copy_v(2)
            split_w("q", 1)
            copy_v(3)
            for i in range(4):
                split_w(*((("q", 2), ("q", 3), ("o", 0), ("o", 1))[i]))
                wait_product(a, "q", i)
                a.activation(qT[:, 2 * i:2 * i + 2, :], pair(ps("q", i)), ACT.Copy).then_inc(q_ready, 1)
            for h in range(HEADS):
                a.wait_ge(smax_ready, h + 1)
                for t in range(TT):
                    a.activation(prob[:, h, t, :], ps("score", h)[:, t * T:(t + 1) * T], ACT.Exp,
                                 bias=sm[:, 1, h, t:t + 1], scale=HD ** -0.5,
                                 accum_out=sm[:, 2, h, t:t + 1]).then_inc(sexp_ready, 1)
            for name, i in (("probT", 0), ("probT", 1), ("attn", 0), ("probT", 2), ("attn", 1), ("probT", 3),
                            ("attn", 2), ("attn", 3)):
                wait_product(a, name, i)
                if name == "probT":
                    a.activation(probT[:, i, :, :], pair(ps(name, i)), ACT.Copy).then_inc(probT_ready, 1)
                else:
                    a.activation(x_hi[:, 2 * i:2 * i + 2, :], pair(ps(name, i)), ACT.Copy).then_inc(at_hi, 1)
            for i in range(4):
                squares(i, xf_ready, xf_sq)
            root(5, stat)
            for i in range(2):
                wait_product(a, "gfin", i)
                a.activation(gfin[:, 512 * i:512 * (i + 1)], ps("gfin", i)[:], ACT.Copy).then_inc(gfin_ready, 1)
            wait_product(a, "logitT")
            a.activation(lgT, ps("logitT")[:, 0:T], ACT.Copy).then_inc(logitT_ready, 1)
            for i in range(4):
                wait_product(a, "htok", i)
                a.activation(h_tok[:, i // 2, 512 * (i % 2):512 * (i % 2) + 512], ps("htok", i)[:],
                             ACT.Copy).then_inc(htok_ready, 1)
            a.wait_ge(top_ready, 1)
            for t in range(TT):
                a.activation(top_g[:, t, 0:TOP], top_v[:, t, 0:TOP], ACT.Exp, bias=t1[:, t, 0:1],
                             accum_out=t1[:, t, 1:2]).then_inc(texp_ready, 1)
            def copy_tokens(n):
                a.wait_ge(gathered, n)
                a.activation(xtok, bank_x[:], ACT.Copy).then_inc(xtok_ready, 1)

            def copy_xg(n):
                a.wait_ge(xgT_done, n)
                a.activation(xg, bank_x[:].rearrange("p (c n) -> p c n", c=4), ACT.Copy).then_inc(xg_ready, 1)

            copy_tokens(1)
            copy_xg(1)
            a.wait_ge(count_ready, 3)
            jobs = a.value_load(n_i[0:1, 0:1], min_val=NE, max_val=JOBS_MAX)
            with a.Fori(0, jobs) as j:
                a.wait_ge(gclip_ready, j + 1)
                a.activation(sg, gc, ACT.Sigmoid, scale=SWIGLU_ALPHA).then_inc(sigm_ready, 1)
                copy_tokens(j + 2)
                a.wait_ge(chunk_used, JOB_CHUNKS * j + (SLOTS + JOB_CHUNKS))
                a.activation(job_out, bank_g[:], ACT.Copy).then_inc(job_out_ready, 1)
                copy_xg(j + 2)

            a.wait_ge(y_done, 1)
            for t in range(TT):
                a.activation(y_sb[:, t, :], y_ps[:, t, :], ACT.Square, accum_out=fin[:, t:t + 1]).then_inc(ysum_ready, 1)
            a.wait_ge(yvar_ready, 1)
            a.activation(fin[:, 0:TT], fin[:, 0:TT], ACT.Sqrt).then_inc(yroot_ready, 1)

        @block.tensor
        def _(pe):
            def product_bank(name, i=0):
                n = AT[(name, i)]
                if n >= NBANK:
                    pe.wait_ge(*read[PRODUCTS[n - NBANK]])
                return bank[n % NBANK]

            def sum_channels(name, src, squared):
                dst = product_bank(name)
                ready, pieces = squared
                for k in range(KT):
                    if k % (KT // pieces) == 0:
                        pe.wait_ge(ready, k // (KT // pieces) + 1)
                    last = nc.tensor.matmul(dst[:, 0:T], ones[:], src[:, k, :], start=k == 0, stop=k == KT - 1)
                last.then_inc(product, 1)

            def project(name, i, src, token_major=False, arrives=None):
                n = CHUNK_AT[(name, i)]
                dst = product_bank(name, i)
                w = pre_slot[n % PRE_SLOTS]
                pe.wait_ge(pre_loaded[n % PRE_SLOTS], 16 * (n // PRE_SLOTS + 1))
                for m in range(2):
                    for k in range(KT):
                        if arrives and m == 0:
                            pe.wait_ge(*arrives(k))
                        if token_major:
                            lhsT, rhs = src[:, k, m * P:(m + 1) * P], w[:, k, :]
                        else:
                            lhsT, rhs = w[:, k, m * P:(m + 1) * P], src[:, k, :]
                        last = nc.tensor.matmul(dst[:, m * T:(m + 1) * T], lhsT, rhs, start=k == 0, stop=k == KT - 1)
                last.then_inc(product, 1)

            def project_parts(name, i, parts, arrives=None):
                dst = product_bank(name, i)
                s = SPLIT_AT[(name, i)]
                b = s % SPLIT_BUFS
                hi, lo = parts
                for m in range(2):
                    for k in range(KT):
                        if m == 0 and k % HALF == 0:
                            pe.wait_ge(w_lo_ready[b], 2 * (s // SPLIT_BUFS) + k // HALF + 1)
                        if arrives and m == 0:
                            pe.wait_ge(*arrives(k))
                        cols = slice(m * P, (m + 1) * P)
                        d = dst[:, m * T:(m + 1) * T]
                        nc.tensor.matmul(d, w_hi[:, b, k, cols], hi[:, k, :], start=k == 0, stop=False)
                        nc.tensor.matmul(d, w_lo[:, b, k, cols], hi[:, k, :], start=False, stop=False)
                        last = nc.tensor.matmul(d, w_hi[:, b, k, cols], lo[:, k, :], start=False, stop=k == KT - 1)
                last.then_inc(product, 1)

            pe.wait_ge(consts, CONSTS)
            sum_channels("sum_x2", lru_a, (x_sq, 2))
            for i in range(4):
                for name in ("cg", "cv", "xr", "gr"):
                    project_parts(name, i, h1_parts,
                                  arrives=(lambda k: (h1_done, k + 1)) if (name, i) == ("cg", 0) else None)
                if i == 0:
                    sum_channels("sum_m2", lru_u, (m_sq, 1))
            for i in range(4):
                project("k", i, memT, arrives=(lambda k: (mem_ready, k + 1)) if i == 0 else None)
            project_parts("ga", 0, h1_parts)
            sum_channels("ln_mean", cv, (conv_ready, 4))

            def lru_gates_of(d, pairs=range(4)):
                for i in pairs:
                    for g, name in enumerate((f"ra{d}", f"ri{d}")):
                        dst = product_bank(name, i)
                        for m in range(2):
                            last = nc.tensor.matmul(dst[:, m * T:(m + 1) * T], lru_gate_w[:, 2 * d + g, 2 * i + m, :],
                                                    xc[:, 2 * i + m, :], start=True, stop=True)
                        last.then_inc(product, 1)

            project_parts("ga", 1, h1_parts)
            pe.wait_ge(lruw_in, 16 * 8)
            pe.wait_ge(xc_ready, 4)
            lru_gates_of(0)
            project_parts("ga", 2, h1_parts)
            sum_channels("ln_var", lru_h, (ln_sq, 1))
            project_parts("ga", 3, h1_parts)
            for i in range(2):
                project_parts("gb", i, h1_parts)
                lru_gates_of(1, (2 * i, 2 * i + 1))
            for i in range(2, 4):
                project_parts("gb", i, h1_parts)
            for i in range(4):
                project_parts("yb", i, swish_parts, arrives=(lambda k: (sw_done, k + 1)) if i == 0 else None)
            for i in range(4):
                project_parts("ya", i, lru_parts, arrives=(lambda k: (lr_done, k // 2 + 1)) if i == 0 else None)
            project("v", 0, memT, token_major=True)
            for i in range(4):
                project_parts("wo", i, merged_parts, arrives=(lambda k: (mg_done, k // 2 + 1)) if i == 0 else None)
            project("v", 1, memT, token_major=True)
            sum_channels("sum_x1", lru_a, (x1_sq, 4))
            for i in range(2, 4):
                project("v", i, memT, token_major=True)
            for i in range(4):
                project_parts("q", i, h2_parts, arrives=(lambda k: (h2_done, k + 1)) if i == 0 else None)
            for h in range(HEADS):
                dst = product_bank("score", h)
                pe.wait_ge(q_ready, h + 1)
                for t in range(TT):
                    for k in range(2):
                        last = nc.tensor.matmul(dst[:, t * T:(t + 1) * T], qT[:, 2 * h + k, t * P:(t + 1) * P],
                                                keyT[:, 2 * h + k, :], start=k == 0, stop=k == 1)
                last.then_inc(product, 1)

            def transpose_prob(h):
                dst = product_bank("probT", h)
                pe.wait_ge(prob_ready, h + 1)
                for m in range(TT):
                    for t in range(TT):
                        last = nc.tensor.transpose(dst[:, m * T + t * P:m * T + (t + 1) * P],
                                                   prob[:, h, t, m * P:(m + 1) * P], ident[:])
                last.then_inc(product, 1)

            def attend(h):
                dst = product_bank("attn", h)
                pe.wait_ge(probT_ready, h + 1)
                for k in range(2):
                    for m in range(TT):
                        last = nc.tensor.matmul(dst[:, k * T:(k + 1) * T], val[:, m, h * HD + k * P:h * HD + (k + 1) * P],
                                                probT[:, h, m, :], start=m == 0, stop=m == TT - 1)
                last.then_inc(product, 1)

            transpose_prob(0)
            for h in range(HEADS):
                if h + 1 < HEADS:
                    transpose_prob(h + 1)
                attend(h)
            for i in range(4):
                project_parts("o", i, attn_parts, arrives=(lambda k: (at_done, k // 2 + 1)) if i == 0 else None)
            sum_channels("sum_xf", lru_a, (xf_sq, 4))
            for t in range(TT):
                for k in range(KT):
                    last = nc.tensor.matmul(y_ps[:, t, k * P:(k + 1) * P], xT[:, k, t * P:(t + 1) * P], ident[:],
                                            start=k % 4 == 0, stop=False, skip_group_check=True)
            last.then_inc(chunk_used, SLOTS)
            pe.wait_ge(gfin_in, 16)
            for i in range(2):
                nc.tensor.matmul(product_bank("gfin", i)[:], ones[0:1, :], gfin_row[:, 512 * i:512 * (i + 1)],
                                 start=True, stop=True).then_inc(product, 1)
            pe.wait_ge(router_in, 32)
            dst = product_bank("logitT")
            for k in range(KT):
                c = k % 4
                pe.wait_ge(h_ready, 2 * KT + k + 1)
                last = nc.tensor.matmul(dst[NE * c:NE * (c + 1), 0:T], router[:, k, :], hT[:, k, :],
                                        start=k < 4, stop=k >= 4)
                for t in range(TT if k == 0 else 0):
                    nc.tensor.matmul(dst[0:NE, t * P:(t + 1) * P], rb_row[:], ones[0:1, :], start=False, stop=False)
            last.then_inc(product, 1)
            dst = product_bank("logit")
            pe.wait_ge(logitT_ready, 1)
            for t in range(TT):
                last = nc.tensor.transpose(dst[:, t * P:(t + 1) * P], lgT[:, t * P:(t + 1) * P], ident[:])
            last.then_inc(product, 1)
            for i in range(4):
                dst = product_bank("htok", i)
                for k in range(4):
                    last = nc.tensor.transpose(dst[:, k * P:(k + 1) * P],
                                               hT[:, 4 * (i % 2) + k, (i // 2) * P:(i // 2 + 1) * P], ident[:])
                last.then_inc(product, 1)
            dst = product_bank("rank")
            pe.wait_ge(mask_ready, 1)
            nc.tensor.matmul(dst[:, 0:NE], before[:], mask[:, 0, :], start=True, stop=True)
            nc.tensor.matmul(dst[:, NE:2 * NE], ones[:], mask[:, 0, :], start=True, stop=False)
            nc.tensor.matmul(dst[:, NE:2 * NE], before[:], mask[:, 1, :], start=False, stop=True)
            for t in range(TT):
                last = nc.tensor.matmul(dst[:, 2 * NE:3 * NE], ones[:], mask[:, t, :], start=t == 0, stop=t == TT - 1)
            last.then_inc(product, 1)
            def gather():
                for t in range(TT):
                    for half in range(2):
                        last = nc.tensor.matmul(bank_x[CAP * half:CAP * (half + 1), :], pick[:, t, :],
                                                h_tok[:, t, 512 * half:512 * (half + 1)],
                                                start=t == 0, stop=t == TT - 1)
                last.then_inc(gathered, 1)

            def transpose_tokens(n):
                pe.wait_ge(xtok_ready, n)
                for c in range(4):
                    last = nc.tensor.transpose(bank_x[:, c * P:(c + 1) * P], xtok[:, c * P:(c + 1) * P], ident[:])
                last.then_inc(xgT_done, 1)

            for i in range(NBANK):
                pe.wait_ge(*read[PRODUCTS[len(PRODUCTS) - NBANK + i]])
            pe.wait_ge(htok_ready, 4)
            pe.wait_ge(pick_ready, 1)
            gather()
            transpose_tokens(1)

            def transpose_wpick(n):
                pe.wait_ge(wpick_ready, n)
                for t in range(TT):
                    last = nc.tensor.transpose(bank_a[:, t * P:(t + 1) * P], wpick[:, t, :], ident[:])
                last.then_inc(wpickT_done, 1)

            def scatter(t, stop=False):
                for half in range(2):
                    last = nc.tensor.matmul(y_ps[:, t, 512 * half:512 * (half + 1)],
                                            wpickT[CAP * half:CAP * (half + 1), t, :],
                                            job_out[CAP * half:CAP * (half + 1), :],
                                            start=False, stop=stop, skip_group_check=True)
                return last

            transpose_wpick(1)
            pe.wait_ge(bdown_in, 32)
            pe.wait_ge(count_ready, 3)
            groups = pe.value_load(n_i[0:1, 2:3], min_val=NE // GROUP, max_val=JOBS_MAX // GROUP)
            def run_job(g, u):
                j = pe.snap(g * GROUP + u)

                def chunk(u, c):
                    turn, slot = divmod(u * JOB_CHUNKS + c, SLOTS)
                    pe.wait_ge(loaded[slot], g * (16 * GROUP * JOB_CHUNKS // SLOTS) + 16 * (turn + 1))
                    return expert_slot[slot]

                pe.wait_ge(bias_in, 16 * j + 16)
                for dst, col in ((bank_u, F), (bank_g, 0)):
                    if dst is bank_g:
                        pe.wait_ge(job_out_ready, j + 1)
                    for half in range(2):
                        last = nc.tensor.matmul(dst[CAP * half:CAP * (half + 1), :], ones[0:1, 0:CAP],
                                                bup_row[0:1, col + 512 * half:col + 512 * (half + 1)],
                                                start=True, stop=False)
                last.then_inc(bias_used, 1)
                pe.wait_ge(xg_ready, j + 1)
                for k in range(KT):
                    w = chunk(u, k)
                    for dst, col in ((bank_g, 0), (bank_u, F)):
                        for half in range(2):
                            last = nc.tensor.matmul(dst[CAP * half:CAP * (half + 1), :],
                                                    xg[:, k % 4, CAP * (k // 4):CAP * (k // 4 + 1)],
                                                    w[:, col + 512 * half:col + 512 * (half + 1)],
                                                    start=False, stop=k == KT - 1)
                    last.then_inc(chunk_used, 1)
                pe.wait_ge(pick_ready, j + 2)
                gather()
                pe.wait_ge(wpickT_ready, j + 1)
                scatter(0)
                pe.wait_ge(act_ready, j + 1)
                for c in range(4):
                    last = nc.tensor.transpose(bank_a[:, c * P:(c + 1) * P], act[:, c * P:(c + 1) * P], ident[:])
                last.then_inc(actT_done, 1)
                scatter(1)
                pe.wait_ge(actT_ready, j + 1)
                for k in range(KT):
                    if k % 2 == 0:
                        w = chunk(u, UP_CHUNKS + k // 2)
                    for half in range(2):
                        col = D * (k % 2) + 512 * half
                        last = nc.tensor.matmul(bank_g[CAP * half:CAP * (half + 1), :],
                                                actT[:, k % 4, CAP * (k // 4):CAP * (k // 4 + 1)],
                                                w[:, col:col + 512], start=k == 0, stop=k == KT - 1)
                    if k % 2:
                        last.then_inc(chunk_used, 1)
                transpose_wpick(j + 2)
                transpose_tokens(j + 2)

            with pe.Fori(0, groups) as g:
                for u in range(GROUP):
                    run_job(g, u)
            jobs = groups * GROUP
            pe.wait_ge(wpickT_ready, jobs + 1)
            pe.wait_ge(job_out_ready, jobs + 1)
            for t in range(TT):
                last = scatter(t, stop=True)
            last.then_inc(y_done, 1)

        @block.vector
        def _(v):
            done = [0]

            def step(ins, lag=0):
                done[0] += 1
                ins.then_inc(v_chain, 1)
                if done[0] > lag:
                    v.wait_ge(v_chain, done[0] - lag)

            def variance(name, buf):
                wait_product(v, name)
                nc.vector.tensor_scalar(buf[:], ps(name)[:, 0:T], 1.0 / D, EPS, ALU.mult, ALU.add).then_inc(var_ready, 1)

            def inverse_root(n, buf):
                v.wait_ge(root_ready, n)
                step(nc.vector.reciprocal(buf[:], buf[:]))

            def split_w(name, i):
                split_w_hi(v, nc.vector.tensor_copy, name, i)

            def lo_part(lo, src, hi, ks, hi_ready, done):
                v.wait_ge(*hi_ready)
                nc.vector.tensor_tensor(lo[:, ks, :], src, hi[:, ks, :], ALU.subtract).then_inc(done, 1)

            def rms_parts(tmp, src, buf, col, parts, hi_ready, done):
                for k in range(KT + 1):
                    if k < KT:
                        nc.vector.scalar_tensor_tensor(tmp[:, k, :], src[:, k, :], par[:, k, col:col + 1], buf[:],
                                                       ALU.mult, ALU.mult).then_inc(h_ready, 1)
                    if k > 0:
                        lo_part(parts[1], tmp[:, k - 1:k, :], parts[0], slice(k - 1, k), (hi_ready, k), done)

            def rms(dst, src, buf, col, ready):
                for k in range(KT):
                    nc.vector.scalar_tensor_tensor(dst[:, k, :], src[:, k, :], par[:, k, col:col + 1], buf[:],
                                                   ALU.mult, ALU.mult).then_inc(ready, 1)

            v.wait_ge(consts, CONSTS)
            step(nc.vector.tensor_copy(iota_f[:], iota_i[:]))
            step(nc.vector.tensor_scalar(iota_c[:], iota_f[:], float(CAP), float(CAP), ALU.is_ge, ALU.mult))
            step(nc.vector.tensor_tensor(iota_c[:], iota_f[:], iota_c[:], ALU.subtract))
            step(nc.vector.tensor_scalar(roff[:], iota_f[:, 0:MAX_ROUNDS + 1], -float(CAP), -1.0, ALU.mult, ALU.add))
            for half in range(2):
                v.wait_ge(x_in[half], 16)
            v.wait_ge(par_in, 16)
            variance("sum_x2", stat)
            inverse_root(1, stat)
            rms_parts(lru_h, xT, stat, P_MIX_G, h1_parts, h1_hi, h1_done)

            lam_in = par[:, :, P_LAM:P_LAM + 2]
            nc.vector.scalar_tensor_tensor(lam[:, 0], lam_in, -1.0, lam_in, ALU.mult, ALU.min).then_inc(lam_abs, 1)
            v.wait_ge(lam_exp, 1)
            step(nc.vector.tensor_scalar(lam[:, 2], lam[:, 1], 2.0, None, ALU.add))
            step(nc.vector.reciprocal(lam[:, 2], lam[:, 2]))
            step(nc.vector.tensor_tensor(lam[:, 2], lam[:, 1], lam[:, 2], ALU.mult))
            step(nc.vector.tensor_tensor(lam[:, 3], lam[:, 2], lam[:, 2], ALU.mult))
            step(nc.vector.memset(lam[:, 4], 1.0 / 17))
            for n in (15, 13, 11, 9, 7, 5, 3, 1):
                step(nc.vector.tensor_tensor(lam[:, 4], lam[:, 4], lam[:, 3], ALU.mult))
                step(nc.vector.tensor_scalar(lam[:, 4], lam[:, 4], 1.0 / n, None, ALU.add))
            step(nc.vector.scalar_tensor_tensor(lam[:, 4], lam[:, 4], 2.0, lam[:, 2], ALU.mult, ALU.mult))
            step(nc.vector.tensor_scalar(lam[:, 3], lam_in, -1.0, 0.0, ALU.mult, ALU.max))
            step(nc.vector.tensor_tensor(lam[:, 4], lam[:, 3], lam[:, 4], ALU.add))
            step(nc.vector.tensor_scalar(lam[:, 5], lam[:, 4], 8.0, None, ALU.mult))
            nc.vector.tensor_scalar(lam[:, 6], lam[:, 4], -8.0, None, ALU.mult).then_inc(lam_ready, 1)

            def conv(dst, src, taps, w_col, b_col, m0, ready):
                for tap in range(taps):
                    for m in (m0, m0 + 1):
                        x = src[:, m, tap:tap + T]
                        w = par[:, m, w_col + tap:w_col + tap + 1]
                        if tap == 0:
                            ins = nc.vector.tensor_scalar(dst[:, m, :], x, w, par[:, m, b_col:b_col + 1],
                                                          ALU.mult, ALU.add)
                        else:
                            ins = nc.vector.scalar_tensor_tensor(dst[:, m, :], x, w, dst[:, m, :], ALU.mult, ALU.add)
                        if tap == taps - 1 and m == m0 + 1:
                            ins.then_inc(ready, 1)
                        else:
                            step(ins, lag=1)

            for i in range(4):
                wait_product(v, "cv", i)
                v.wait_ge(sig_ready, i + 1)
                nc.vector.tensor_tensor(glu[:, 2 * i:2 * i + 2, CONF_LEFT:CONF_LEFT + T], pair(ps("cv", i)),
                                        sig[:, i % 2].rearrange("p (m t) -> p m t", m=2), ALU.mult).then_inc(glu_ready, 1)
                v.wait_ge(glu_ready, i + 1)
                conv(cv, glu, CONF_TAPS, P_DW_W, P_DW_B, 2 * i, conv_ready)
                if i == 0:
                    variance("sum_m2", mstat)
                if i == 1:
                    inverse_root(2, mstat)
                    v.wait_ge(mem_in, 16)
                    rms(memT, memT, mstat, P_MEM_G, mem_ready)
            for i in range(4):
                v.wait_ge(xr_ready, i + 1)
                conv(xc, xr, LRU_TAPS, P_LRU_W, P_LRU_CB, 2 * i, xc_ready)

            wait_product(v, "ln_mean")
            nc.vector.tensor_scalar(mstat[:], ps("ln_mean")[:, 0:T], 1.0 / D, None, ALU.mult).then_inc(mean_read, 1)
            v.wait_ge(mean_read, 1)
            v.wait_ge(conv_ready, 4)
            spread = lambda s: s[:].rearrange("p (a t) -> p a t", a=1).to_broadcast([P, KT, T])
            nc.vector.tensor_tensor(cv[:], cv[:], spread(mstat), ALU.subtract).then_inc(centred, 1)
            v.wait_ge(xc_ready, 4)
            def lru(d):
                for i in range(4):
                    pr = slice(2 * i, 2 * i + 2)
                    tmp = sig[:, i % 2].rearrange("p (m t) -> p m t", m=2)
                    v.wait_ge(lru_gates, 16 * d + 4 * i + 4)
                    step(nc.vector.tensor_tensor(lru_u[:, pr, :], lru_u[:, pr, :], xc[:, pr, :], ALU.mult), lag=1)
                    if d == 0 and i == 0:
                        split_w("gb", 0)
                    v.wait_ge(lru_exp, KT * d + 2 * i + 2)
                    step(nc.vector.tensor_tensor(tmp, lru_a[:, pr, :], lru_a[:, pr, :], ALU.mult))
                    nc.vector.scalar_tensor_tensor(lru_t[:, pr, :], tmp, 1.0, lru_t[:, pr, :], ALU.add,
                                                   ALU.mult).then_inc(lru_sq, 1)
                if d == 0:
                    wait_product(v, "ln_var")
                for i in range(4):
                    pr = slice(2 * i, 2 * i + 2)
                    v.wait_ge(lru_root, 4 * d + i + 1)
                    step(nc.vector.tensor_tensor(lru_u[:, pr, :], lru_u[:, pr, :], lru_t[:, pr, :], ALU.mult))
                    for m in (2 * i, 2 * i + 1):
                        dst, c, u = (x[:, m, :] for x in ((lru_t if d else lru_h), lru_a, lru_u))
                        if d:
                            dst, c, u = dst[:, ::-1], c[:, ::-1], u[:, ::-1]
                        nc.vector.tensor_tensor_scan(dst, c, u, 0.0, ALU.mult, ALU.add).then_inc(lru_scanned, 1)
            lru(0)
            variance("ln_var", stat)
            inverse_root(3, stat)
            v.wait_ge(centred, 1)
            nc.vector.tensor_tensor(cv[:], cv[:], spread(stat), ALU.mult).then_inc(ln_ready, 1)
            split_w("gb", 1)
            wait_product(v, "gb", 3)
            for k in range(KT):
                v.wait_ge(swish_ready, k + 1)
                nc.vector.tensor_copy(x_hi[:, k, :], cv[:, k, :]).then_inc(sw_hi, 1)
                if k > 0:
                    lo_part(h1_lo, cv[:, k - 1:k, :], x_hi, slice(k - 1, k), (sw_hi, k), sw_done)
            lo_part(h1_lo, cv[:, KT - 1:KT, :], x_hi, slice(KT - 1, KT), (sw_hi, KT), sw_done)
            lru(1)
            v.wait_ge(lru_scanned, 2 * KT)
            v.wait_ge(gl_ready, 4)
            for i in range(5):
                pr, before_pr = slice(2 * i, 2 * i + 2), slice(2 * i - 2, 2 * i)
                if i < 4:
                    step(nc.vector.tensor_tensor(lru_h[:, pr, :], lru_h[:, pr, :], lru_t[:, pr, :], ALU.add))
                    nc.vector.tensor_tensor(gl[:, pr, :], gl[:, pr, :], lru_h[:, pr, :], ALU.mult).then_inc(lru_ready, 1)
                if i > 0:
                    lo_part(lru_lo, gl[:, before_pr, :], lru_hi, before_pr, (lr_hi, i), lr_done)

            for i in range(4):
                pr = slice(2 * i, 2 * i + 2)
                wait_product(v, "yb", i)
                v.wait_ge(mgate_ready, 10 + 2 * i)
                nc.vector.tensor_tensor(gate_b[:, pr, :], pair(ps("yb", i)), gate_b[:, pr, :], ALU.mult).then_inc(yb_read, 1)
            for i in range(4):
                pr = slice(2 * i, 2 * i + 2)
                wait_product(v, "ya", i)
                split_w(*SPLIT[SPLIT_AT[("ya", i)] + SPLIT_BUFS])
                nc.vector.tensor_tensor(gate_a[:, pr, :], pair(ps("ya", i)), gate_a[:, pr, :], ALU.mult).then_inc(ya_read, 1)
                v.wait_ge(ya_read, i + 1)
                v.wait_ge(yb_read, i + 1)
                nc.vector.tensor_tensor(gate_a[:, pr, :], gate_a[:, pr, :], gate_b[:, pr, :], ALU.add).then_inc(merged, 1)
                lo_part(mid_lo, gate_a[:, pr, :], x_hi, pr, (mg_hi, i + 1), mg_done)

            def residual(name, ready):
                for i in range(4):
                    pr = slice(2 * i, 2 * i + 2)
                    wait_product(v, name, i)
                    nc.vector.tensor_tensor(xT[:, pr, :], pair(ps(name, i)), xT[:, pr, :], ALU.add).then_inc(ready, 1)
                    if i < 2:
                        split_w(name, i + 2)

            residual("wo", x1_ready)
            variance("sum_x1", stat)
            inverse_root(4, stat)
            rms_parts(lru_u, xT, stat, P_XA_G, h2_parts, h2_hi, h2_done)

            for h in range(HEADS):
                wait_product(v, "score", h)
                step(nc.vector.reduce_max(sm[:, 0, h, :], pair(ps("score", h)), AX.X))
                nc.vector.tensor_scalar(sm[:, 1, h, :], sm[:, 0, h, :], -HD ** -0.5, None, ALU.mult).then_inc(smax_ready, 1)
            for h in range(HEADS):
                v.wait_ge(sexp_ready, 2 * h + 2)
                step(nc.vector.reciprocal(sm[:, 3, h, :], sm[:, 2, h, :]))
                for t in range(TT):
                    ins = nc.vector.tensor_scalar(prob[:, h, t, :], prob[:, h, t, :], sm[:, 3, h, t:t + 1], None, ALU.mult)
                    if t == 0:
                        step(ins)
                    else:
                        ins.then_inc(prob_ready, 1)

            for i in range(4):
                pr = slice(2 * i, 2 * i + 2)
                lo_part(attn_lo, pair(ps("attn", i)), x_hi, pr, (at_hi, i + 1), at_done)
            residual("o", xf_ready)
            variance("sum_xf", stat)
            inverse_root(5, stat)
            rms(hT, xT, stat, P_FFN_G, h_ready)
            step(nc.vector.memset(wpick, 0.0))

            wait_product(v, "logit")
            parts = ps("logit")[:, 0:TT * P].rearrange("p (t c e) -> p t e c", t=TT, c=4)
            nc.vector.reduce_sum(lg[:], parts, AX.X).then_inc(logit_read, 1)
            v.wait_ge(logit_read, 1)
            for t in range(TT):
                step(nc.vector.max(top_v[:, t, :], lg[:, t, :]), lag=1)
            v.wait_ge(v_chain, done[0])
            nc.vector.tensor_scalar(t1[:, :, 0:1], top_v[:, :, 0:1], -1.0, None, ALU.mult).then_inc(top_ready, 1)
            for t in range(TT):
                step(nc.vector.max_index(top_i[:, t, :], top_v[:, t, :], lg[:, t, :]), lag=1)
            v.wait_ge(v_chain, done[0])
            step(nc.vector.tensor_copy(top_f[:], top_i[:]))

            def on_experts(x):
                return x[:, :, 0:TOP].rearrange("p t (n a) -> p t n a", a=1).to_broadcast([P, TT, TOP, NE])

            experts = iota_f[:, 0:NE].rearrange("p (t n e) -> p t n e", t=1, n=1).to_broadcast([P, TT, TOP, NE])
            step(nc.vector.tensor_tensor(hot, experts, on_experts(top_f), ALU.is_equal))
            nc.vector.reduce_sum(mask[:], hot.rearrange("p t n e -> p t e n"), AX.X).then_inc(mask_ready, 1)
            def on_rounds(x):
                return x[:].rearrange("p t (r e) -> p t r e", r=1).to_broadcast([P, TT, MAX_ROUNDS + 1, NE])

            by_round = lambda x: x[:].rearrange("p t (r e) -> p t r e", e=NE)

            wait_product(v, "rank")
            v.wait_ge(mask_ready, 1)
            rank_ps = ps("rank")[:, 0:TT * NE].rearrange("p (t e) -> p t e", t=TT)
            step(nc.vector.scalar_tensor_tensor(rank[:], rank_ps, 1.0, mask[:], ALU.add, ALU.mult))
            step(nc.vector.tensor_tensor(by_round(pos), on_rounds(rank),
                                         roff[:].rearrange("p (t r e) -> p t r e", t=1, e=1).to_broadcast(
                                             [P, TT, MAX_ROUNDS + 1, NE]), ALU.add))

            def pick_tokens(j):
                for t in range(TT):
                    last = nc.vector.tensor_scalar(pick[:, t, :], iota_f[:, 0:CAP], pos[:, t, bass.ds(j, 1)], None,
                                                   ALU.is_equal)
                last.then_inc(pick_ready, 1)

            pick_tokens(0)
            nc.vector.reduce_max(count[:, 0:1], ps("rank")[0:1, 2 * NE:3 * NE], AX.X).then_inc(rank_read, 1)
            v.wait_ge(rank_read, 1)
            step(nc.vector.tensor_scalar(count[:, 1:2], count[:, 0:1], float(CAP), 1.0, ALU.is_gt, ALU.add))
            for r in range(2, MAX_ROUNDS):
                step(nc.vector.scalar_tensor_tensor(count[:, 1:2], count[:, 0:1], float(CAP * r), count[:, 1:2],
                                                    ALU.is_gt, ALU.add))
            nc.vector.tensor_scalar(n_i[:, 0:1], count[:, 1:2], float(NE), None, ALU.mult).then_inc(count_ready, 1)
            nc.vector.tensor_copy(n_i[:, 1:2], count[:, 1:2]).then_inc(count_ready, 1)
            nc.vector.tensor_scalar(n_i[:, 2:3], count[:, 1:2], float(NE // GROUP), None, ALU.mult).then_inc(count_ready, 1)
            v.wait_ge(texp_ready, TT)
            step(nc.vector.reciprocal(t1[:, :, 2:3], t1[:, :, 1:2]))
            step(nc.vector.tensor_tensor(top_g[:, :, 0:TOP], top_g[:, :, 0:TOP],
                                         t1[:, :, 2:3].to_broadcast([P, TT, TOP]), ALU.mult))
            step(nc.vector.tensor_tensor(ghot, hot, on_experts(top_g), ALU.mult))
            step(nc.vector.reduce_sum(gate[:], ghot.rearrange("p t n e -> p t e n"), AX.X))
            step(nc.vector.tensor_copy(by_round(gatej), on_rounds(gate)), lag=1)
            wide = wpick.rearrange("p t (h c) -> p t h c", h=2)[:, :, :, 0:NE]
            nc.vector.tensor_copy(wide, gate[:].rearrange("p t (h e) -> p t h e", h=1).to_broadcast(
                [P, TT, 2, NE])).then_inc(wpick_ready, 1)
            v.wait_ge(v_chain, done[0])

            def copy_wpickT(n):
                v.wait_ge(wpickT_done, n)
                nc.vector.tensor_copy(wpickT, bank_a[:, 0:TT * P].rearrange("p (t c) -> p t c", t=TT)).then_inc(wpickT_ready, 1)

            copy_wpickT(1)
            v.wait_ge(count_ready, 3)
            jobs = v.value_load(n_i[0:1, 0:1], min_val=NE, max_val=JOBS_MAX)
            with v.Fori(0, jobs) as j:
                v.wait_ge(gathered, j + 1)
                pick_tokens(v.snap(j + 1))
                for t in range(TT):
                    last = nc.vector.tensor_scalar(wpick[:, t, :], iota_c[:], pos[:, t, bass.ds(j, 1)],
                                                   gatej[:, t, bass.ds(j, 1)], ALU.is_equal, ALU.mult)
                last.then_inc(wpick_ready, 1)
                v.wait_ge(chunk_used, JOB_CHUNKS * j + (SLOTS + UP_CHUNKS))
                nc.vector.tensor_scalar(gc, bank_g[:], LIMIT, None, ALU.min).then_inc(gclip_ready, 1)
                nc.vector.tensor_scalar(uc, bank_u[:], LIMIT, -LIMIT, ALU.min, ALU.max).then_inc(uclip_ready, 1)
                v.wait_ge(uclip_ready, j + 1)
                nc.vector.scalar_tensor_tensor(uc, uc, 1.0, gc, ALU.add, ALU.mult).then_inc(ug_ready, 1)
                v.wait_ge(ug_ready, j + 1)
                v.wait_ge(sigm_ready, j + 1)
                nc.vector.tensor_tensor(act, uc, sg, ALU.mult).then_inc(act_ready, 1)
                v.wait_ge(actT_done, j + 1)
                nc.vector.tensor_copy(actT, bank_a[:].rearrange("p (c n) -> p c n", c=4)).then_inc(actT_ready, 1)
                copy_wpickT(v.snap(j + 2))

            v.wait_ge(ysum_ready, TT)
            nc.vector.tensor_scalar(fin[:, 0:TT], fin[:, 0:TT], 1.0 / D, EPS, ALU.mult, ALU.add).then_inc(yvar_ready, 1)
            v.wait_ge(yroot_ready, 1)
            step(nc.vector.reciprocal(fin[:, TT:2 * TT], fin[:, 0:TT]))
            v.wait_ge(gfin_ready, 2)
            for t in range(TT):
                nc.vector.scalar_tensor_tensor(y_sb[:, t, :], y_ps[:, t, :], fin[:, TT + t:TT + t + 1], gfin,
                                               ALU.mult, ALU.mult).then_inc(y_ready, 1)


_PLAIN = ["w_in", "lru_w_a", "lru_w_i", "w_rnn_out", "w_conf_out", "w_out", "xa_w_q", "xa_w_kv", "xa_w_o",
          "router_w", "router_b", "exp_w_up", "exp_b_up", "exp_w_down", "exp_b_down"]


def kernel(**inputs):
    import numpy as np
    import concourse.bacc as bacc
    from concourse.bass_utils import run_bass_kernel_spmd

    a = {k: np.asarray(v) for k, v in inputs.items()}
    rows = [a["norm_mix_g"], a["lru_conv_b"], a["lru_b_a"][0], a["lru_b_i"][0], a["lru_lambda"][0], a["conf_dw_b"],
            a["conf_ln_g"], a["conf_ln_b"], a["norm_xa_g"], a["norm_mem_g"], a["norm_ffn_g"],
            a["b_branch_gate"][0], a["lru_conv_w"][0], a["conf_dw_w"][0]]
    par = np.ascontiguousarray(np.concatenate(rows, axis=0).reshape(N_PAR, KT, P).transpose(2, 1, 0))

    def channel_major(x):
        return np.ascontiguousarray(x[0].reshape(T, KT, P).transpose(2, 1, 0))

    arrays = {"xT": channel_major(a["x"]), "memT": channel_major(a["mem"]), "par": par}
    for name in _PLAIN:
        arrays[name] = np.ascontiguousarray(a[name] if name == "router_b" else a[name][0])
    arrays["final_norm_g"] = np.ascontiguousarray(a["final_norm_g"].reshape(1, D))

    nc = bacc.Bacc("TRN2", target_bir_lowering=False, num_devices=1)
    aps = [nc.dram_tensor("in_" + k, x.shape, mybir.dt.from_np(x.dtype), kind="ExternalInput").ap()
           for k, x in arrays.items()]
    out = nc.dram_tensor("out_y", (T, D), F32, kind="ExternalOutput").ap()
    encoder_kernel(nc, *aps, out)
    r = run_bass_kernel_spmd(nc, [{"in_" + k: x for k, x in arrays.items()}], core_ids=[0])
    return r.results[0]["out_y"].reshape(1, T, D)
```

```python
from contextlib import ExitStack

import concourse.bass as bass
from concourse import mybir

F32 = mybir.dt.float32
F32R = mybir.dt.float32r
I32 = mybir.dt.int32
U32 = mybir.dt.uint32
ALU = mybir.AluOpType
ACT = mybir.ActivationFunctionType
AX = mybir.AxisListType

P = 128
D = 1024
KT = D // P
T = 256
TT = T // P
HEADS = 4
HD = D // HEADS
NE = 32
TOP = 4
F = D
EPS = 1e-5
SWIGLU_ALPHA, LIMIT = 1.702, 7.0
LRU_TAPS, CONF_TAPS = 4, 31
LRU_LEFT, CONF_LEFT = 2, 15

CHUNK = 2048
COLS = CHUNK // KT
PRE_SLOTS = 3
SPLIT_BUFS = 2
UP_CHUNKS = KT
DOWN_CHUNKS = KT // 2
JOB_CHUNKS = UP_CHUNKS + DOWN_CHUNKS
SLOTS = 16
MAIN_SLOTS = 12
GROUP = SLOTS // 4
CAP = 64
MAX_ROUNDS = T // CAP
JOBS_MAX = NE * MAX_ROUNDS
POS_W = NE * (MAX_ROUNDS + 1)
NBANK = 4

(P_MIX_G, P_LRU_CB, P_BA, P_BI, P_LAM, P_DW_B, P_LN_G, P_LN_B, P_XA_G, P_MEM_G, P_FFN_G, P_GATE_B,
 P_LRU_W, P_DW_W, N_PAR) = (0, 1, 2, 4, 6, 8, 9, 10, 11, 12, 13, 14, 16, 20, 51)

WEIGHTED = ("cg", "cv", "xr", "gr", "k", "v", "ga", "gb", "ya", "yb", "wo", "q", "o")
PRODUCTS = (
    [("sum_x2", 0)] + [(n, 0) for n in ("cg", "cv", "xr", "gr")] + [("sum_m2", 0)]
    + [(n, i) for i in range(1, 4) for n in ("cg", "cv", "xr", "gr")]
    + [("k", i) for i in range(4)]
    + [(n, i) for i in range(4) for n in ("ra0", "ri0")] + [("ga", 0)]
    + [("ga", 1), ("ga", 2), ("ln_mean", 0), ("ga", 3), ("gb", 0), ("ln_var", 0)]
    + [(n, i) for i in range(4) for n in ("ra1", "ri1")] + [("gb", 1), ("gb", 2), ("gb", 3)]
    + [("yb", i) for i in range(4)] + [("ya", i) for i in range(4)]
    + [("v", 0)]
    + [("wo", i) for i in range(4)] + [("v", 1), ("sum_x1", 0), ("v", 2), ("v", 3)]
    + [("q", i) for i in range(4)]
    + [("score", h) for h in range(HEADS)]
    + [("probT", 0), ("probT", 1), ("attn", 0), ("probT", 2), ("attn", 1), ("probT", 3), ("attn", 2), ("attn", 3)]
    + [("o", i) for i in range(4)] + [("logitT", 0), ("logit", 0)]
    + [("htok", i) for i in range(4)] + [("gfin", 0), ("gfin", 1), ("rank", 0)]
)
AT = {name: i for i, name in enumerate(PRODUCTS)}
CHUNKS = [x for x in PRODUCTS if x[0] in WEIGHTED]
CHUNK_AT = {name: i for i, name in enumerate(CHUNKS)}
SPLIT = [x for x in CHUNKS if x[0] != "v"]
SPLIT_AT = {name: i for i, name in enumerate(SPLIT)}


def encoder_kernel(nc, xT_d, memT_d, par_d, w_in, lru_w_a, lru_w_i, w_rnn_out, w_conf_out, w_out,
                   w_q, w_kv, w_o, router_w, router_b, w_up, b_up, w_down, b_down, g_final, out):
    sources = {"xr": (w_in, 0), "gr": (w_in, D), "cv": (w_in, 2 * D), "cg": (w_in, 3 * D),
               "ga": (w_in, 4 * D), "gb": (w_in, 5 * D), "k": (w_kv, 0), "v": (w_kv, D),
               "ya": (w_rnn_out, 0), "yb": (w_conf_out, 0), "wo": (w_out, 0), "q": (w_q, 0),
               "o": (w_o, 0)}

    with ExitStack() as ctx:
        def sb(name, shape, dt=F32):
            return ctx.enter_context(nc.sbuf_tensor(name, shape, dt))

        def sem(name):
            return ctx.enter_context(nc.semaphore(name))

        def split_tile(name, shape, over):
            return nc.alloc_sbuf_tensor_at(name, shape, F32R, offset=over)

        def next_offset():
            return -(-nc.sbuf_base // 32) * 32

        place = {"ring": next_offset()}
        ring = sb("ring", [P, MAIN_SLOTS, CHUNK])
        w_hi = split_tile("w_hi", [P, SPLIT_BUFS, KT, COLS], place["ring"])
        w_lo = split_tile("w_lo", [P, SPLIT_BUFS, KT, COLS], place["ring"] + SPLIT_BUFS * CHUNK * 4)
        lru_gate_w = ring[:, 4:6, :].rearrange("p s (a m n) -> p (s a) m n", m=KT, n=P)
        memT = ring[:, 6, :].rearrange("p (k t) -> p k t", k=KT)
        lru_t = ring[:, 8, :].rearrange("p (k t) -> p k t", k=KT)
        xc = ring[:, 7, :].rearrange("p (k t) -> p k t", k=KT)
        pre_slot = [ring[:, MAIN_SLOTS - PRE_SLOTS + i, :].rearrange("p (k n) -> p k n", k=KT)
                    for i in range(PRE_SLOTS)]

        def act_tile(name, width=T):
            place[name] = next_offset()
            return sb(name, [P, KT, width])

        xT = act_tile("xT")
        hT = act_tile("hT")
        glu = act_tile("glu", T + CONF_TAPS - 1)
        cv = act_tile("cv")
        xr = act_tile("xr", T + LRU_TAPS - 1)
        gl = act_tile("gl")
        keyT = act_tile("keyT")
        place["val"] = next_offset()
        val = sb("val", [P, TT, D])
        lru_a = act_tile("lru_a")
        lru_u = act_tile("lru_u")
        lru_h = act_tile("lru_h")
        ln_squares = xr[:, :, 0:T]
        gate_a, gate_b = glu[:, :, 0:T], xr[:, :, 0:T]
        qT = lru_a
        prob = lru_u[:, :, :].rearrange("p (h t) m -> p h t m", h=HEADS)
        probT = lru_h[:, :, :].rearrange("p (h t) m -> p h t m", h=HEADS)
        x_tile = lambda name, over: split_tile(name, [P, KT, T], place[over])
        x_hi = x_tile("x_hi", "hT")
        h1_lo, lru_hi, lru_lo = x_tile("h1_lo", "val"), x_tile("lru_hi", "lru_a"), x_tile("lru_lo", "lru_u")
        mid_lo, attn_lo = x_tile("mid_lo", "lru_h"), x_tile("attn_lo", "gl")
        mem_parts = (lru_hi, lru_lo)
        h1_parts, swish_parts, lru_parts = (x_hi, h1_lo), (x_hi, h1_lo), (lru_hi, lru_lo)
        merged_parts, h2_parts, attn_parts = (x_hi, mid_lo), (x_hi, mid_lo), (x_hi, attn_lo)
        sig = sb("sig", [P, 2, 2 * T])
        ssq = sb("ssq", [P, 2, TT])
        tok_rms = sb("tok_rms", [P, TT])
        lgT = sig[:, 0, 0:T]
        hot = sig[:, 1, 0:T].rearrange("p (t n e) -> p t n e", t=TT, n=TOP)
        ghot = sig[:, 1, T:2 * T].rearrange("p (t n e) -> p t n e", t=TT, n=TOP)
        par = sb("par", [P, KT, N_PAR])
        ident = sb("ident", [P, P])
        ones = sb("ones", [P, P])
        before = sb("before", [P, P])
        stat = sb("stat", [P, T])
        mstat = sb("mstat", [P, T])
        lam = sb("lam", [P, 7, KT, 2])
        router = sb("router", [P, KT, NE])
        rb_row = sb("rb_row", [1, NE])
        sm = sb("sm", [P, 4, HEADS, TT])
        lg = sb("lg", [P, TT, NE])
        top_v = sb("top_v", [P, TT, 8])
        top_i = sb("top_i", [P, TT, 8], U32)
        top_f = sb("top_f", [P, TT, 8])
        top_g = sb("top_g", [P, TT, 8])
        t1 = sb("t1", [P, TT, 4])
        iota_i = sb("iota_i", [P, P], I32)
        iota_f = sb("iota_f", [P, P])
        iota_c = sb("iota_c", [P, P])
        mask = sb("mask", [P, TT, NE])
        gate = sb("gate", [P, TT, NE])
        roff = sb("roff", [P, MAX_ROUNDS + 1])
        rank = sb("rank", [P, TT, NE])
        pos = sb("pos", [P, TT, POS_W])
        gatej = sb("gatej", [P, TT, POS_W])
        count = sb("count", [1, 4])
        n_i = sb("n_i", [1, 3], I32)
        xgT = val[:, :, :].rearrange("p m (k t) -> p (m k) t", t=T)
        h_tok = keyT[:, :, :].rearrange("p (t k) c -> p t (k c)", t=TT)
        gc, uc = val[:, 0, 0:512], val[:, 0, 512:1024]
        sg, act = val[:, 1, 0:512], val[:, 1, 512:1024]
        xg = lru_a[:, 0:2, :].rearrange("p a (h c) -> p (a h) c", c=P)
        xtok = lru_u[:, 1:3, :].rearrange("p a c -> p (a c)")
        actT = lru_a[:, 2:4, :].rearrange("p a (h c) -> p (a h) c", c=P)
        job_out = lru_a[:, 4:6, :].rearrange("p a c -> p (a c)")
        pick = lru_a[:, 6, 0:TT * CAP].rearrange("p (t c) -> p t c", t=TT)
        wpick = lru_a[:, 7, :].rearrange("p (t c) -> p t c", t=TT)
        wpickT = lru_u[:, 0, :].rearrange("p (t c) -> p t c", t=TT)
        half_row = lambda x, k: x[0:1, k:k + 4, :].rearrange("p k t -> p (k t)")
        bup_rows = ((half_row(lru_h, 0), half_row(lru_h, 4)), (half_row(cv, 4), half_row(lru_u, 4)))
        more_slots = [x[:, :, :].rearrange("p k t -> p (k t)")[:, 0:CHUNK] for x in (glu, xr, gl, hT)]
        expert_slot = [ring[:, i, :] for i in range(MAIN_SLOTS)] + more_slots
        y_sb = xT[:, :, :].rearrange("p (t k) c -> p t (k c)", t=TT)
        gfin = cv[:, 0:4, :].rearrange("p k t -> p (k t)")
        gfin_row = cv[0:1, 4:8, :].rearrange("p k t -> p (k t)")
        fin = sb("fin", [P, 3])

        bank = [ctx.enter_context(nc.psum_tensor(f"bank{i}", [P, 512], F32)) for i in range(NBANK)]
        y_ps = ctx.enter_context(nc.psum_tensor("y_ps", [P, TT, D], F32))

        x_in = [sem("x_in0"), sem("x_in1")]
        mem_in, par_in, lruw_in, router_in, gfin_in = map(sem, (
            "mem_in", "par_in", "lruw_in", "router_in", "gfin_in"))
        zeroed, consts = sem("zeroed"), sem("consts")
        pre_loaded = [sem(f"pre_loaded{i}") for i in range(PRE_SLOTS)]
        w_hi_ready = [sem(f"w_hi_ready{b}") for b in range(SPLIT_BUFS)]
        w_lo_ready = [sem(f"w_lo_ready{b}") for b in range(SPLIT_BUFS)]
        h1_hi, h1_done, h2_hi, h2_done, sw_hi, sw_done = map(sem, (
            "h1_hi", "h1_lo_ready", "h2_hi", "h2_lo_ready", "swish_hi", "swish_lo_ready"))
        mem_hi, mem_done = sem("mem_hi"), sem("mem_lo_ready")
        lr_hi, lr_done, mg_hi, mg_done, at_hi, at_done = map(sem, (
            "lru_hi_ready", "lru_lo_ready", "merged_hi", "merged_lo_ready", "attn_hi", "attn_lo_ready"))
        product = sem("product")
        mean_read, logit_read, rank_read, yb_read, ya_read = map(sem, (
            "mean_read", "logit_read", "rank_read", "yb_read", "ya_read"))
        logitT_ready = sem("logitT_ready")
        x_sq, m_sq, ln_sq, x1_sq = map(sem, ("x_sq", "m_sq", "ln_sq", "x1_sq"))
        y_set, xf_ssq, tok_ready = sem("y_set"), sem("xf_ssq"), sem("tok_ready")
        var_ready, root_ready = sem("var_ready"), sem("root_ready")
        lam_abs, lam_exp, lam_ready = sem("lam_abs"), sem("lam_exp"), sem("lam_ready")
        h_ready, mem_ready = sem("h_ready"), sem("mem_ready")
        sig_ready, glu_ready, xr_ready, gl_ready, k_ready, v_ready = map(sem, (
            "sig_ready", "glu_ready", "xr_ready", "gl_ready", "k_ready", "v_ready"))
        conv_ready, xc_ready, centred, ln_ready, swish_ready = map(sem, (
            "conv_ready", "xc_ready", "centred", "ln_ready", "swish_ready"))
        lru_gates, lru_exp, lru_sq, lru_root, lru_scanned, lru_ready = map(sem, (
            "lru_gates", "lru_exp", "lru_sq", "lru_root", "lru_scanned", "lru_ready"))
        mgate_ready, merged, x1_ready, xf_ready = map(sem, ("mgate_ready", "merged", "x1_ready", "xf_ready"))
        q_ready, smax_ready, sexp_ready, prob_ready, probT_ready = map(sem, (
            "q_ready", "smax_ready", "sexp_ready", "prob_ready", "probT_ready"))
        top_ready, texp_ready, mask_ready, count_ready, htok_ready, gfin_ready = map(sem, (
            "top_ready", "texp_ready", "mask_ready", "count_ready", "htok_ready", "gfin_ready"))
        loaded = [sem(f"loaded{s}") for s in range(SLOTS)]
        chunk_used, bias_in = sem("chunk_used"), [sem("bias_in0"), sem("bias_in1")]
        pick_ready, wpickT_done, wpickT_ready, gathered, xtok_ready, xgT_done, xg_ready = map(sem, (
            "pick_ready", "wpickT_done", "wpickT_ready", "gathered", "xtok_ready", "xgT_done", "xg_ready"))
        gclip_ready, sigm_ready, act_ready, actT_done, actT_ready = map(sem, (
            "gclip_ready", "sigm_ready", "act_ready", "actT_done", "actT_ready"))
        job_out_ready, y_done, ysum_ready, yvar_ready, yroot_ready, y_ready, stored = map(sem, (
            "job_out_ready", "y_done", "ysum_ready", "yvar_ready", "yroot_ready", "y_ready", "stored"))
        wpick_ready, bdown_in = sem("wpick_ready"), sem("bdown_in")
        v_chain, uclip_ready, ug_ready = sem("v_chain"), sem("uclip_ready"), sem("ug_ready")

        bank_g, bank_u, bank_x, bank_a = bank

        def pair(x):
            return x[:].rearrange("p (m t) -> p m t", m=2)

        def ps(name, i=0):
            return bank[AT[(name, i)] % NBANK]

        def wait_product(eng, name, i=0):
            eng.wait_ge(product, AT[(name, i)] + 1)

        read = {("sum_x2", 0): (var_ready, 1), ("sum_m2", 0): (var_ready, 2), ("ln_mean", 0): (mean_read, 1),
                ("ln_var", 0): (var_ready, 3), ("sum_x1", 0): (var_ready, 4),
                ("logit", 0): (logit_read, 2), ("logitT", 0): (logitT_ready, 1), ("rank", 0): (rank_read, 1)}
        for i in range(4):
            read.update({("cg", i): (sig_ready, i + 1), ("cv", i): (glu_ready, i + 1), ("xr", i): (xr_ready, i + 1),
                         ("gr", i): (gl_ready, i + 1), ("k", i): (k_ready, i + 1), ("v", i): (v_ready, i + 1),
                         ("ga", i): (mgate_ready, 2 * i + 2), ("gb", i): (mgate_ready, 2 * i + 10),
                         ("yb", i): (yb_read, i + 1), ("ya", i): (ya_read, i + 1), ("wo", i): (x1_ready, i + 1),
                         ("q", i): (q_ready, i + 1), ("score", i): (sexp_ready, 2 * i + 2),
                         ("probT", i): (probT_ready, i + 1), ("attn", i): (at_done, i + 1),
                         ("o", i): (xf_ready, i + 1), ("htok", i): (htok_ready, i + 1)})
            for d in range(2):
                read.update({(f"ra{d}", i): (lru_gates, 16 * d + 4 * i + 2),
                             (f"ri{d}", i): (lru_gates, 16 * d + 4 * i + 4)})
        for i in range(2):
            read[("gfin", i)] = (gfin_ready, i + 1)

        HALF = KT // 2

        def split_w_hi(eng, copy, name, i):
            s, n = SPLIT_AT[(name, i)], CHUNK_AT[(name, i)]
            b = s % SPLIT_BUFS
            eng.wait_ge(pre_loaded[n % PRE_SLOTS], 16 * (n // PRE_SLOTS + 1))
            if s >= SPLIT_BUFS:
                wait_product(eng, *SPLIT[s - SPLIT_BUFS])
            for ks in (slice(0, HALF), slice(HALF, KT)):
                copy(w_hi[:, b, ks, :], pre_slot[n % PRE_SLOTS][:, ks, :]).then_inc(w_hi_ready[b], 1)

        block = ctx.enter_context(nc.Block())

        @block.sync
        def _(sp):
            for half in range(2):
                ks = slice(HALF * half, HALF * (half + 1))
                sp.dma_start(xT[:, ks, :], xT_d[:, ks, :]).then_inc(x_in[half], 16)

            def former_used(n):
                if CHUNKS[n] in SPLIT_AT:
                    s = SPLIT_AT[CHUNKS[n]]
                    sp.wait_ge(w_lo_ready[s % SPLIT_BUFS], 2 * (s // SPLIT_BUFS) + 2)
                else:
                    wait_product(sp, *CHUNKS[n])

            def load_projection(n):
                name, i = CHUNKS[n]
                w, col = sources[name]
                src = w[:, col + COLS * i:col + COLS * (i + 1)].rearrange("(k p) n -> p k n", p=P)
                if n >= PRE_SLOTS:
                    former_used(n - PRE_SLOTS)
                sp.dma_start(pre_slot[n % PRE_SLOTS], src).then_inc(pre_loaded[n % PRE_SLOTS], 16)

            def expert_source(e, s):
                if s < UP_CHUNKS:
                    return w_up[e, P * s:P * (s + 1), :].rearrange("a p n -> p (a n)")
                k = 2 * (s - UP_CHUNKS)
                return w_down[e, P * k:P * (k + 2), :].rearrange("a (k p) n -> p (a k) n", p=P)

            def load_expert(e, c, slot):
                dst = expert_slot[slot] if c < UP_CHUNKS else expert_slot[slot].rearrange("p (k n) -> p k n", k=2)
                sp.dma_start(dst, expert_source(e, c)).then_inc(loaded[slot], 16)

            def load_first(slot):
                e = slot // JOB_CHUNKS
                load_expert(slice(e, e + 1), slot % JOB_CHUNKS, slot)

            early = {("v", 1): 4, ("v", 2): 5, ("v", 3): 7, ("q", 0): 8, ("q", 1): 12, ("q", 2): 13, ("q", 3): 6}
            for n in range(len(CHUNKS)):
                load_projection(n)
                if n == 3:
                    sp.wait_ge(zeroed, 1)
                    for d in range(2):
                        for g, w in enumerate((lru_w_a, lru_w_i)):
                            for odd in range(2):
                                src = w[d].rearrange("(m o) i j -> o i m j", o=2)[odd]
                                block_diag = lru_gate_w[64 * odd:64 * odd + 64, 2 * d + g, :, 64 * odd:64 * odd + 64]
                                sp.dma_start(block_diag, src).then_inc(lruw_in, 16)
                    sp.dma_start(router[:], router_w.rearrange("(k p) e -> p k e", p=P)).then_inc(router_in, 16)
                    sp.dma_start(rb_row[:], router_b).then_inc(router_in, 16)
                if CHUNKS[n] in early:
                    slot = early[CHUNKS[n]]
                    sp.wait_ge(mg_done, 4)
                    if slot == 6:
                        wait_product(sp, "v", 3)
                    load_first(slot)

            def load_bias(expert, job_parity):
                for dst, col in zip(bup_rows[job_parity], (0, F)):
                    sp.dma_start(dst, b_up[expert, col:col + F]).then_inc(bias_in[job_parity], 16)

            wait_product(sp, "attn", 3)
            load_bias(slice(0, 1), 0)
            for n in range(len(CHUNKS) - PRE_SLOTS, len(CHUNKS)):
                former_used(n)
                load_first(MAIN_SLOTS - PRE_SLOTS + n % PRE_SLOTS)
            for b in range(SPLIT_BUFS):
                wait_product(sp, *SPLIT[len(SPLIT) - SPLIT_BUFS + b])
                load_first(b)
                load_first(SPLIT_BUFS + b)
            load_first(14)
            load_first(15)
            wait_product(sp, "gfin", 1)
            load_bias(slice(1, 2), 1)

            sp.wait_ge(job_out_ready, 1)
            for half in range(2):
                sp.dma_start(job_out[CAP * half:CAP * half + NE, :],
                             b_down[:, 512 * half:512 * (half + 1)]).then_inc(bdown_in, 16)

            def load_chunk(expert, u, c, first_chunk):
                n = u * JOB_CHUNKS + c
                sp.wait_ge(chunk_used, first_chunk + n + 1)
                if c == 0:
                    load_bias(expert, u % 2)
                load_expert(expert, c, n % SLOTS)

            for n in range(SLOTS, GROUP * JOB_CHUNKS):
                u, c = divmod(n, JOB_CHUNKS)
                load_chunk(slice(u, u + 1), u, c, 0)
            sp.wait_ge(count_ready, 3)
            rounds = sp.value_load(n_i[0:1, 1:2], min_val=1, max_val=MAX_ROUNDS)
            with sp.Fori(0, rounds) as r:
                first = sp.snap((((r + 3) >> 2) + 1) & 1)
                base = sp.snap(r * NE)
                with sp.Fori(first, NE // GROUP) as g:
                    e0 = sp.snap(g * GROUP)
                    job0 = sp.snap(base + e0)
                    first_chunk = sp.snap(job0 * JOB_CHUNKS)
                    for u in range(GROUP):
                        e = sp.snap(e0 + u)
                        for c in range(JOB_CHUNKS):
                            load_chunk(bass.ds(e, 1), u, c, first_chunk)

            for t in range(TT):
                sp.wait_ge(y_ready, t + 1)
                sp.dma_start(out[P * t:P * (t + 1), :], y_sb[:, t, :]).then_inc(stored, 16)
            sp.wait_ge(stored, 16 * TT)

        @block.gpsimd
        def _(pool):
            pool.memset(lru_gate_w, 0.0).then_inc(zeroed, 1)
            pool.memset(ones[:], 1.0).then_inc(consts, 1)
            pool.memset(ident[:], 0.0).then_inc(consts, 1)
            pool.wait_ge(consts, 2)
            pool.affine_select(out=ident[:], in_=ident[:], compare_op=ALU.not_equal, fill=1.0, base=0,
                               pattern=[[-1, P]], channel_multiplier=1).then_inc(consts, 1)
            pool.affine_select(out=before[:], in_=ones[:], compare_op=ALU.is_gt, fill=0.0, base=0,
                               pattern=[[1, P]], channel_multiplier=-1).then_inc(consts, 1)
            pool.iota(iota_i[:], pattern=[[1, P]], base=0, channel_multiplier=0).then_inc(consts, 1)
            pool.memset(glu[:, :, 0:CONF_LEFT], 0.0).then_inc(consts, 1)
            pool.memset(glu[:, :, CONF_LEFT + T:], 0.0).then_inc(consts, 1)
            pool.memset(xr[:, :, 0:LRU_LEFT], 0.0).then_inc(consts, 1)
            pool.memset(xr[:, :, LRU_LEFT + T:], 0.0).then_inc(consts, 1)
            for s, chunk in enumerate(SPLIT):
                b, n = s % SPLIT_BUFS, CHUNK_AT[chunk]
                if s >= SPLIT_BUFS:
                    wait_product(pool, *SPLIT[s - SPLIT_BUFS])
                for half, ks in enumerate((slice(0, HALF), slice(HALF, KT))):
                    pool.wait_ge(w_hi_ready[b], 2 * (s // SPLIT_BUFS) + half + 1)
                    pool.tensor_tensor(w_lo[:, b, ks, :], pre_slot[n % PRE_SLOTS][:, ks, :], w_hi[:, b, ks, :],
                                       ALU.subtract).then_inc(w_lo_ready[b], 1)
            wait_product(pool, "score", 3)
            pool.memset(job_out, 0.0).then_inc(job_out_ready, 1)
        CONSTS = 9

        @block.scalar
        def _(a):
            a.dma_start(par[:], par_d).then_inc(par_in, 16)
            a.dma_start(memT, memT_d).then_inc(mem_in, 16)

            def root(n, buf):
                a.wait_ge(var_ready, n)
                a.activation(buf[:], buf[:], ACT.Sqrt).then_inc(root_ready, 1)

            def split_w(name, i):
                split_w_hi(a, lambda dst, src: a.activation(dst, src, ACT.Copy), name, i)

            def split_x(src, ready, done, start=0, step=1):
                for n in range(KT // step):
                    a.wait_ge(ready, start + n + 1)
                    ks = slice(n * step, (n + 1) * step)
                    a.activation(x_hi[:, ks, :], src[:, ks, :], ACT.Copy).then_inc(done, 1)

            for half in range(2):
                ks = slice(HALF * half, HALF * (half + 1))
                a.wait_ge(x_in[half], 16)
                a.activation(lru_a[:, ks, :], xT[:, ks, :], ACT.Square).then_inc(x_sq, 1)
            a.wait_ge(consts, CONSTS)
            a.activation(fin[:, 2:3], ones[:, 0:1], ACT.Sqrt)
            root(1, stat)
            split_x(lru_h, h_ready, h1_hi)
            split_w("cv", 0)
            a.wait_ge(mem_in, 16)
            a.activation(lru_u[:], memT, ACT.Square).then_inc(m_sq, 1)
            a.wait_ge(lam_abs, 1)
            a.activation(lam[:, 1], lam[:, 0], ACT.Exp).then_inc(lam_exp, 1)

            for i in range(4):
                split_w("xr", i)
                wait_product(a, "cg", i)
                if i >= 2:
                    a.wait_ge(glu_ready, i - 1)
                a.activation(sig[:, i % 2], ps("cg", i)[:], ACT.Sigmoid).then_inc(sig_ready, 1)
                split_w("gr", i)
                following = (("cg", i + 1), ("cv", i + 1)) if i < 3 else (("k", 0), ("k", 1))
                split_w(*following[0])
                wait_product(a, "xr", i)
                a.activation(xr[:, 2 * i:2 * i + 2, LRU_LEFT:LRU_LEFT + T], pair(ps("xr", i)),
                             ACT.Copy).then_inc(xr_ready, 1)
                split_w(*following[1])
                wait_product(a, "gr", i)
                a.activation(gl[:, 2 * i:2 * i + 2, :], pair(ps("gr", i)),
                             ACT.Gelu_apprx_tanh).then_inc(gl_ready, 1)
                if i == 1:
                    root(2, mstat)
            for i in range(4):
                split_w(*(("k", 2), ("k", 3), ("ga", 0), ("ga", 1))[i])
                wait_product(a, "k", i)
                a.activation(keyT[:, 2 * i:2 * i + 2, :], pair(ps("k", i)), ACT.Copy).then_inc(k_ready, 1)

            def copy_v(i):
                wait_product(a, "v", i)
                a.activation(val[:, :, COLS * i:COLS * (i + 1)], pair(ps("v", i)), ACT.Copy).then_inc(v_ready, 1)

            def lru_sigmoids(d):
                for i in range(4):
                    for name, bias, dst in (("ra", P_BA, lru_a), ("ri", P_BI, lru_u)):
                        wait_product(a, f"{name}{d}", i)
                        for m in range(2):
                            a.activation(dst[:, 2 * i + m, :], ps(f"{name}{d}", i)[:, m * T:(m + 1) * T], ACT.Sigmoid,
                                         bias=par[:, 2 * i + m, bias + d:bias + d + 1]).then_inc(lru_gates, 1)

            def lru_tanhs(d):
                a.wait_ge(lru_gates, 16 * (d + 1))
                for m in range(KT):
                    a.activation(lru_t[:, m, :], lru_a[:, m, :], ACT.Tanh, scale=lam[:, 5, m, d:d + 1])

            def lru_exponentials(d):
                for m in range(KT):
                    a.activation(lru_a[:, m, :], lru_a[:, m, :], ACT.Exp,
                                 scale=lam[:, 6, m, d:d + 1]).then_inc(lru_exp, 1)

            def lru_roots(d):
                for i in range(4):
                    a.wait_ge(lru_sq, 4 * d + i + 1)
                    a.activation(lru_t[:, 2 * i:2 * i + 2, :], lru_t[:, 2 * i:2 * i + 2, :],
                                 ACT.Sqrt).then_inc(lru_root, 1)

            def merge_gate(name, i, col, dst):
                wait_product(a, name, i)
                for m in range(2):
                    a.activation(dst[:, 2 * i + m, :], ps(name, i)[:, m * T:(m + 1) * T], ACT.Sigmoid,
                                 bias=par[:, 2 * i + m, col:col + 1]).then_inc(mgate_ready, 1)

            a.wait_ge(lam_ready, 1)
            lru_sigmoids(0)
            lru_tanhs(0)
            split_w("ga", 2)
            lru_exponentials(0)
            split_w("ga", 3)
            a.wait_ge(conv_ready, 4)
            merge_gate("ga", 0, P_GATE_B, gate_a)
            merge_gate("ga", 1, P_GATE_B, gate_a)
            split_w("gb", 0)
            lru_roots(0)
            a.wait_ge(centred, 1)
            a.wait_ge(xc_ready, 4)
            a.activation(ln_squares, cv[:], ACT.Square).then_inc(ln_sq, 1)
            merge_gate("ga", 2, P_GATE_B, gate_a)
            root(3, stat)
            merge_gate("ga", 3, P_GATE_B, gate_a)
            wait_product(a, "ln_var")
            a.wait_ge(lru_scanned, KT)
            merge_gate("gb", 0, P_GATE_B + 1, gate_b)
            lru_sigmoids(1)
            split_w("gb", 2)
            a.wait_ge(ln_ready, 1)
            for m in range(KT):
                a.activation(cv[:, m, :], cv[:, m, :], ACT.Silu, bias=par[:, m, P_LN_B:P_LN_B + 1],
                             scale=par[:, m, P_LN_G:P_LN_G + 1]).then_inc(swish_ready, 1)
            split_w("gb", 3)
            merge_gate("gb", 1, P_GATE_B + 1, gate_b)
            lru_tanhs(1)
            split_w("yb", 0)
            lru_exponentials(1)
            split_w("yb", 1)
            lru_roots(1)
            split_w("yb", 2)
            merge_gate("gb", 2, P_GATE_B + 1, gate_b)
            merge_gate("gb", 3, P_GATE_B + 1, gate_b)
            split_w("yb", 3)
            for i in range(4):
                a.wait_ge(lru_ready, i + 1)
                a.activation(lru_hi[:, 2 * i:2 * i + 2, :], gl[:, 2 * i:2 * i + 2, :], ACT.Copy).then_inc(lr_hi, 1)
            split_w("ya", 0)
            split_w("ya", 1)
            wait_product(a, "yb", 3)
            a.dma_start(gfin_row, g_final).then_inc(gfin_in, 16)
            split_x(gate_a, merged, mg_hi, step=2)
            copy_v(0)

            for i in range(4):
                pr = slice(2 * i, 2 * i + 2)
                a.wait_ge(x1_ready, i + 1)
                a.activation(lru_a[:, pr, :], xT[:, pr, :], ACT.Square).then_inc(x1_sq, 1)
            copy_v(1)
            root(4, stat)
            split_x(lru_u, h_ready, h2_hi, start=KT)
            split_w("q", 0)
            copy_v(2)
            split_w("q", 1)
            copy_v(3)
            for i in range(4):
                split_w(*((("q", 2), ("q", 3), ("o", 0), ("o", 1))[i]))
                wait_product(a, "q", i)
                a.activation(qT[:, 2 * i:2 * i + 2, :], pair(ps("q", i)), ACT.Copy).then_inc(q_ready, 1)
            for h in range(HEADS):
                a.wait_ge(smax_ready, h + 1)
                for t in range(TT):
                    a.activation(prob[:, h, t, :], ps("score", h)[:, t * T:(t + 1) * T], ACT.Exp,
                                 bias=sm[:, 1, h, t:t + 1], scale=HD ** -0.5,
                                 accum_out=sm[:, 2, h, t:t + 1]).then_inc(sexp_ready, 1)
            for name, i in (("probT", 0), ("probT", 1), ("attn", 0), ("probT", 2), ("attn", 1), ("probT", 3),
                            ("attn", 2), ("attn", 3)):
                wait_product(a, name, i)
                if name == "probT":
                    a.activation(probT[:, i, :, :], pair(ps(name, i)), ACT.Copy).then_inc(probT_ready, 1)
                else:
                    a.activation(x_hi[:, 2 * i:2 * i + 2, :], pair(ps(name, i)), ACT.Copy).then_inc(at_hi, 1)
            a.activation(fin[:, 2:3], ones[:, 0:1], ACT.Sqrt)
            for half in range(2):
                for t in range(TT):
                    a.wait_ge(y_set, half + 1)
                    where = (lru_u[:, 4:8, :] if half else lru_a[:, 0:4, :])[:, 2 * t:2 * t + 2, :]
                    a.activation(where.rearrange("p k t -> p (k t)"), y_ps[:, t, 512 * half:512 * (half + 1)],
                                 ACT.Square, accum_out=ssq[:, half, t:t + 1]).then_inc(xf_ssq, 1)
            root(5, tok_rms)
            a.wait_ge(tok_ready, 1)
            for i in range(4):
                t = i // 2
                wait_product(a, "htok", i)
                a.activation(h_tok[:, t, 512 * (i % 2):512 * (i % 2) + 512], ps("htok", i)[:],
                             ACT.Copy, scale=tok_rms[:, t:t + 1]).then_inc(htok_ready, 1)
            a.wait_ge(top_ready, 1)
            for t in range(TT):
                a.activation(top_g[:, t, 0:TOP], top_v[:, t, 0:TOP], ACT.Exp, bias=t1[:, t, 0:1],
                             accum_out=t1[:, t, 1:2]).then_inc(texp_ready, 1)
            for i in range(2):
                wait_product(a, "gfin", i)
                a.activation(gfin[:, 512 * i:512 * (i + 1)], ps("gfin", i)[:], ACT.Copy).then_inc(gfin_ready, 1)

            def copy_tokens(n):
                a.wait_ge(gathered, n)
                a.activation(xtok, bank_x[:], ACT.Copy).then_inc(xtok_ready, 1)

            def copy_xg(n):
                a.wait_ge(xgT_done, n)
                a.activation(xg, bank_x[:].rearrange("p (c n) -> p c n", c=4), ACT.Copy).then_inc(xg_ready, 1)

            copy_tokens(1)
            copy_xg(1)
            a.wait_ge(count_ready, 3)
            jobs = a.value_load(n_i[0:1, 0:1], min_val=NE, max_val=JOBS_MAX)
            with a.Fori(0, jobs) as j:
                a.wait_ge(gclip_ready, j + 1)
                a.activation(sg, gc, ACT.Sigmoid, scale=SWIGLU_ALPHA).then_inc(sigm_ready, 1)
                copy_tokens(j + 2)
                a.wait_ge(chunk_used, JOB_CHUNKS * j + (SLOTS + JOB_CHUNKS))
                a.activation(job_out, bank_g[:], ACT.Copy).then_inc(job_out_ready, 1)
                copy_xg(j + 2)

            a.activation(fin[:, 2:3], ones[:, 0:1], ACT.Sqrt)
            for t in range(TT):
                a.wait_ge(y_done, t + 1)
                a.activation(y_sb[:, t, :], y_ps[:, t, :], ACT.Square, accum_out=fin[:, t:t + 1]).then_inc(ysum_ready, 1)
                a.wait_ge(yvar_ready, t + 1)
                a.activation(fin[:, t:t + 1], fin[:, t:t + 1], ACT.Sqrt).then_inc(yroot_ready, 1)

        @block.tensor
        def _(pe):
            def product_bank(name, i=0):
                n = AT[(name, i)]
                if n >= NBANK:
                    pe.wait_ge(*read[PRODUCTS[n - NBANK]])
                return bank[n % NBANK]

            def sum_channels(name, src, squared):
                dst = product_bank(name)
                ready, pieces = squared
                for k in range(KT):
                    if k % (KT // pieces) == 0:
                        pe.wait_ge(ready, k // (KT // pieces) + 1)
                    last = nc.tensor.matmul(dst[:, 0:T], ones[:], src[:, k, :], start=k == 0, stop=k == KT - 1)
                last.then_inc(product, 1)

            def project(name, i, src, token_major=False, arrives=None):
                n = CHUNK_AT[(name, i)]
                dst = product_bank(name, i)
                w = pre_slot[n % PRE_SLOTS]
                pe.wait_ge(pre_loaded[n % PRE_SLOTS], 16 * (n // PRE_SLOTS + 1))
                for m in range(2):
                    for k in range(KT):
                        if arrives and m == 0:
                            pe.wait_ge(*arrives(k))
                        if token_major:
                            lhsT, rhs = src[:, k, m * P:(m + 1) * P], w[:, k, :]
                        else:
                            lhsT, rhs = w[:, k, m * P:(m + 1) * P], src[:, k, :]
                        last = nc.tensor.matmul(dst[:, m * T:(m + 1) * T], lhsT, rhs, start=k == 0, stop=k == KT - 1)
                last.then_inc(product, 1)

            def project_parts(name, i, parts, arrives=None):
                dst = product_bank(name, i)
                s = SPLIT_AT[(name, i)]
                b = s % SPLIT_BUFS
                hi, lo = parts
                for m in range(2):
                    for k in range(KT):
                        if m == 0 and k % HALF == 0:
                            pe.wait_ge(w_lo_ready[b], 2 * (s // SPLIT_BUFS) + k // HALF + 1)
                        if arrives and m == 0:
                            pe.wait_ge(*arrives(k))
                        cols = slice(m * P, (m + 1) * P)
                        d = dst[:, m * T:(m + 1) * T]
                        nc.tensor.matmul(d, w_hi[:, b, k, cols], hi[:, k, :], start=k == 0, stop=False)
                        nc.tensor.matmul(d, w_lo[:, b, k, cols], hi[:, k, :], start=False, stop=False)
                        last = nc.tensor.matmul(d, w_hi[:, b, k, cols], lo[:, k, :], start=False, stop=k == KT - 1)
                last.then_inc(product, 1)

            pe.wait_ge(consts, CONSTS)
            sum_channels("sum_x2", lru_a, (x_sq, 2))
            for i in range(4):
                for name in ("cg", "cv", "xr", "gr"):
                    project_parts(name, i, h1_parts,
                                  arrives=(lambda k: (h1_done, k + 1)) if (name, i) == ("cg", 0) else None)
                if i == 0:
                    sum_channels("sum_m2", lru_u, (m_sq, 1))
            for i in range(4):
                project_parts("k", i, mem_parts, arrives=(lambda k: (mem_done, 1)) if i == 0 else None)

            def lru_gates_of(d):
                for i in range(4):
                    for g, name in enumerate((f"ra{d}", f"ri{d}")):
                        dst = product_bank(name, i)
                        for m in range(2):
                            last = nc.tensor.matmul(dst[:, m * T:(m + 1) * T], lru_gate_w[:, 2 * d + g, 2 * i + m, :],
                                                    xc[:, 2 * i + m, :], start=True, stop=True)
                        last.then_inc(product, 1)

            pe.wait_ge(lruw_in, 16 * 8)
            pe.wait_ge(xc_ready, 4)
            lru_gates_of(0)
            for i in range(3):
                project_parts("ga", i, h1_parts)
            sum_channels("ln_mean", cv, (conv_ready, 4))
            project_parts("ga", 3, h1_parts)
            project_parts("gb", 0, h1_parts)
            sum_channels("ln_var", ln_squares, (ln_sq, 1))
            lru_gates_of(1)
            for i in range(1, 4):
                project_parts("gb", i, h1_parts)
            for i in range(4):
                project_parts("yb", i, swish_parts, arrives=(lambda k: (sw_done, k + 1)) if i == 0 else None)
            for i in range(4):
                project_parts("ya", i, lru_parts, arrives=(lambda k: (lr_done, k // 2 + 1)) if i == 0 else None)
            project("v", 0, memT, token_major=True)
            for i in range(4):
                project_parts("wo", i, merged_parts, arrives=(lambda k: (mg_done, k // 2 + 1)) if i == 0 else None)
            project("v", 1, memT, token_major=True)
            sum_channels("sum_x1", lru_a, (x1_sq, 4))
            for i in range(2, 4):
                project("v", i, memT, token_major=True)
            for i in range(4):
                project_parts("q", i, h2_parts, arrives=(lambda k: (h2_done, k + 1)) if i == 0 else None)
            for h in range(HEADS):
                dst = product_bank("score", h)
                pe.wait_ge(q_ready, h + 1)
                for t in range(TT):
                    for k in range(2):
                        last = nc.tensor.matmul(dst[:, t * T:(t + 1) * T], qT[:, 2 * h + k, t * P:(t + 1) * P],
                                                keyT[:, 2 * h + k, :], start=k == 0, stop=k == 1)
                last.then_inc(product, 1)

            def transpose_prob(h):
                dst = product_bank("probT", h)
                pe.wait_ge(prob_ready, h + 1)
                for m in range(TT):
                    for t in range(TT):
                        last = nc.tensor.transpose(dst[:, m * T + t * P:m * T + (t + 1) * P],
                                                   prob[:, h, t, m * P:(m + 1) * P], ident[:])
                last.then_inc(product, 1)

            def attend(h):
                dst = product_bank("attn", h)
                pe.wait_ge(probT_ready, h + 1)
                for k in range(2):
                    for m in range(TT):
                        last = nc.tensor.matmul(dst[:, k * T:(k + 1) * T], val[:, m, h * HD + k * P:h * HD + (k + 1) * P],
                                                probT[:, h, m, :], start=m == 0, stop=m == TT - 1)
                last.then_inc(product, 1)

            transpose_prob(0)
            for h in range(HEADS):
                if h + 1 < HEADS:
                    transpose_prob(h + 1)
                attend(h)
            def set_out(i):
                pe.wait_ge(xf_ready, i + 1)
                for k in (2 * i, 2 * i + 1):
                    for t in range(TT):
                        last = nc.tensor.matmul(y_ps[:, t, k * P:(k + 1) * P], xT[:, k, t * P:(t + 1) * P], ident[:],
                                                start=k % 4 == 0, stop=False, skip_group_check=True)
                if i % 2:
                    last.then_inc(y_set, 1)
                for k in (2 * i, 2 * i + 1):
                    c = k % 4
                    pe.wait_ge(h_ready, 2 * KT + k + 1)
                    last = nc.tensor.matmul(logitT_bank[NE * c:NE * (c + 1), 0:T], router[:, k, :], xgT[:, k, :],
                                            start=k < 4, stop=k >= 4)
                return last

            pe.wait_ge(router_in, 32)
            for i in range(4):
                project_parts("o", i, attn_parts, arrives=(lambda k: (at_done, k // 2 + 1)) if i == 0 else None)
                if i == 1:
                    logitT_bank = product_bank("logitT")
                if i >= 1:
                    set_out(i - 1)
            set_out(3).then_inc(product, 1)
            dst = product_bank("logit")
            nc.tensor.matmul(dst[:, TT * P:TT * P + NE], ones[0:1, :], rb_row[:], start=True,
                             stop=True).then_inc(chunk_used, SLOTS)
            pe.wait_ge(logitT_ready, 1)
            for t in range(TT):
                last = nc.tensor.transpose(dst[:, t * P:(t + 1) * P], lgT[:, t * P:(t + 1) * P], ident[:])
            last.then_inc(product, 1)
            for i in range(4):
                dst = product_bank("htok", i)
                for k in range(4):
                    last = nc.tensor.transpose(dst[:, k * P:(k + 1) * P],
                                               xgT[:, 4 * (i % 2) + k, (i // 2) * P:(i // 2 + 1) * P], ident[:])
                last.then_inc(product, 1)
            pe.wait_ge(gfin_in, 16)
            for i in range(2):
                nc.tensor.matmul(product_bank("gfin", i)[:], ones[0:1, :], gfin_row[:, 512 * i:512 * (i + 1)],
                                 start=True, stop=True).then_inc(product, 1)
            dst = product_bank("rank")
            pe.wait_ge(mask_ready, 1)
            nc.tensor.matmul(dst[:, 0:NE], before[:], mask[:, 0, :], start=True, stop=True)
            nc.tensor.matmul(dst[:, NE:2 * NE], ones[:], mask[:, 0, :], start=True, stop=False)
            nc.tensor.matmul(dst[:, NE:2 * NE], before[:], mask[:, 1, :], start=False, stop=True)
            for t in range(TT):
                last = nc.tensor.matmul(dst[:, 2 * NE:3 * NE], ones[:], mask[:, t, :], start=t == 0, stop=t == TT - 1)
            last.then_inc(product, 1)
            def wait_bank(b):
                pe.wait_ge(*read[[x for n, x in enumerate(PRODUCTS) if n % NBANK == b][-1]])

            def gather():
                for t in range(TT):
                    for half in range(2):
                        last = nc.tensor.matmul(bank_x[CAP * half:CAP * (half + 1), :], pick[:, t, :],
                                                h_tok[:, t, 512 * half:512 * (half + 1)],
                                                start=t == 0, stop=t == TT - 1)
                last.then_inc(gathered, 1)

            def transpose_tokens(n):
                pe.wait_ge(xtok_ready, n)
                for c in range(4):
                    last = nc.tensor.transpose(bank_x[:, c * P:(c + 1) * P], xtok[:, c * P:(c + 1) * P], ident[:])
                last.then_inc(xgT_done, 1)

            wait_bank(2)
            pe.wait_ge(htok_ready, 4)
            pe.wait_ge(pick_ready, 1)
            gather()
            pe.wait_ge(count_ready, 3)
            groups = pe.value_load(n_i[0:1, 2:3], min_val=NE // GROUP, max_val=JOBS_MAX // GROUP)
            transpose_tokens(1)

            def transpose_wpick(n):
                pe.wait_ge(wpick_ready, n)
                for t in range(TT):
                    last = nc.tensor.transpose(bank_a[:, t * P:(t + 1) * P], wpick[:, t, :], ident[:])
                last.then_inc(wpickT_done, 1)

            def scatter(t, stop=False):
                for half in range(2):
                    last = nc.tensor.matmul(y_ps[:, t, 512 * half:512 * (half + 1)],
                                            wpickT[CAP * half:CAP * (half + 1), t, :],
                                            job_out[CAP * half:CAP * (half + 1), :],
                                            start=False, stop=stop, skip_group_check=True)
                return last

            wait_bank(3)
            transpose_wpick(1)
            wait_bank(0)
            wait_bank(1)
            pe.wait_ge(bdown_in, 32)
            def run_job(g, u):
                j = pe.snap(g * GROUP + u)

                def chunk(u, c):
                    turn, slot = divmod(u * JOB_CHUNKS + c, SLOTS)
                    pe.wait_ge(loaded[slot], g * (16 * GROUP * JOB_CHUNKS // SLOTS) + 16 * (turn + 1))
                    return expert_slot[slot]

                pe.wait_ge(bias_in[u % 2], g * (16 * GROUP) + 32 * (u // 2 + 1))
                for dst, row in ((bank_u, bup_rows[u % 2][1]), (bank_g, bup_rows[u % 2][0])):
                    if dst is bank_g:
                        pe.wait_ge(job_out_ready, j + 1)
                    for half in range(2):
                        nc.tensor.matmul(dst[CAP * half:CAP * (half + 1), :], ones[0:1, 0:CAP],
                                         row[:, 512 * half:512 * (half + 1)], start=True, stop=False)
                pe.wait_ge(xg_ready, j + 1)
                for k in range(KT):
                    w = chunk(u, k)
                    for dst, col in ((bank_g, 0), (bank_u, F)):
                        for half in range(2):
                            last = nc.tensor.matmul(dst[CAP * half:CAP * (half + 1), :],
                                                    xg[:, k % 4, CAP * (k // 4):CAP * (k // 4 + 1)],
                                                    w[:, col + 512 * half:col + 512 * (half + 1)],
                                                    start=False, stop=k == KT - 1)
                    last.then_inc(chunk_used, 1)
                pe.wait_ge(pick_ready, j + 2)
                gather()
                pe.wait_ge(wpickT_ready, j + 1)
                scatter(0)
                pe.wait_ge(act_ready, j + 1)
                for c in range(4):
                    last = nc.tensor.transpose(bank_a[:, c * P:(c + 1) * P], act[:, c * P:(c + 1) * P], ident[:])
                last.then_inc(actT_done, 1)
                scatter(1)
                pe.wait_ge(actT_ready, j + 1)
                for k in range(KT):
                    if k % 2 == 0:
                        w = chunk(u, UP_CHUNKS + k // 2)
                    for half in range(2):
                        col = D * (k % 2) + 512 * half
                        last = nc.tensor.matmul(bank_g[CAP * half:CAP * (half + 1), :],
                                                actT[:, k % 4, CAP * (k // 4):CAP * (k // 4 + 1)],
                                                w[:, col:col + 512], start=k == 0, stop=k == KT - 1)
                    if k % 2:
                        last.then_inc(chunk_used, 1)
                transpose_wpick(j + 2)
                transpose_tokens(j + 2)

            with pe.Fori(0, groups) as g:
                for u in range(GROUP):
                    run_job(g, u)
            jobs = groups * GROUP
            pe.wait_ge(wpickT_ready, jobs + 1)
            pe.wait_ge(job_out_ready, jobs + 1)
            for t in range(TT):
                scatter(t, stop=True).then_inc(y_done, 1)

        @block.vector
        def _(v):
            done = [0]

            def step(ins, lag=0):
                done[0] += 1
                ins.then_inc(v_chain, 1)
                if done[0] > lag:
                    v.wait_ge(v_chain, done[0] - lag)

            def variance(name, buf):
                wait_product(v, name)
                nc.vector.tensor_scalar(buf[:], ps(name)[:, 0:T], 1.0 / D, EPS, ALU.mult, ALU.add).then_inc(var_ready, 1)

            def inverse_root(n, buf):
                v.wait_ge(root_ready, n)
                step(nc.vector.reciprocal(buf[:], buf[:]))

            def split_w(name, i):
                split_w_hi(v, nc.vector.tensor_copy, name, i)

            def lo_part(lo, src, hi, ks, hi_ready, done):
                v.wait_ge(*hi_ready)
                nc.vector.tensor_tensor(lo[:, ks, :], src, hi[:, ks, :], ALU.subtract).then_inc(done, 1)

            def rms_parts(tmp, src, buf, col, parts, hi_ready, done):
                for k in range(KT + 1):
                    if k < KT:
                        nc.vector.scalar_tensor_tensor(tmp[:, k, :], src[:, k, :], par[:, k, col:col + 1], buf[:],
                                                       ALU.mult, ALU.mult).then_inc(h_ready, 1)
                    if k > 0:
                        lo_part(parts[1], tmp[:, k - 1:k, :], parts[0], slice(k - 1, k), (hi_ready, k), done)

            def rms(dst, src, buf, col, ready):
                for k in range(KT):
                    nc.vector.scalar_tensor_tensor(dst[:, k, :], src[:, k, :], par[:, k, col:col + 1], buf[:],
                                                   ALU.mult, ALU.mult).then_inc(ready, 1)

            v.wait_ge(consts, CONSTS)
            step(nc.vector.tensor_copy(iota_f[:], iota_i[:]))
            step(nc.vector.tensor_scalar(iota_c[:], iota_f[:], float(CAP), float(CAP), ALU.is_ge, ALU.mult))
            step(nc.vector.tensor_tensor(iota_c[:], iota_f[:], iota_c[:], ALU.subtract))
            step(nc.vector.tensor_scalar(roff[:], iota_f[:, 0:MAX_ROUNDS + 1], -float(CAP), -1.0, ALU.mult, ALU.add))
            for half in range(2):
                v.wait_ge(x_in[half], 16)
            v.wait_ge(par_in, 16)
            variance("sum_x2", stat)
            split_w("cg", 0)
            inverse_root(1, stat)
            rms_parts(lru_h, xT, stat, P_MIX_G, h1_parts, h1_hi, h1_done)

            lam_in = par[:, :, P_LAM:P_LAM + 2]
            nc.vector.scalar_tensor_tensor(lam[:, 0], lam_in, -1.0, lam_in, ALU.mult, ALU.min).then_inc(lam_abs, 1)
            v.wait_ge(lam_exp, 1)
            step(nc.vector.tensor_scalar(lam[:, 2], lam[:, 1], 2.0, None, ALU.add))
            step(nc.vector.reciprocal(lam[:, 2], lam[:, 2]))
            step(nc.vector.tensor_tensor(lam[:, 2], lam[:, 1], lam[:, 2], ALU.mult))
            step(nc.vector.tensor_tensor(lam[:, 3], lam[:, 2], lam[:, 2], ALU.mult))
            step(nc.vector.memset(lam[:, 4], 1.0 / 17))
            for n in (15, 13, 11, 9, 7, 5, 3, 1):
                step(nc.vector.tensor_tensor(lam[:, 4], lam[:, 4], lam[:, 3], ALU.mult))
                step(nc.vector.tensor_scalar(lam[:, 4], lam[:, 4], 1.0 / n, None, ALU.add))
            step(nc.vector.scalar_tensor_tensor(lam[:, 4], lam[:, 4], 2.0, lam[:, 2], ALU.mult, ALU.mult))
            step(nc.vector.tensor_scalar(lam[:, 3], lam_in, -1.0, 0.0, ALU.mult, ALU.max))
            step(nc.vector.tensor_tensor(lam[:, 4], lam[:, 3], lam[:, 4], ALU.add))
            step(nc.vector.tensor_scalar(lam[:, 5], lam[:, 4], 8.0, None, ALU.mult))
            nc.vector.tensor_scalar(lam[:, 6], lam[:, 4], -8.0, None, ALU.mult).then_inc(lam_ready, 1)

            def conv(dst, src, taps, w_col, b_col, m0, ready):
                for tap in range(taps):
                    if taps == CONF_TAPS and m0 == 4 and tap == 3 * taps // 4:
                        gated(3)
                    for m in (m0, m0 + 1):
                        x = src[:, m, tap:tap + T]
                        w = par[:, m, w_col + tap:w_col + tap + 1]
                        if tap == 0:
                            ins = nc.vector.tensor_scalar(dst[:, m, :], x, w, par[:, m, b_col:b_col + 1],
                                                          ALU.mult, ALU.add)
                        else:
                            ins = nc.vector.scalar_tensor_tensor(dst[:, m, :], x, w, dst[:, m, :], ALU.mult, ALU.add)
                        if tap == taps - 1 and m == m0 + 1:
                            ins.then_inc(ready, 1)
                        else:
                            step(ins, lag=1)

            def gated(i):
                wait_product(v, "cv", i)
                v.wait_ge(sig_ready, i + 1)
                nc.vector.tensor_tensor(glu[:, 2 * i:2 * i + 2, CONF_LEFT:CONF_LEFT + T], pair(ps("cv", i)),
                                        sig[:, i % 2].rearrange("p (m t) -> p m t", m=2), ALU.mult).then_inc(glu_ready, 1)

            for i in range(4):
                if i < 3:
                    gated(i)
                if i == 3:
                    for n in range(4):
                        v.wait_ge(xr_ready, n + 1)
                        conv(xc, xr, LRU_TAPS, P_LRU_W, P_LRU_CB, 2 * n, xc_ready)
                v.wait_ge(glu_ready, i + 1)
                conv(cv, glu, CONF_TAPS, P_DW_W, P_DW_B, 2 * i, conv_ready)
                if i == 0:
                    variance("sum_m2", mstat)
                if i == 1:
                    inverse_root(2, mstat)
                    v.wait_ge(mem_in, 16)
                    rms(memT, memT, mstat, P_MEM_G, mem_ready)
                    v.wait_ge(mem_ready, KT)
                    nc.vector.tensor_copy(lru_hi[:, :, :], memT).then_inc(mem_hi, 1)
                    lo_part(lru_lo, memT, lru_hi, slice(0, KT), (mem_hi, 1), mem_done)

            def lru_inputs(d):
                for i in range(4):
                    pr = slice(2 * i, 2 * i + 2)
                    v.wait_ge(lru_gates, 16 * d + 4 * i + 4)
                    step(nc.vector.tensor_tensor(lru_u[:, pr, :], lru_u[:, pr, :], xc[:, pr, :], ALU.mult), lag=1)

            def lru_squares(d):
                for i in range(4):
                    pr = slice(2 * i, 2 * i + 2)
                    tmp = sig[:, i % 2].rearrange("p (m t) -> p m t", m=2)
                    v.wait_ge(lru_exp, KT * d + 2 * i + 2)
                    step(nc.vector.tensor_tensor(tmp, lru_a[:, pr, :], lru_a[:, pr, :], ALU.mult))
                    nc.vector.scalar_tensor_tensor(lru_t[:, pr, :], tmp, 1.0, lru_t[:, pr, :], ALU.add,
                                                   ALU.mult).then_inc(lru_sq, 1)

            v.wait_ge(xc_ready, 4)
            lru_inputs(0)
            lru_squares(0)

            wait_product(v, "ln_mean")
            nc.vector.tensor_scalar(mstat[:], ps("ln_mean")[:, 0:T], 1.0 / D, None, ALU.mult).then_inc(mean_read, 1)
            v.wait_ge(mean_read, 1)
            v.wait_ge(conv_ready, 4)
            spread = lambda s: s[:].rearrange("p (a t) -> p a t", a=1).to_broadcast([P, KT, T])
            nc.vector.tensor_tensor(cv[:], cv[:], spread(mstat), ALU.subtract).then_inc(centred, 1)
            def lru_scan(d):
                for i in range(4):
                    pr = slice(2 * i, 2 * i + 2)
                    v.wait_ge(lru_root, 4 * d + i + 1)
                    step(nc.vector.tensor_tensor(lru_u[:, pr, :], lru_u[:, pr, :], lru_t[:, pr, :], ALU.mult))
                    for m in (2 * i, 2 * i + 1):
                        dst, c, u = (x[:, m, :] for x in ((lru_t if d else lru_h), lru_a, lru_u))
                        if d:
                            dst, c, u = dst[:, ::-1], c[:, ::-1], u[:, ::-1]
                        nc.vector.tensor_tensor_scan(dst, c, u, 0.0, ALU.mult, ALU.add).then_inc(lru_scanned, 1)
            lru_scan(0)
            variance("ln_var", stat)
            inverse_root(3, stat)
            v.wait_ge(centred, 1)
            nc.vector.tensor_tensor(cv[:], cv[:], spread(stat), ALU.mult).then_inc(ln_ready, 1)
            split_w("gb", 1)
            lru_inputs(1)
            wait_product(v, "gb", 3)
            for k in range(KT):
                v.wait_ge(swish_ready, k + 1)
                nc.vector.tensor_copy(x_hi[:, k, :], cv[:, k, :]).then_inc(sw_hi, 1)
                if k > 0:
                    lo_part(h1_lo, cv[:, k - 1:k, :], x_hi, slice(k - 1, k), (sw_hi, k), sw_done)
            lo_part(h1_lo, cv[:, KT - 1:KT, :], x_hi, slice(KT - 1, KT), (sw_hi, KT), sw_done)
            lru_squares(1)
            lru_scan(1)
            v.wait_ge(lru_scanned, 2 * KT)
            v.wait_ge(gl_ready, 4)
            for i in range(5):
                pr, before_pr = slice(2 * i, 2 * i + 2), slice(2 * i - 2, 2 * i)
                if i < 4:
                    step(nc.vector.tensor_tensor(lru_h[:, pr, :], lru_h[:, pr, :], lru_t[:, pr, :], ALU.add))
                    nc.vector.tensor_tensor(gl[:, pr, :], gl[:, pr, :], lru_h[:, pr, :], ALU.mult).then_inc(lru_ready, 1)
                if i > 0:
                    lo_part(lru_lo, gl[:, before_pr, :], lru_hi, before_pr, (lr_hi, i), lr_done)

            for i in range(4):
                pr = slice(2 * i, 2 * i + 2)
                wait_product(v, "yb", i)
                v.wait_ge(mgate_ready, 10 + 2 * i)
                nc.vector.tensor_tensor(gate_b[:, pr, :], pair(ps("yb", i)), gate_b[:, pr, :], ALU.mult).then_inc(yb_read, 1)
            for i in range(4):
                pr = slice(2 * i, 2 * i + 2)
                wait_product(v, "ya", i)
                split_w(*SPLIT[SPLIT_AT[("ya", i)] + SPLIT_BUFS])
                nc.vector.tensor_tensor(gate_a[:, pr, :], pair(ps("ya", i)), gate_a[:, pr, :], ALU.mult).then_inc(ya_read, 1)
                v.wait_ge(ya_read, i + 1)
                v.wait_ge(yb_read, i + 1)
                nc.vector.tensor_tensor(gate_a[:, pr, :], gate_a[:, pr, :], gate_b[:, pr, :], ALU.add).then_inc(merged, 1)
                lo_part(mid_lo, gate_a[:, pr, :], x_hi, pr, (mg_hi, i + 1), mg_done)

            def residual(name, ready, then=None):
                for i in range(4):
                    pr = slice(2 * i, 2 * i + 2)
                    wait_product(v, name, i)
                    nc.vector.tensor_tensor(xT[:, pr, :], pair(ps(name, i)), xT[:, pr, :], ALU.add).then_inc(ready, 1)
                    if then:
                        then(i)
                    if i < 2:
                        split_w(name, i + 2)

            residual("wo", x1_ready)
            variance("sum_x1", stat)
            inverse_root(4, stat)
            rms_parts(lru_u, xT, stat, P_XA_G, h2_parts, h2_hi, h2_done)

            for h in range(HEADS):
                wait_product(v, "score", h)
                step(nc.vector.reduce_max(sm[:, 0, h, :], pair(ps("score", h)), AX.X))
                nc.vector.tensor_scalar(sm[:, 1, h, :], sm[:, 0, h, :], -HD ** -0.5, None, ALU.mult).then_inc(smax_ready, 1)
            for h in range(HEADS):
                v.wait_ge(sexp_ready, 2 * h + 2)
                step(nc.vector.reciprocal(sm[:, 3, h, :], sm[:, 2, h, :]))
                for t in range(TT):
                    ins = nc.vector.tensor_scalar(prob[:, h, t, :], prob[:, h, t, :], sm[:, 3, h, t:t + 1], None, ALU.mult)
                    if t == 0:
                        step(ins)
                    else:
                        ins.then_inc(prob_ready, 1)

            for i in range(4):
                pr = slice(2 * i, 2 * i + 2)
                lo_part(attn_lo, pair(ps("attn", i)), x_hi, pr, (at_hi, i + 1), at_done)
            def times_gain(i):
                v.wait_ge(xf_ready, i + 1)
                for k in (2 * i, 2 * i + 1):
                    nc.vector.tensor_scalar(xgT[:, k, :], xT[:, k, :], par[:, k, P_FFN_G:P_FFN_G + 1], None,
                                            ALU.mult).then_inc(h_ready, 1)

            residual("o", xf_ready, times_gain)
            step(nc.vector.memset(wpick, 0.0))
            wait_product(v, "logitT")
            nc.vector.tensor_copy(lgT, ps("logitT")[:, 0:T]).then_inc(logitT_ready, 1)
            v.wait_ge(xf_ssq, TT)
            step(nc.vector.tensor_scalar(ssq[:, 0, :], ssq[:, 0, :], 1.0 / D, EPS, ALU.mult, ALU.add))
            v.wait_ge(xf_ssq, 2 * TT)
            nc.vector.scalar_tensor_tensor(tok_rms[:], ssq[:, 1, :], 1.0 / D, ssq[:, 0, :], ALU.mult,
                                           ALU.add).then_inc(var_ready, 1)
            v.wait_ge(root_ready, 5)
            nc.vector.reciprocal(tok_rms[:], tok_rms[:]).then_inc(tok_ready, 1)
            v.wait_ge(tok_ready, 1)

            wait_product(v, "logit")
            parts = ps("logit")[:, 0:TT * P].rearrange("p (t c e) -> p t e c", t=TT, c=4)
            step(nc.vector.reduce_sum(lg[:], parts, AX.X))
            for t in range(TT):
                nc.vector.scalar_tensor_tensor(lg[:, t, :], lg[:, t, :], tok_rms[:, t:t + 1],
                                               ps("logit")[:, TT * P:TT * P + NE], ALU.mult, ALU.add).then_inc(logit_read, 1)
            v.wait_ge(logit_read, 2)
            for t in range(TT):
                step(nc.vector.max(top_v[:, t, :], lg[:, t, :]), lag=1)
            v.wait_ge(v_chain, done[0])
            nc.vector.tensor_scalar(t1[:, :, 0:1], top_v[:, :, 0:1], -1.0, None, ALU.mult).then_inc(top_ready, 1)
            for t in range(TT):
                step(nc.vector.max_index(top_i[:, t, :], top_v[:, t, :], lg[:, t, :]), lag=1)
            v.wait_ge(v_chain, done[0])
            step(nc.vector.tensor_copy(top_f[:], top_i[:]))

            def on_experts(x):
                return x[:, :, 0:TOP].rearrange("p t (n a) -> p t n a", a=1).to_broadcast([P, TT, TOP, NE])

            experts = iota_f[:, 0:NE].rearrange("p (t n e) -> p t n e", t=1, n=1).to_broadcast([P, TT, TOP, NE])
            step(nc.vector.tensor_tensor(hot, experts, on_experts(top_f), ALU.is_equal))
            nc.vector.reduce_sum(mask[:], hot.rearrange("p t n e -> p t e n"), AX.X).then_inc(mask_ready, 1)
            def on_rounds(x):
                return x[:].rearrange("p t (r e) -> p t r e", r=1).to_broadcast([P, TT, MAX_ROUNDS + 1, NE])

            by_round = lambda x: x[:].rearrange("p t (r e) -> p t r e", e=NE)

            wait_product(v, "rank")
            v.wait_ge(mask_ready, 1)
            rank_ps = ps("rank")[:, 0:TT * NE].rearrange("p (t e) -> p t e", t=TT)
            step(nc.vector.scalar_tensor_tensor(rank[:], rank_ps, 1.0, mask[:], ALU.add, ALU.mult))
            step(nc.vector.tensor_tensor(by_round(pos), on_rounds(rank),
                                         roff[:].rearrange("p (t r e) -> p t r e", t=1, e=1).to_broadcast(
                                             [P, TT, MAX_ROUNDS + 1, NE]), ALU.add))

            def pick_tokens(j):
                for t in range(TT):
                    last = nc.vector.tensor_scalar(pick[:, t, :], iota_f[:, 0:CAP], pos[:, t, bass.ds(j, 1)], None,
                                                   ALU.is_equal)
                last.then_inc(pick_ready, 1)

            pick_tokens(0)
            nc.vector.reduce_max(count[:, 0:1], ps("rank")[0:1, 2 * NE:3 * NE], AX.X).then_inc(rank_read, 1)
            v.wait_ge(rank_read, 1)
            step(nc.vector.tensor_scalar(count[:, 1:2], count[:, 0:1], float(CAP), 1.0, ALU.is_gt, ALU.add))
            for r in range(2, MAX_ROUNDS):
                step(nc.vector.scalar_tensor_tensor(count[:, 1:2], count[:, 0:1], float(CAP * r), count[:, 1:2],
                                                    ALU.is_gt, ALU.add))
            nc.vector.tensor_scalar(n_i[:, 0:1], count[:, 1:2], float(NE), None, ALU.mult).then_inc(count_ready, 1)
            nc.vector.tensor_copy(n_i[:, 1:2], count[:, 1:2]).then_inc(count_ready, 1)
            nc.vector.tensor_scalar(n_i[:, 2:3], count[:, 1:2], float(NE // GROUP), None, ALU.mult).then_inc(count_ready, 1)
            v.wait_ge(texp_ready, TT)
            step(nc.vector.reciprocal(t1[:, :, 2:3], t1[:, :, 1:2]))
            step(nc.vector.tensor_tensor(top_g[:, :, 0:TOP], top_g[:, :, 0:TOP],
                                         t1[:, :, 2:3].to_broadcast([P, TT, TOP]), ALU.mult))
            step(nc.vector.tensor_tensor(ghot, hot, on_experts(top_g), ALU.mult))
            step(nc.vector.reduce_sum(gate[:], ghot.rearrange("p t n e -> p t e n"), AX.X))
            step(nc.vector.tensor_copy(by_round(gatej), on_rounds(gate)), lag=1)
            wide = wpick.rearrange("p t (h c) -> p t h c", h=2)[:, :, :, 0:NE]
            nc.vector.tensor_copy(wide, gate[:].rearrange("p t (h e) -> p t h e", h=1).to_broadcast(
                [P, TT, 2, NE])).then_inc(wpick_ready, 1)
            v.wait_ge(v_chain, done[0])

            def copy_wpickT(n):
                v.wait_ge(wpickT_done, n)
                nc.vector.tensor_copy(wpickT, bank_a[:, 0:TT * P].rearrange("p (t c) -> p t c", t=TT)).then_inc(wpickT_ready, 1)

            copy_wpickT(1)
            v.wait_ge(count_ready, 3)
            jobs = v.value_load(n_i[0:1, 0:1], min_val=NE, max_val=JOBS_MAX)
            with v.Fori(0, jobs) as j:
                v.wait_ge(gathered, j + 1)
                pick_tokens(v.snap(j + 1))
                for t in range(TT):
                    last = nc.vector.tensor_scalar(wpick[:, t, :], iota_c[:], pos[:, t, bass.ds(j, 1)],
                                                   gatej[:, t, bass.ds(j, 1)], ALU.is_equal, ALU.mult)
                last.then_inc(wpick_ready, 1)
                v.wait_ge(chunk_used, JOB_CHUNKS * j + (SLOTS + UP_CHUNKS))
                nc.vector.tensor_scalar(gc, bank_g[:], LIMIT, None, ALU.min).then_inc(gclip_ready, 1)
                nc.vector.tensor_scalar(uc, bank_u[:], LIMIT, -LIMIT, ALU.min, ALU.max).then_inc(uclip_ready, 1)
                v.wait_ge(uclip_ready, j + 1)
                nc.vector.scalar_tensor_tensor(uc, uc, 1.0, gc, ALU.add, ALU.mult).then_inc(ug_ready, 1)
                v.wait_ge(ug_ready, j + 1)
                v.wait_ge(sigm_ready, j + 1)
                nc.vector.tensor_tensor(act, uc, sg, ALU.mult).then_inc(act_ready, 1)
                v.wait_ge(actT_done, j + 1)
                nc.vector.tensor_copy(actT, bank_a[:].rearrange("p (c n) -> p c n", c=4)).then_inc(actT_ready, 1)
                copy_wpickT(v.snap(j + 2))

            v.wait_ge(gfin_ready, 2)
            for t in range(TT):
                x = fin[:, t:t + 1]
                v.wait_ge(ysum_ready, t + 1)
                nc.vector.tensor_scalar(x, x, 1.0 / D, EPS, ALU.mult, ALU.add).then_inc(yvar_ready, 1)
                v.wait_ge(yroot_ready, t + 1)
                step(nc.vector.reciprocal(x, x))
                nc.vector.scalar_tensor_tensor(y_sb[:, t, :], y_ps[:, t, :], x, gfin, ALU.mult, ALU.mult).then_inc(y_ready, 1)


_PLAIN = ["w_in", "lru_w_a", "lru_w_i", "w_rnn_out", "w_conf_out", "w_out", "xa_w_q", "xa_w_kv", "xa_w_o",
          "router_w", "router_b", "exp_w_up", "exp_b_up", "exp_w_down", "exp_b_down"]


def kernel(**inputs):
    import numpy as np
    import concourse.bacc as bacc
    from concourse.bass_utils import run_bass_kernel_spmd

    a = {k: np.asarray(v) for k, v in inputs.items()}
    rows = [a["norm_mix_g"], a["lru_conv_b"], a["lru_b_a"][0], a["lru_b_i"][0], a["lru_lambda"][0], a["conf_dw_b"],
            a["conf_ln_g"], a["conf_ln_b"], a["norm_xa_g"], a["norm_mem_g"], a["norm_ffn_g"],
            a["b_branch_gate"][0], a["lru_conv_w"][0], a["conf_dw_w"][0]]
    par = np.ascontiguousarray(np.concatenate(rows, axis=0).reshape(N_PAR, KT, P).transpose(2, 1, 0))

    def channel_major(x):
        return np.ascontiguousarray(x[0].reshape(T, KT, P).transpose(2, 1, 0))

    arrays = {"xT": channel_major(a["x"]), "memT": channel_major(a["mem"]), "par": par}
    for name in _PLAIN:
        arrays[name] = np.ascontiguousarray(a[name] if name == "router_b" else a[name][0])
    arrays["final_norm_g"] = np.ascontiguousarray(a["final_norm_g"].reshape(1, D))

    nc = bacc.Bacc("TRN2", target_bir_lowering=False, num_devices=1)
    aps = [nc.dram_tensor("in_" + k, x.shape, mybir.dt.from_np(x.dtype), kind="ExternalInput").ap()
           for k, x in arrays.items()]
    out = nc.dram_tensor("out_y", (T, D), F32, kind="ExternalOutput").ap()
    encoder_kernel(nc, *aps, out)
    r = run_bass_kernel_spmd(nc, [{"in_" + k: x for k, x in arrays.items()}], core_ids=[0])
    return r.results[0]["out_y"].reshape(1, T, D)
```
